# Optimizing a Trainium2 kernel written in Bass

```python
import jax, jax.numpy as jnp
from jax import lax
import numpy as np
import math

D_MODEL = 1024
BATCH = 1
SEQ = 512
DEPTH = 2

HEAD_DIM = 64
DSW_GROUPS = ((128, 1), (512, 4), (2048, 16))
DSW_HEADS_PER_GROUP = 4
DSW_HEADS = DSW_HEADS_PER_GROUP * len(DSW_GROUPS)
SB_HEADS = D_MODEL // (4 * HEAD_DIM)
W_A = DSW_HEADS * HEAD_DIM
W_B = SB_HEADS * HEAD_DIM
OUT_A = DSW_HEADS_PER_GROUP * HEAD_DIM
OUT_B = W_B
N_IN = 3 * W_A + 3 * W_B + 2 * D_MODEL
BLOCK = 128
D_FF = 2816
CONV_WIDTH = 3
RMS_EPS = 1e-6


def rmsnorm(x, g):
    xf = x.astype(jnp.float32)
    y = xf * lax.rsqrt(jnp.mean(xf * xf, axis=-1, keepdims=True) + RMS_EPS)
    return (y * g.astype(jnp.float32)).astype(x.dtype)

def alibi_slopes(n):
    return jnp.asarray(2.0 ** (-8.0 * np.arange(1, n + 1) / n), dtype=jnp.float32)

def dilated_window_attention(q, k, v, slopes, window, dilation):
    B, S, H, hd = q.shape
    W = window // dilation
    L = S // dilation
    nb = -(-L // W)
    Lp = nb * W

    def to_sub(a):
        a = a.reshape(B, L, dilation, H, hd).transpose(0, 2, 3, 1, 4)
        return jnp.pad(a, ((0, 0), (0, 0), (0, 0), (0, Lp - L), (0, 0)))

    def windows(a):
        ap = jnp.pad(to_sub(a), ((0, 0), (0, 0), (0, 0), (W, 0), (0, 0))).reshape(B, dilation, H, nb + 1, W, hd)
        return jnp.concatenate([ap[:, :, :, :-1], ap[:, :, :, 1:]], axis=-2)

    qs = to_sub(q).reshape(B, dilation, H, nb, W, hd)
    kw = windows(k)
    vw = windows(v).astype(jnp.float32)
    scores = jnp.einsum('brhnqc,brhnkc->brhnqk', qs, kw).astype(jnp.float32) * (hd ** -0.5)
    qi = jnp.arange(W)[:, None]
    kj = jnp.arange(2 * W)[None, :]
    delta = qi + W - kj
    key_sub = (jnp.arange(nb) * W - W)[:, None, None] + kj[None]
    valid = (delta >= 0) & (delta <= W) & (key_sub >= 0)
    bias = -slopes[:, None, None, None] * (delta * dilation).astype(jnp.float32)
    scores = jnp.where(valid, scores + bias, -jnp.inf)
    mx = jnp.max(scores, axis=-1, keepdims=True)
    p = jnp.exp(scores - mx)
    den = jnp.sum(p, axis=-1, keepdims=True)
    o = jnp.einsum('brhnqk,brhnkc->brhnqc', p, vw) / den
    lse = (mx + jnp.log(den))[..., 0]
    o = o.reshape(B, dilation, H, Lp, hd)[:, :, :, :L].transpose(0, 3, 1, 2, 4).reshape(B, S, H, hd)
    lse = lse.reshape(B, dilation, H, Lp)[:, :, :, :L].transpose(0, 3, 1, 2).reshape(B, S, H)
    return o, lse

def dilated_mixture(q, k, v):
    B, S = q.shape[:2]
    slopes = alibi_slopes(DSW_HEADS)
    outs, lses = [], []
    for g, (window, dilation) in enumerate(DSW_GROUPS):
        hs = slice(g * DSW_HEADS_PER_GROUP, (g + 1) * DSW_HEADS_PER_GROUP)
        o, lse = dilated_window_attention(q[:, :, hs], k[:, :, hs], v[:, :, hs], slopes[hs], window, dilation)
        outs.append(o)
        lses.append(lse)
    alpha = jax.nn.softmax(jnp.stack(lses, axis=0), axis=0)
    o = jnp.sum(alpha[..., None] * jnp.stack(outs, axis=0), axis=0)
    return o.reshape(B, S, OUT_A).astype(q.dtype)

def stick_breaking_attention(q, k, v):
    B, S, H, hd = q.shape
    nq = S // BLOCK
    scale = hd ** -0.5
    qb = q.reshape(B, nq, BLOCK, H, hd).transpose(1, 0, 3, 2, 4)
    kt = k.transpose(0, 2, 1, 3)
    vt = v.transpose(0, 2, 1, 3).astype(jnp.float32)
    key_pos = jnp.arange(S)

    def block(args):
        q_blk, i = args
        z = jnp.einsum('bhqc,bhkc->bhqk', q_blk, kt).astype(jnp.float32) * scale
        qpos = i * BLOCK + jnp.arange(BLOCK)
        causal = key_pos[None, :] < qpos[:, None]
        log_stay = jnp.where(causal, jax.nn.log_sigmoid(-z), 0.0)
        later = lax.cumsum(log_stay, axis=3, reverse=True) - log_stay
        attn = jnp.where(causal, jnp.exp(jax.nn.log_sigmoid(z) + later), 0.0)
        return jnp.einsum('bhqk,bhkc->bhqc', attn, vt)

    o = lax.map(block, (qb, jnp.arange(nq)))
    return o.transpose(1, 0, 3, 2, 4).reshape(B, S, H * hd).astype(q.dtype)

def causal_depthwise_conv(a, w, b):
    S = a.shape[1]
    ap = jnp.pad(a, ((0, 0), (CONV_WIDTH - 1, 0), (0, 0)))
    y = b
    for i in range(CONV_WIDTH):
        y = y + ap[:, i:i + S] * w[i]
    return y

def first_inputs(seed: int = 0) -> dict:
    key = jax.random.key(seed)
    ks = jax.random.split(key, 12)
    f32 = jnp.float32
    x = jax.random.normal(ks[0], (BATCH, SEQ, D_MODEL), f32)
    norm1 = 1.0 + 0.05 * jax.random.normal(ks[1], (DEPTH, D_MODEL), f32)
    w_in = jax.random.normal(ks[2], (DEPTH, D_MODEL, N_IN), f32) * D_MODEL ** -0.5
    b_gate = 0.01 * jax.random.normal(ks[3], (DEPTH, 2 * D_MODEL), f32)
    w_br = jax.random.normal(ks[4], (DEPTH, OUT_A + OUT_B, D_MODEL), f32) * OUT_A ** -0.5
    w_o = jax.random.normal(ks[5], (DEPTH, D_MODEL, D_MODEL), f32) * D_MODEL ** -0.5
    norm2 = 1.0 + 0.05 * jax.random.normal(ks[6], (DEPTH, D_MODEL), f32)
    w_up = jax.random.normal(ks[7], (DEPTH, D_MODEL, 2 * D_FF), f32) * D_MODEL ** -0.5
    conv_w = jax.random.normal(ks[8], (DEPTH, CONV_WIDTH, D_FF), f32) * CONV_WIDTH ** -0.5
    conv_b = 0.01 * jax.random.normal(ks[9], (DEPTH, D_FF), f32)
    w_down = jax.random.normal(ks[10], (DEPTH, D_FF, D_MODEL), f32) * D_FF ** -0.5
    norm_f = 1.0 + 0.05 * jax.random.normal(ks[11], (D_MODEL,), f32)
    return {"x": x, "norm1": norm1, "w_in": w_in, "b_gate": b_gate, "w_br": w_br, "w_o": w_o,
            "norm2": norm2, "w_up": w_up, "conv_w": conv_w, "conv_b": conv_b, "w_down": w_down,
            "norm_f": norm_f}

def first_block(x, norm1, w_in, b_gate, w_br, w_o, norm2, w_up, conv_w, conv_b, w_down, norm_f):
    B, S, _ = x.shape
    splits = [W_A, 2 * W_A, 3 * W_A, 3 * W_A + W_B, 3 * W_A + 2 * W_B, 3 * W_A + 3 * W_B]
    for l in range(DEPTH):
        h = rmsnorm(x, norm1[l])
        proj = h @ w_in[l]
        qa, ka, va, qb, kb, vb, gate_pre = jnp.split(proj, splits, axis=-1)
        hd4 = lambda t, n: t.reshape(B, S, n, HEAD_DIM)
        o_a = dilated_mixture(hd4(qa, DSW_HEADS), hd4(ka, DSW_HEADS), hd4(va, DSW_HEADS))
        o_b = stick_breaking_attention(hd4(qb, SB_HEADS), hd4(kb, SB_HEADS), hd4(vb, SB_HEADS))
        gates = jax.nn.sigmoid(gate_pre + b_gate[l])
        g_a, g_b = gates[..., :D_MODEL], gates[..., D_MODEL:]
        merged = g_a * (o_a @ w_br[l, :OUT_A]) + g_b * (o_b @ w_br[l, OUT_A:])
        x = x + merged @ w_o[l]
        h2 = rmsnorm(x, norm2[l])
        up = h2 @ w_up[l]
        a, v = up[..., :D_FF], up[..., D_FF:]
        a = causal_depthwise_conv(a, conv_w[l], conv_b[l])
        x = x + (jax.nn.gelu(a, approximate=False) * v) @ w_down[l]
    return rmsnorm(x, norm_f)


CTX_LEN = 256
GRID_W = 64
HG_WIDTH = D_MODEL // 2
HG_DIM = 128
HG_HEADS = HG_WIDTH // HG_DIM
CHUNK = 64
DA_WIDTH = D_MODEL // 4
DA_HEADS = 4
DA_V = DA_WIDTH // DA_HEADS
DA_QK = DA_V // 2
DA_QK_WIDTH = DA_HEADS * 2 * DA_QK
Q_BLOCK = 128
ROPE_THETA = 10000.0
ROPE_AXIS_DIM = DA_QK // 2
FT_WIDTH = D_MODEL // 4
FT_GROUPS = 4
MIX_WIDTH = HG_WIDTH + DA_WIDTH + FT_WIDTH
IN_SPLITS = (HG_WIDTH, HG_WIDTH, HG_WIDTH, HG_WIDTH, HG_WIDTH, DA_QK_WIDTH, DA_QK_WIDTH, DA_WIDTH, FT_WIDTH)
IN_WIDTH = sum(IN_SPLITS)
FF_HIDDEN = ((8 * D_MODEL // 3 + 255) // 256) * 256
N_MOD = 6
EPS = 1e-6


def rms_norm(x, g):
    xf = x.astype(jnp.float32)
    y = xf * lax.rsqrt(jnp.mean(xf * xf, axis=-1, keepdims=True) + EPS)
    return (y * g.astype(jnp.float32)).astype(x.dtype)

def adaln(x, g, shift, scale):
    return rms_norm(x, g) * (1 + scale) + shift

def modulation(cond, w, b):
    return jnp.split(jax.nn.silu(cond) @ w + b, N_MOD, axis=-1)

def split_heads(a, h):
    return a.reshape(a.shape[:-1] + (h, a.shape[-1] // h))

def split_projection(p):
    offsets = [int(o) for o in np.cumsum(IN_SPLITS)[:-1]]
    return jnp.split(p, offsets, axis=-1)

def axial_rope(t_len):
    n_rows = t_len // GRID_W
    rows = jnp.broadcast_to(jnp.arange(n_rows)[:, None], (n_rows, GRID_W)).reshape(-1)
    cols = jnp.broadcast_to(jnp.arange(GRID_W)[None, :], (n_rows, GRID_W)).reshape(-1)
    inv_freq = 1.0 / (ROPE_THETA ** (jnp.arange(0, ROPE_AXIS_DIM, 2, dtype=jnp.float32) / ROPE_AXIS_DIM))
    ang = jnp.stack([rows, cols], axis=-1).astype(jnp.float32)[:, :, None] * inv_freq
    return jnp.cos(ang), jnp.sin(ang)

def apply_rope(x, cos, sin):
    xs = x.reshape(x.shape[:-1] + (2, 2, ROPE_AXIS_DIM // 2)).astype(jnp.float32)
    cs, sn = cos[None, :, None, None], sin[None, :, None, None]
    x1, x2 = xs[..., 0, :], xs[..., 1, :]
    out = jnp.stack([x1 * cs - x2 * sn, x2 * cs + x1 * sn], axis=-2)
    return out.reshape(x.shape).astype(x.dtype)

def gla_chunkwise(q, k, v, log_f, s0):
    b_, t_, h_, _ = q.shape
    dv = v.shape[-1]
    n = t_ // CHUNK

    def chunks(a):
        return a.astype(jnp.float32).reshape(b_, n, CHUNK, h_, a.shape[-1]).transpose(1, 0, 3, 2, 4)

    incl = jnp.tril(jnp.ones((CHUNK, CHUNK), dtype=bool))[:, :, None]

    def step(state, inp):
        qi, ki, vi, gi = inp
        bcum = jnp.cumsum(gi, axis=2)
        o_inter = jnp.einsum('bhtk,bhkv->bhtv', qi * jnp.exp(bcum), state)
        rel = bcum[:, :, :, None, :] - bcum[:, :, None, :, :]
        decay = jnp.exp(jnp.where(incl, rel, -jnp.inf))
        scores = jnp.einsum('bhtk,bhsk,bhtsk->bhts', qi, ki, decay)
        o_intra = jnp.einsum('bhts,bhsv->bhtv', scores, vi)
        blast = bcum[:, :, -1:, :]
        state = state * jnp.exp(blast[:, :, 0, :, None]) + jnp.einsum(
            'bhsk,bhsv->bhkv', ki * jnp.exp(blast - bcum), vi)
        return state, o_inter + o_intra

    s_fin, o = lax.scan(step, s0, (chunks(q), chunks(k), chunks(v), chunks(log_f)))
    return o.transpose(1, 0, 3, 2, 4).reshape(b_, t_, h_, dv), s_fin

def hgrn2_scan(q, v, z, lb, s0, reverse):
    f = lb + (1.0 - lb) * jax.nn.sigmoid(z.astype(jnp.float32))
    k = split_heads(1.0 - f, HG_HEADS)
    log_f = split_heads(jnp.log(f), HG_HEADS)
    if reverse:
        q, k, v, log_f = jnp.flip(q, 1), jnp.flip(k, 1), jnp.flip(v, 1), jnp.flip(log_f, 1)
    o, s = gla_chunkwise(q, k, v, log_f, s0)
    if reverse:
        o = jnp.flip(o, 1)
    return o, s

def diff_softmax_attend(q, keys, vals, lam):
    s = jnp.einsum('bqhmd,bkhmd->bhmqk', q, keys).astype(jnp.float32) * (DA_QK ** -0.5)
    p = jax.nn.softmax(s, axis=-1)
    w = p[:, :, 0] - lam * p[:, :, 1]
    return jnp.einsum('bhqk,bkhv->bqhv', w.astype(vals.dtype), vals)

def fourier_mix(u):
    uh = split_heads(u, FT_GROUPS).astype(jnp.float32)
    y = jnp.fft.fft2(uh, axes=(1, 3), norm="ortho").real
    return y.reshape(u.shape).astype(u.dtype)

def mixer(hl, hc, w_in, w_out, lb_f, lb_b, hg_onorm, da_lam, da_subln, lam_init, cos, sin, with_ctx):
    pl = split_projection(hl @ w_in)
    pc = split_projection(hc @ w_in)
    bsz, t_lat = hl.shape[0], hl.shape[1]

    s0 = jnp.zeros((bsz, HG_HEADS, HG_DIM, HG_DIM), jnp.float32)
    q_c, v_c = split_heads(jax.nn.silu(pc[0]), HG_HEADS), split_heads(pc[1], HG_HEADS)
    q_l, v_l = split_heads(jax.nn.silu(pl[0]), HG_HEADS), split_heads(pl[1], HG_HEADS)
    oc_f, st_f = hgrn2_scan(q_c, v_c, pc[3], lb_f, s0, False)
    oc_b, st_b = hgrn2_scan(q_c, v_c, pc[4], lb_b, s0, True)
    ol_f, _ = hgrn2_scan(q_l, v_l, pl[3], lb_f, st_f, False)
    ol_b, _ = hgrn2_scan(q_l, v_l, pl[4], lb_b, st_b, True)

    def hgrn_out(o, g):
        return (rms_norm(o, hg_onorm).reshape(g.shape) * jax.nn.silu(g)).astype(g.dtype)

    def qk_heads(a):
        return a.reshape(a.shape[:-1] + (DA_HEADS, 2, DA_QK))

    lam_f = da_lam.astype(jnp.float32)
    lam = jnp.exp(jnp.sum(lam_f[0] * lam_f[1])) - jnp.exp(jnp.sum(lam_f[2] * lam_f[3])) + lam_init
    dq_l, dk_l = apply_rope(qk_heads(pl[5]), cos, sin), apply_rope(qk_heads(pl[6]), cos, sin)
    dv_l = split_heads(pl[7], DA_HEADS)
    dq_c, dk_c, dv_c = qk_heads(pc[5]), qk_heads(pc[6]), split_heads(pc[7], DA_HEADS)
    keys = jnp.concatenate([dk_l, dk_c], axis=1)
    vals = jnp.concatenate([dv_l, dv_c], axis=1)
    nb = t_lat // Q_BLOCK
    qb = dq_l.reshape((bsz, nb, Q_BLOCK) + dq_l.shape[2:]).transpose(1, 0, 2, 3, 4, 5)
    od_l = lax.map(lambda qq: diff_softmax_attend(qq, keys, vals, lam), qb)
    od_l = od_l.transpose(1, 0, 2, 3, 4).reshape(bsz, t_lat, DA_HEADS, DA_V)

    def diff_out(o):
        return (rms_norm(o, da_subln) * (1.0 - lam_init)).reshape(o.shape[:2] + (DA_WIDTH,))

    yl = jnp.concatenate([hgrn_out(ol_f + ol_b, pl[2]), diff_out(od_l).astype(hl.dtype),
                          fourier_mix(pl[8])], axis=-1) @ w_out
    if not with_ctx:
        return yl, None
    od_c = diff_softmax_attend(dq_c, dk_c, dv_c, lam)
    yc = jnp.concatenate([hgrn_out(oc_f + oc_b, pc[2]), diff_out(od_c).astype(hc.dtype),
                          fourier_mix(pc[8])], axis=-1) @ w_out
    return yl, yc

def swiglu(h, w_i, w_o):
    g, u = jnp.split(h @ w_i, 2, axis=-1)
    return (jax.nn.silu(g) * u) @ w_o

def second_inputs(seed: int = 0) -> dict:
    key = jax.random.key(seed)
    ks = jax.random.split(key, 15)
    f32 = jnp.float32
    nrm = lambda k, s: jax.random.normal(k, s, f32)
    return {
        "x": nrm(ks[0], (BATCH, SEQ, D_MODEL)),
        "c": nrm(ks[1], (BATCH, D_MODEL)),
        "ctx": nrm(ks[2], (BATCH, CTX_LEN, D_MODEL)),
        "c_ctx": nrm(ks[3], (D_MODEL,)),
        "w_mod": nrm(ks[4], (DEPTH, D_MODEL, N_MOD * D_MODEL)) * (0.5 * D_MODEL ** -0.5),
        "b_mod": nrm(ks[5], (DEPTH, N_MOD * D_MODEL)) * 0.01,
        "norm_g": 1.0 + 0.02 * nrm(ks[6], (DEPTH, 4, D_MODEL)),
        "w_in": nrm(ks[7], (DEPTH, D_MODEL, IN_WIDTH)) * D_MODEL ** -0.5,
        "w_out": nrm(ks[8], (DEPTH, MIX_WIDTH, D_MODEL)) * MIX_WIDTH ** -0.5,
        "hg_lb_logits": 0.1 * nrm(ks[9], (2, DEPTH, HG_WIDTH)),
        "hg_onorm": 1.0 + 0.02 * nrm(ks[10], (DEPTH, HG_DIM)),
        "da_lambda": 0.1 * nrm(ks[11], (DEPTH, 4, DA_QK)),
        "da_subln": 1.0 + 0.02 * nrm(ks[12], (DEPTH, DA_V)),
        "w_ffn_in": nrm(ks[13], (DEPTH, D_MODEL, 2 * FF_HIDDEN)) * D_MODEL ** -0.5,
        "w_ffn_out": nrm(ks[14], (DEPTH, FF_HIDDEN, D_MODEL)) * FF_HIDDEN ** -0.5,
    }

def second_block(x, c, ctx, c_ctx, w_mod, b_mod, norm_g, w_in, w_out, hg_lb_logits, hg_onorm,
              da_lambda, da_subln, w_ffn_in, w_ffn_out):
    cos, sin = axial_rope(x.shape[1])
    lb_p = jax.nn.softmax(hg_lb_logits.astype(jnp.float32), axis=1)
    lower_bounds = jnp.cumsum(lb_p, axis=1) - lb_p[:, :1]
    xl, xc = x, ctx
    for l in range(DEPTH):
        with_ctx = l < DEPTH - 1
        lam_init = 0.8 - 0.6 * math.exp(-0.3 * l)
        ml = modulation(c[:, None, :], w_mod[l], b_mod[l])
        mc = modulation(c_ctx[None, None, :], w_mod[l], b_mod[l])
        g = norm_g[l]
        hl = adaln(xl, g[0], ml[0], ml[1])
        hc = adaln(xc, g[0], mc[0], mc[1])
        yl, yc = mixer(hl, hc, w_in[l], w_out[l], lower_bounds[0, l], lower_bounds[1, l], hg_onorm[l],
                       da_lambda[l], da_subln[l], lam_init, cos, sin, with_ctx)
        xl = xl + ml[2] * rms_norm(yl, g[1])
        xl = xl + ml[5] * rms_norm(swiglu(adaln(xl, g[2], ml[3], ml[4]), w_ffn_in[l], w_ffn_out[l]), g[3])
        if with_ctx:
            xc = xc + mc[2] * rms_norm(yc, g[1])
            xc = xc + mc[5] * rms_norm(swiglu(adaln(xc, g[2], mc[3], mc[4]), w_ffn_in[l], w_ffn_out[l]), g[3])
    return xl


def setup_inputs(seed=0):
    out = dict(first_inputs(seed))
    for name, value in second_inputs(seed + 1).items():
        if name != "x":
            out[name + "_2"] = value
    return out


def reference(
    x, norm1, w_in, b_gate, w_br, w_o, norm2, w_up, conv_w, conv_b, w_down, norm_f, c_2, ctx_2,
    c_ctx_2, w_mod_2, b_mod_2, norm_g_2, w_in_2, w_out_2, hg_lb_logits_2, hg_onorm_2,
    da_lambda_2, da_subln_2, w_ffn_in_2, w_ffn_out_2,
):
    x = first_block(
        x, norm1, w_in, b_gate, w_br, w_o, norm2, w_up, conv_w, conv_b, w_down, norm_f,
    )
    return second_block(
        x, c_2, ctx_2, c_ctx_2, w_mod_2, b_mod_2, norm_g_2, w_in_2, w_out_2, hg_lb_logits_2,
        hg_onorm_2, da_lambda_2, da_subln_2, w_ffn_in_2, w_ffn_out_2,
    )


_drawn_inputs = setup_inputs


def setup_inputs(seed=0):
    import zlib

    import numpy as np

    out = dict(_drawn_inputs(seed))
    spreads = {}
    factors = {'b_gate': 8.0,
     'conv_b': 7.041,
     'norm_g_2': 3.025,
     'hg_lb_logits_2': 8.0,
     'hg_onorm_2': 8.0,
     'da_subln_2': 8.0}
    for name, (base, spread) in spreads.items():
        noise = np.random.default_rng([zlib.crc32(name.encode()), seed]).standard_normal(out[name].shape)
        drawn = base * np.exp(spread * noise) if base else spread * noise
        out[name] = __import__('jax').numpy.asarray(drawn.astype(out[name].dtype))
    for name, factor in factors.items():
        out[name] = (out[name] * factor).astype(out[name].dtype)
    return out
```

```python
import math

import numpy as np

import concourse.bass as bass
from concourse import mybir

F32 = mybir.dt.float32
F32R = mybir.dt.float32r
U8 = mybir.dt.uint8
ACT = mybir.ActivationFunctionType
ALU = mybir.AluOpType
AX = mybir.AxisListType

P = 128
D = 1024
DC = D // P
S = 512
ST = S // P
CTX = 256
CT = CTX // P
T2 = S + CTX
FF = 2816
FC = FF // P
DEPTH = 2
EPS = 1e-6

HD = 64
GROUPS = ((128, 1), (512, 4), (2048, 16))
ORDER = (1, 4, 4)
GH = 4
W_A = GH * len(GROUPS) * HD
W_B = 256
GATE0 = 3 * W_A + 3 * W_B
SLOPES = [float(np.float32(2.0 ** (-8.0 * n / 12))) for n in range(1, 13)]
FAR = 1e32

HGH = 4
LEVELS = 7
DAH = 4
GRID_W = 64

SLAB_K, SLAB_F = 8, 256



def distances(kind):
    window, dil = GROUPS[kind]
    q = np.arange(P)[:, None]
    if kind == 0:
        k = np.arange(2 * P)[None, :]
        delta = q + P - k
        ok = (delta >= 0) & (delta <= window)
    else:
        k = np.arange(P)[None, :]
        delta = (q - k) * ORDER[kind]
        ok = (delta >= 0) & (delta % dil == 0) & (delta <= window)
    return np.where(ok, -delta, -FAR).astype(np.float32)


def gla_masks():
    s, t = np.arange(P)[:, None], np.arange(P)[None, :]
    out = np.zeros((2, LEVELS + 1, P, P), np.float32)
    for lv in range(LEVELS):
        m = 1 << lv
        same = s // (2 * m) == t // (2 * m)
        out[0, lv] = same & (s // m % 2 == 0) & (t // m % 2 == 1)
        out[1, lv] = same & (s // m % 2 == 1) & (t // m % 2 == 0)
    out[:, LEVELS] = s == t
    return out


def constants():
    j = np.arange(P)
    c = {}
    c["c_ident"] = np.eye(P, dtype=np.float32)
    c["c_ones"] = np.ones((P, P), np.float32)
    c["c_pair"] = (j[:, None] // HD == j[None, :] // HD).astype(np.float32)
    c["c_dist0"], c["c_dist1"], c["c_dist2"] = distances(0), distances(1), distances(2)
    before = j[None, :] < j[:, None]
    c["c_causal"] = before.astype(np.float32)
    c["c_causal_neg"] = np.where(before, 0.0, -1e30).astype(np.float32)
    c["c_gla"] = np.ascontiguousarray(gla_masks().transpose(2, 0, 1, 3))
    f32 = np.float32
    inv = f32(1.0) / (f32(10000.0) ** (np.arange(0, 16, 2, dtype=f32) / f32(16)))
    t = np.arange(S)
    pos = np.stack([t // GRID_W, t % GRID_W]).astype(f32)
    feat = j % 32
    ang = pos[feat // 16, :] * inv[feat % 8][:, None].astype(f32)
    c["c_cos"], c["c_sin"] = np.cos(ang).astype(f32), np.sin(ang).astype(f32)
    rot = np.zeros((P, P), f32)
    for f in range(P):
        if f // 8 % 2 == 0:
            rot[f + 8, f] = -1.0
        else:
            rot[f - 8, f] = 1.0
    c["c_rot"] = rot
    a = 2 * np.pi * np.outer(np.arange(64), np.arange(64)) / 64
    d64 = np.zeros((P, 2, P))
    for g in range(2):
        d64[64 * g:64 * g + 64, 0, 64 * g:64 * g + 64] = np.cos(a)
        d64[64 * g:64 * g + 64, 1, 64 * g:64 * g + 64] = -np.sin(a)
    c["c_dft64"] = d64.astype(f32)
    for name, n in (("c_dftl", S), ("c_dftc", CTX)):
        a = 2 * np.pi * (np.outer(np.arange(n), np.arange(n)) % n) / n
        w = np.stack([np.cos(a), np.sin(a)]) / math.sqrt(n * 64)
        c[name] = np.ascontiguousarray(w.reshape(2, n // P, P, n).transpose(2, 0, 1, 3)).astype(f32)
    return c



class Stream:

    def __init__(self, nc, engine, name):
        self.engine, self.sem = engine, nc.alloc_semaphore(f"{name}_done")
        self.count, self.seen = 0, {}

    def wait(self, marks):
        for sem, value in marks:
            if self.seen.get(sem.name, 0) < value:
                self.engine.wait_ge(sem, value)
                self.seen[sem.name] = value

    def mark(self, instruction):
        instruction.then_inc(self.sem, 1)
        self.count += 1
        return (self.sem, self.count)

    def now(self):
        return (self.sem, self.count)

    def go(self, after, op, *args, **kw):
        self.wait(after)
        return self.mark(op(*args, **kw))


class Slot:

    def __init__(self, ap):
        self.ap, self.free = ap, []


class Ring:
    def __init__(self, aps):
        self.slots, self.at = [Slot(a) for a in aps], 0

    def take(self):
        s = self.slots[self.at % len(self.slots)]
        self.at += 1
        return s


class Banks:

    def __init__(self, banks):
        self.idle = [Slot(b) for b in banks]

    def take(self):
        return self.idle.pop(0)

    def give(self, slot, marks):
        slot.free = list(marks)
        self.idle.append(slot)


class DmaQueue:

    def __init__(self, nc, stream, name, n):
        self.stream, self.sems, self.at = stream, [nc.alloc_semaphore(f"{name}{i}") for i in range(n)], 0
        self.used = [0] * n

    def start(self, after, dst, src):
        i = self.at % len(self.sems)
        self.at += 1
        if self.used[i]:
            self.stream.wait([(self.sems[i], self.used[i])])
        self.stream.wait(after)
        self.stream.engine.dma_start(dst, src).then_inc(self.sems[i], 16)
        self.used[i] += 16
        return (self.sems[i], self.used[i])


def weave(main, filler, ratio=1):
    for _ in main:
        for _ in range(ratio):
            next(filler, None)


def pipeline(units, stages):
    for step in range(len(units) + len(stages) - 1):
        for k in reversed(range(len(stages))):
            if 0 <= step - k < len(units):
                stages[k](units[step - k])
        yield



class Core:
    pass


SBUF_END = 229344
ARENA_KB = 149
ARENA = SBUF_END - ARENA_KB * 1024
AT_X = 0
AT_H = 24
AT_WORK = 72


def place(k, name, kb, shape, dtype=F32):
    size = 4 * int(np.prod(shape))
    assert kb * 1024 + size <= ARENA_KB * 1024, name
    return k.nc.alloc_sbuf_tensor_at(name, [P] + list(shape), dtype, offset=ARENA + int(kb * 1024))


def set_up(nc, ins):
    k = Core()
    k.nc, k.ins = nc, ins
    k.pe, k.v = Stream(nc, nc.tensor, "pe"), Stream(nc, nc.vector, "dve")
    k.a, k.g = Stream(nc, nc.scalar, "act"), Stream(nc, nc.gpsimd, "pool")
    k.sp = Stream(nc, nc.sync, "sp")
    k.weights = DmaQueue(nc, k.sp, "weights_in", 4)
    k.loads = DmaQueue(nc, k.a, "loads", 8)
    k.stores = DmaQueue(nc, k.sp, "stores", 4)
    k.const_sems = 0

    k.banks = Banks([nc.alloc_psum_tensor(f"bank{i}", [P, 512], F32) for i in range(8)])
    SLAB = SLAB_K * SLAB_F
    k.raw = Ring([nc.alloc_sbuf_tensor(f"w_raw{i}", [P, SLAB], F32) for i in range(2)])
    k.whi = Ring([nc.alloc_sbuf_tensor(f"w_hi{i}", [P, SLAB], F32R) for i in range(2)])
    k.wlo = Ring([nc.alloc_sbuf_tensor(f"w_lo{i}", [P, SLAB], F32R) for i in range(2)])

    def const(name, shape, dtype=F32):
        t = nc.alloc_sbuf_tensor(name[2:] + "_c", [P] + shape, dtype)
        m = k.loads.start([], t[:], ins[name])
        return t, m

    k.ident, k.m_ident = const("c_ident", [P])
    k.ones, k.m_ones = const("c_ones", [P])
    k.pair, k.m_pair = const("c_pair", [P])
    k.dist, k.m_dist = zip(const("c_dist0", [2 * P]), const("c_dist1", [P]), const("c_dist2", [P]))
    k.causal, k.m_causal = const("c_causal", [P])
    k.causal_neg, k.m_causal_neg = const("c_causal_neg", [P])
    k.zeros = nc.alloc_sbuf_tensor("zeros", [P, 1], F32)
    k.m_zeros = k.v.go([], nc.vector.memset, k.zeros[:], 0.0)
    k.eps = nc.alloc_sbuf_tensor("eps", [P, 1], F32)
    k.m_eps = k.v.go([], nc.vector.memset, k.eps[:], EPS)

    k.turn = 0
    return k


def now(k):
    return [k.pe.now(), k.v.now(), k.a.now(), k.g.now()]


def copy_out(k, after, out, in_, scale=None):
    k.turn += 1
    if k.turn % 2:
        return k.a.go(after, k.nc.scalar.activation, out, in_, ACT.Copy, scale=1.0 if scale is None else scale)
    if scale is None:
        return k.v.go(after, k.nc.vector.tensor_copy, out, in_)
    return k.v.go(after, k.nc.vector.tensor_scalar, out, in_, scale, None, ALU.mult)


def load_vectors(k, stage):
    nc, ins = k.nc, k.ins

    def rows(name, pattern, **kw):
        return ins[name].rearrange(pattern, p=P, **kw)

    lists = [
        ("norm1", rows("norm1", "l (c p) -> (l c) p")), ("b_gate", rows("b_gate", "l (c p) -> (l c) p")),
        ("norm2", rows("norm2", "l (c p) -> (l c) p")), ("conv_w", rows("conv_w", "l w (c p) -> (l w c) p")),
        ("conv_b", rows("conv_b", "l (c p) -> (l c) p")), ("norm_f", rows("norm_f", "(c p) -> c p")),
        ("b_mod", rows("b_mod_2", "l (c p) -> (l c) p")), ("norm_g", rows("norm_g_2", "l n (c p) -> (l n c) p")),
        ("lb", rows("hg_lb_logits_2", "d l (c p) -> (d l c) p")), ("onorm", ins["hg_onorm_2"]),
        ("c", rows("c_2", "o (c p) -> (o c) p")), ("c_ctx", rows("c_ctx_2", "(c p) -> c p")),
        ("subln", None),
    ]
    at, base, loaded = 0, {}, []
    for name, src in lists:
        base[name] = at
        n = DEPTH if src is None else src.shape[0]
        done = 0
        while done < n:
            row, tile = (at + done) % P, (at + done) // P
            m = min(n - done, P - row)
            dst = stage[row:row + m, tile * P:(tile + 1) * P]
            if src is None:
                for h in range(2):
                    loaded.append(k.loads.start([], dst[:, 64 * h:64 * h + 64], ins["da_subln_2"][done:done + m, :]))
            else:
                loaded.append(k.loads.start([], dst, src[done:done + m, :]))
            done += m
        at += n
    k.vecs = nc.alloc_sbuf_tensor("vectors", [P, at], F32)
    bank, k.m_vecs = k.banks.take(), []
    for tile in range(-(-at // P)):
        n = min(P, at - tile * P)
        k.pe.wait(loaded + [k.m_ident])
        done = k.pe.mark(nc.tensor.transpose(bank.ap[:, tile * P:tile * P + n], stage[0:n, tile * P:(tile + 1) * P],
                                             k.ident[0:n, 0:n]))
    k.m_vecs = [k.v.go([done], nc.vector.tensor_copy, k.vecs[:], bank.ap[:, 0:at])]
    k.banks.give(bank, k.m_vecs)
    k.vec = lambda name, i, n=1: k.vecs[:, base[name] + i:base[name] + i + n]



class Weights:

    def __init__(self, k, slabs):
        self.k, self.slabs, self.ready, self.next = k, slabs, [], 0

    def prepare(self):
        if self.next >= len(self.slabs):
            return
        k, nc = self.k, self.k.nc
        name, src, split = self.slabs[self.next]
        nk, nf = src.shape[1], src.shape[2]
        raw = k.raw.take()
        view = lambda t: t[:, 0:nk * nf].rearrange("p (k f) -> p k f", k=nk)
        loaded = k.weights.start(raw.free, view(raw.ap), src)
        if split:
            hi, lo = k.whi.take(), k.wlo.take()
            flat = slice(0, nk * nf)
            m_hi = k.a.go([loaded] + hi.free, nc.scalar.activation, hi.ap[:, flat], raw.ap[:, flat], ACT.Copy)
            m_lo = k.g.go([loaded, m_hi] + lo.free, nc.gpsimd.tensor_tensor, lo.ap[:, flat], raw.ap[:, flat],
                          hi.ap[:, flat].bitcast(F32), ALU.subtract)
            raw.free = [m_lo]
            self.ready.append((name, view(hi.ap), view(lo.ap), [m_hi, m_lo], (hi, lo)))
        else:
            self.ready.append((name, view(raw.ap), None, [loaded], (raw,)))
        self.next += 1

    def take(self, name):
        while not self.ready:
            self.prepare()
        got = self.ready.pop(0)
        assert got[0] == name, (got[0], name)
        if not self.ready:
            self.prepare()
        return got[1:]


def products(pe, nc, out, w_hi, w_lo, x_hi, x_lo, first, last):
    nc.tensor.matmul(out, w_hi, x_hi, start=first, stop=False)
    nc.tensor.matmul(out, w_hi, x_lo, start=False, stop=False)
    return nc.tensor.matmul(out, w_lo, x_hi, start=False, stop=last)


def project(k, name, n_slabs, x_hi, x_lo, x_ready, spans, evacuate, chunk0=0, k0=0, parts=None):
    nc = k.nc
    for s in range(n_slabs):
        w_hi, w_lo, w_ready, slots = k.w.take(name)
        nk, nf = w_hi.shape[1], w_hi.shape[2]
        for j in range(nf // P):
            cols = slice(j * P, (j + 1) * P)
            for part in parts or [(0, nk)]:
                banks = [k.banks.take() for _ in spans]
                k.pe.wait(w_ready + x_ready)
                for (t0, t1), bank in zip(spans, banks):
                    k.pe.wait(bank.free)
                for kk in range(*part):
                    for (t0, t1), bank in zip(spans, banks):
                        last = products(k.pe, nc, bank.ap[:, 0:t1 - t0], w_hi[:, kk, cols], w_lo[:, kk, cols],
                                        x_hi[:, k0 + kk, t0:t1], x_lo[:, k0 + kk, t0:t1],
                                        kk == part[0], kk == part[1] - 1)
                done = k.pe.mark(last)
                chunk = chunk0 + s * (nf // P) + j
                args = (chunk, part[0]) if parts else (chunk,)
                freed = evacuate(*args, [(b.ap[:, 0:t1 - t0], t0, t1) for (t0, t1), b in zip(spans, banks)], done)
                for bank in banks:
                    k.banks.give(bank, freed)
        for slot in slots:
            slot.free = [done]
        yield


def project_tokens(k, name, x_hi, x_lo, x_ready, tiles, evacuate):
    nc = k.nc
    w_hi, w_lo, w_ready, slots = k.w.take(name)
    nk, nf = w_hi.shape[1], w_hi.shape[2]
    for i, tokens in enumerate(tiles):
        bank = k.banks.take()
        k.pe.wait(w_ready + x_ready + bank.free)
        for kk in range(nk):
            last = products(k.pe, nc, bank.ap[:, 0:nf], x_hi[:, kk, tokens], x_lo[:, kk, tokens],
                            w_hi[:, kk, :], w_lo[:, kk, :], kk == 0, kk == nk - 1)
        done = k.pe.mark(last)
        k.banks.give(bank, evacuate(i, bank.ap[:, 0:nf], done))
    for slot in slots:
        slot.free = [done]


def split_into(k, after, hi, lo, value):
    m_hi = k.a.go(after, k.nc.scalar.activation, hi, value, ACT.Copy)
    m_lo = k.v.go([m_hi] + list(after), k.nc.vector.tensor_tensor, lo, value, hi.bitcast(F32), ALU.subtract)
    return [m_hi, m_lo]


def inverse_rms(k, after, chunks, spans, temps, out, width, ones=None, ones_ready=None):
    nc = k.nc
    ones = k.ones if ones is None else ones
    banks = [k.banks.take() for _ in spans]
    for bank in banks:
        k.pe.wait(bank.free)
    k.pe.wait([k.m_ones, k.m_pair])
    n = len(chunks)
    for c, x in enumerate(chunks):
        t = temps.take()
        t0, t1 = spans[0][0], spans[-1][1]
        sq = k.a.go(after + t.free, nc.scalar.activation, t.ap[:, 0:t1 - t0], x[:, t0:t1], ACT.Square)
        k.pe.wait([sq])
        for (a, b), bank in zip(spans, banks):
            last = nc.tensor.matmul(bank.ap[:, 0:b - a], ones[:], t.ap[:, a - t0:b - t0], start=c == 0, stop=c == n - 1)
        t.free = [k.pe.mark(last)]
    marks = []
    for (a, b), bank in zip(spans, banks):
        ln = k.a.go(t.free + [k.m_eps], nc.scalar.activation, out[:, a:b], bank.ap[:, 0:b - a], ACT.Ln,
                    scale=1.0 / width, bias=k.eps[:])
        k.banks.give(bank, [ln])
        marks.append(k.a.go([ln], nc.scalar.activation, out[:, a:b], out[:, a:b], ACT.Exp, scale=-0.5))
    return marks



def transpose_in(k, src, tiles, x, stage, ready):
    nc = k.nc
    loaded = [k.loads.start(ready, stage[:, i, :], src[i * P:(i + 1) * P, :]) for i in range(tiles)]
    marks = []
    for c in range(DC):
        bank = k.banks.take()
        k.pe.wait(loaded + [k.m_ident] + bank.free)
        for i in range(tiles):
            last = nc.tensor.transpose(bank.ap[:, i * P:(i + 1) * P], stage[:, i, c * P:(c + 1) * P], k.ident[:])
        marks.append(copy_out(k, [k.pe.mark(last)] + ready, x[:, c, :], bank.ap[:, 0:tiles * P]))
        k.banks.give(bank, marks[-1:])
    return marks[-2:]


def norm_plain(k, x, x_ready, gain, hi, lo, spans, rstd, temps, out=None):
    nc = k.nc
    t0, t1 = spans[0][0], spans[-1][1]
    ready = inverse_rms(k, x_ready, [x[:, c, :] for c in range(DC)], spans, temps, rstd, D)
    marks = []
    for c in range(DC):
        if out is not None:
            marks = [k.v.go(ready + k.m_vecs, nc.vector.scalar_tensor_tensor, out[:, c, t0:t1], x[:, c, t0:t1],
                            gain(c), rstd[:, t0:t1], ALU.mult, ALU.mult)]
            continue
        t = temps.take()
        n = k.v.go(ready + k.m_vecs + t.free, nc.vector.scalar_tensor_tensor, t.ap[:, t0:t1], x[:, c, t0:t1],
                   gain(c), rstd[:, t0:t1], ALU.mult, ALU.mult)
        marks = split_into(k, [n], hi[:, c, t0:t1], lo[:, c, t0:t1], t.ap[:, t0:t1])
        t.free = marks
    return marks


def by_residue(ap, dil):
    return ap.rearrange("p (l r) -> p r l", r=dil)


def mixer_a(k, l, m, qk, v, qkv_ready, o_hi, o_lo):
    nc = k.nc
    stats = m.stats
    units = [(g, i, par) for g in range(3) for i in range(ST) for par in range(2)]
    state, held, evac = {}, {}, {}

    def keys(g, i):
        return 2 * P if g == 0 and i > 0 else P

    def scores(u):
        g, i, par = u
        n = keys(g, i)
        bank = k.banks.take()
        k.pe.wait(qkv_ready + bank.free)
        for j in range(2):
            rows = slice(HD * par, HD * par + HD)
            last = nc.tensor.matmul(bank.ap[:, j * n:(j + 1) * n], qk[rows, 2 * g + j, i * P:(i + 1) * P],
                                    qk[rows, 6 + 2 * g + j, (i + 1) * P - n:(i + 1) * P], start=True, stop=True)
        done = k.pe.mark(last)
        sb = m.probs.take()
        dist = k.dist[g]
        off = 2 * P - n if g == 0 else 0
        for j in range(2):
            slope = SLOPES[GH * g + 2 * j + par]
            last = k.v.go([done, k.m_dist[g]] + sb.free, nc.vector.scalar_tensor_tensor, sb.ap[:, j * n:(j + 1) * n],
                          dist[:, off:off + n], slope, bank.ap[:, j * n:(j + 1) * n], ALU.mult, ALU.add)
        k.banks.give(bank, [last])
        both = sb.ap[:, 0:2 * n].rearrange("p (j n) -> p j n", j=2)
        neg = stats[:, 0, g, i, par:par + 3:2]
        negmax = k.v.go([last], nc.vector.tensor_reduce, neg, both, AX.X, ALU.max, negate=True)
        for j in range(2):
            h = par + 2 * j
            e = k.a.go([negmax], nc.scalar.activation, both[:, j, :], both[:, j, :], ACT.Exp,
                       bias=stats[:, 0, g, i, h:h + 1], accum_out=stats[:, 1, g, i, h:h + 1])
        state[u] = (sb, e)

    def turn(u):
        g, i, par = u
        n = keys(g, i)
        sb, e = state[u]
        bank = k.banks.take()
        k.pe.wait([e, k.m_ident] + bank.free)
        for b in range(2 * n // P):
            last = nc.tensor.transpose(bank.ap[:, b * P:(b + 1) * P], sb.ap[:, b * P:(b + 1) * P], k.ident[:])
        done = k.pe.mark(last)
        sb.free = [done]
        pt = m.turned.take()
        copied = copy_out(k, [done] + pt.free, pt.ap[:, 0:2 * n], bank.ap[:, 0:2 * n])
        k.banks.give(bank, [copied])
        state[u] = (pt, copied)

    def values(u):
        g, i, par = u
        n = keys(g, i)
        pt, copied = state.pop(u)
        for j in range(2):
            if (g, j) not in held:
                held[g, j] = k.banks.take()
            bank = held[g, j]
            k.pe.wait([copied] + qkv_ready + bank.free)
            h = par + 2 * j
            for b in range(n // P):
                tile = i - (n // P - 1) + b
                last = nc.tensor.matmul(bank.ap[HD * par:HD * par + HD, i * P:(i + 1) * P],
                                        v[:, tile, g * 256 + h * HD:g * 256 + (h + 1) * HD],
                                        pt.ap[:, j * n + b * P:j * n + (b + 1) * P],
                                        start=b == 0, stop=b == n // P - 1)
        done = k.pe.mark(last)
        pt.free = [done]
        if i == ST - 1 and par == 1:
            dil = ORDER[g]
            for j in range(2):
                bank = held[g, j]
                src = bank.ap[:, :] if dil == 1 else bank.ap[:, :].rearrange("p (r l) -> p l r", r=dil)
                dst = m.oa[:, g, j, :] if dil == 1 else m.oa[:, g, j, :].rearrange("p (l r) -> p l r", r=dil)
                evac[g, j] = copy_out(k, [done] + m.start, dst, src)
                k.banks.give(bank, [evac[g, j]])

    yield from pipeline(units, [scores, turn, values])

    def spread(which, g, c):
        bank = k.banks.take()
        k.pe.wait(bank.free + [k.a.now(), k.v.now()])
        for i in range(ST):
            for j in range(2):
                col = stats[:, which, g, i, 2 * c + j:2 * c + j + 1].broadcast_to([P, HD])
                last = nc.tensor.matmul(bank.ap[HD * j:HD * j + HD, i * P:(i + 1) * P], col, k.ident[:],
                                        start=True, stop=True)
        dil = ORDER[g]
        src = bank.ap[:, :] if dil == 1 else bank.ap[:, :].rearrange("p (r l) -> p l r", r=dil)
        return bank, src, [k.pe.mark(last)]

    def natural(t, dil):
        return t if dil == 1 else t.rearrange("p (l r) -> p l r", r=dil)

    mix = Ring(m.mix_buffers)
    for slot in mix.slots:
        slot.free = now(k)
    for c in range(2):
        n = [mix.take() for _ in range(3)]
        marks = []
        for g in range(3):
            bank, src, done = spread(0, g, c)
            marks.append(k.a.go(done + n[g].free, nc.scalar.activation, natural(n[g].ap[:, 0:S], ORDER[g]), src, ACT.Copy))
            k.banks.give(bank, marks[-1:])
        least = mix.take()
        t = k.v.go(marks + least.free, nc.vector.tensor_tensor, least.ap[:, 0:S], n[0].ap[:, 0:S], n[1].ap[:, 0:S], ALU.min)
        t = k.v.go([t], nc.vector.tensor_tensor, least.ap[:, 0:S], least.ap[:, 0:S], n[2].ap[:, 0:S], ALU.min)
        total = mix.take()
        for g in range(3):
            t1 = k.g.go([t], nc.gpsimd.tensor_tensor, n[g].ap[:, 0:S], least.ap[:, 0:S], n[g].ap[:, 0:S], ALU.subtract)
            e = k.a.go([t1], nc.scalar.activation, n[g].ap[:, 0:S], n[g].ap[:, 0:S], ACT.Exp)
            bank, src, done = spread(1, g, c)
            den = mix.take() if g else total
            mul = k.v.go([e] + done + den.free, nc.vector.tensor_tensor, natural(den.ap[:, 0:S], ORDER[g]),
                         natural(n[g].ap[:, 0:S], ORDER[g]), src, ALU.mult)
            k.banks.give(bank, [mul])
            if g:
                mul = k.v.go([mul], nc.vector.tensor_tensor, total.ap[:, 0:S], total.ap[:, 0:S], den.ap[:, 0:S], ALU.add)
                den.free = [mul]
        r = k.v.go([mul], nc.vector.reciprocal, total.ap[:, 0:S], total.ap[:, 0:S])
        for g in range(3):
            p = k.g.go([e, mul, evac[g, c]], nc.gpsimd.tensor_tensor, n[g].ap[:, 0:S], n[g].ap[:, 0:S], m.oa[:, g, c, :], ALU.mult)
        s1 = k.g.go([p], nc.gpsimd.tensor_tensor, n[0].ap[:, 0:S], n[0].ap[:, 0:S], n[1].ap[:, 0:S], ALU.add)
        s2 = k.g.go([s1], nc.gpsimd.tensor_tensor, n[0].ap[:, 0:S], n[0].ap[:, 0:S], n[2].ap[:, 0:S], ALU.add)
        f = k.v.go([s2, r], nc.vector.tensor_tensor, least.ap[:, 0:S], n[0].ap[:, 0:S], total.ap[:, 0:S], ALU.mult)
        marks = split_into(k, [f] + m.start, o_hi[:, c, :], o_lo[:, c, :], least.ap[:, 0:S])
        for slot in n + [least, total]:
            slot.free = marks + [f]
        m.done += marks
        yield


def mixer_b(k, l, m, qk, v, qkv_ready, o_hi, o_lo):
    nc = k.nc
    units = [(c, i, par) for c in range(2) for i in range(ST) for par in range(2)]
    state, held = {}, {}

    def scores(u):
        c, i, par = u
        n = (i + 1) * P
        bank = k.banks.take()
        rows = slice(HD * par, HD * par + HD)
        k.pe.wait(qkv_ready + bank.free)
        done = k.pe.mark(nc.tensor.matmul(bank.ap[:, 0:n], qk[rows, 12 + c, i * P:n], qk[rows, 14 + c, 0:n],
                                          start=True, stop=True))
        z, sp = m.stick.take(), m.stick.take()
        t = k.v.go([done] + z.free, nc.vector.tensor_copy, z.ap[:, 0:n], bank.ap[:, 0:n])
        k.banks.give(bank, [t])
        t = k.a.go([t] + sp.free, nc.scalar.activation, sp.ap[:, 0:n], z.ap[:, 0:n], ACT.Abs)
        t = k.a.go([t], nc.scalar.activation, sp.ap[:, 0:n], sp.ap[:, 0:n], ACT.Exp, scale=-1.0)
        t = k.a.go([t], nc.scalar.activation, sp.ap[:, 0:n], sp.ap[:, 0:n], ACT.Ln, bias=1.0)
        state[u] = (z, sp, t)

    def sums(u):
        c, i, par = u
        n = (i + 1) * P
        z, sp, t = state[u]
        own = slice(i * P, n)
        t = k.v.go([t], nc.vector.scalar_tensor_tensor, sp.ap[:, 0:n], z.ap[:, 0:n], 0.0, sp.ap[:, 0:n], ALU.max, ALU.add)
        t = k.v.go([t, k.m_causal], nc.vector.tensor_tensor, sp.ap[:, own], sp.ap[:, own], k.causal[:], ALU.mult)
        neg = k.g.go([t, k.m_causal_neg], nc.gpsimd.tensor_tensor, z.ap[:, own], z.ap[:, own], k.causal_neg[:], ALU.add)
        back = sp.ap[:, n - 1::-1] if n == S else sp.ap[:, 0:n][:, ::-1]
        t = k.v.go([t, k.m_zeros], nc.vector.tensor_tensor_scan, back, back, k.zeros[:, 0:1].broadcast_to([P, n]), 0.0,
                   ALU.add, ALU.add)
        t = k.v.go([t, neg], nc.vector.tensor_tensor, z.ap[:, 0:n], z.ap[:, 0:n], sp.ap[:, 0:n], ALU.subtract)
        sp.free = [t]
        t = k.a.go([t], nc.scalar.activation, z.ap[:, 0:n], z.ap[:, 0:n], ACT.Exp)
        state[u] = (z, t)

    def turn(u):
        c, i, par = u
        z, t = state[u]
        bank = k.banks.take()
        k.pe.wait([t, k.m_ident] + bank.free)
        for b in range(i + 1):
            last = nc.tensor.transpose(bank.ap[:, b * P:(b + 1) * P], z.ap[:, b * P:(b + 1) * P], k.ident[:])
        done = k.pe.mark(last)
        z.free = [done]
        pt = m.turned.take()
        copied = copy_out(k, [done] + pt.free, pt.ap[:, 0:(i + 1) * P], bank.ap[:, 0:(i + 1) * P])
        k.banks.give(bank, [copied])
        state[u] = (pt, copied)

    def values(u):
        c, i, par = u
        pt, copied = state.pop(u)
        if c not in held:
            held[c] = k.banks.take()
        bank = held[c]
        k.pe.wait([copied] + qkv_ready + bank.free)
        col = 3 * 256 + (2 * c + par) * HD
        for b in range(i + 1):
            last = nc.tensor.matmul(bank.ap[HD * par:HD * par + HD, i * P:(i + 1) * P], v[:, b, col:col + HD],
                                    pt.ap[:, b * P:(b + 1) * P], start=b == 0, stop=b == i)
        done = k.pe.mark(last)
        pt.free = [done]
        if i == ST - 1 and par == 1:
            marks = split_into(k, [done] + m.start, o_hi[:, 2 + c, :], o_lo[:, 2 + c, :], bank.ap[:, :])
            k.banks.give(bank, marks)
            m.done += marks

    yield from pipeline(units, [scores, sums, turn, values])


SPAN1 = [(0, S)]


def first_slabs(ins):
    out = []

    def cols(name, w, r0, nr, c0, nc_, step=SLAB_F):
        for c in range(c0, c0 + nc_, step):
            f = min(step, c0 + nc_ - c)
            out.append((name, w[r0:r0 + nr, c:c + f].rearrange("(k p) f -> p k f", p=P), True))

    for l in range(DEPTH):
        w = ins["w_in"][l]
        cols("qk", w, 0, D, 0, 2 * W_A)
        cols("qk", w, 0, D, 3 * W_A, 2 * W_B)
        cols("v", w, 0, D, 2 * W_A, W_A)
        cols("v", w, 0, D, 3 * W_A + 2 * W_B, W_B)
        for j in range(D // SLAB_F):
            cols("gate_a", w, 0, D, GATE0 + j * SLAB_F, SLAB_F)
            cols("gate_b", w, 0, D, GATE0 + D + j * SLAB_F, SLAB_F)
            cols("branch", ins["w_br"][l], 0, 2 * W_B, j * SLAB_F, SLAB_F)
        cols("w_o", ins["w_o"][l], 0, D, 0, D)
        for c0, n in FF_PARTS1:
            for c in range(0, n, 2):
                m = min(2, n - c)
                cols("up_a", ins["w_up"][l], 0, D, (c0 + c) * P, m * P)
                cols("up_v", ins["w_up"][l], 0, D, FF + (c0 + c) * P, m * P)
            cols("down", ins["w_down"][l], c0 * P, n * P, 0, D)
    return out


FF_PARTS1 = [(0, 8), (8, 8), (16, 6)]


def add_to(k, x, first):
    def evacuate(chunk, banks, done):
        src, t0, t1 = banks[0]
        first[:] = [k.v.go([done], k.nc.vector.tensor_tensor, x[:, chunk, t0:t1], x[:, chunk, t0:t1], src, ALU.add)]
        return first
    return evacuate


def first_layer(k, l, x, x_ready):
    nc = k.nc
    m = Core()
    tag = f"a{l}_"
    start = now(k)
    h = place(k, tag + "h", AT_H, [2, DC, S], F32R)
    o = place(k, tag + "o", AT_H + 32, [2, 4, S], F32R)
    qk = place(k, tag + "qk", AT_WORK, [16, S])
    v = place(k, tag + "v", AT_WORK + 32, [ST, W_A + W_B])
    m.oa = place(k, tag + "oa", AT_WORK + 48, [3, 2, S])
    temps = [place(k, f"{tag}t{i}", AT_WORK + 60 + 2 * i, [S]) for i in range(8)]
    m.stats = place(k, tag + "stats", AT_WORK + 76, [2, 3, ST, GH])
    rstd = temps[7]

    def fresh(aps):
        r = Ring(aps)
        for s in r.slots:
            s.free = now(k)
        return r

    norm_temps = fresh(temps[0:3])
    k.v.wait(start), k.a.wait(start)
    h_ready = norm_plain(k, x, x_ready + start, lambda c: k.vec("norm1", DC * l + c), h[:, 0], h[:, 1], SPAN1, rstd,
                         norm_temps)

    qkv = []

    def keep_qk(chunk, banks, done):
        src = banks[0][0]
        dst = qk[:, chunk, :]
        query = chunk < 6 or chunk in (12, 13)
        group = chunk % 6 // 2 if chunk < 12 else 0
        if group:
            dil = ORDER[group]
            src, dst = by_residue(src, dil), dst.rearrange("p (r l) -> p r l", r=dil)
        mark = copy_out(k, [done] + start, dst, src, HD ** -0.5 if query else None)
        qkv.append(mark)
        return [mark]

    def keep_v(g):
        def evacuate(i, src, done):
            mark = copy_out(k, [done] + start, v[:, i, g * 256:(g + 1) * 256], src)
            qkv.append(mark)
            return [mark]
        return evacuate

    for _ in project(k, "qk", 8, h[:, 0], h[:, 1], h_ready, SPAN1, keep_qk):
        pass
    for g in range(4):
        dil = ORDER[g] if g < 3 else 1
        tiles = [slice(i * P, (i + 1) * P) if dil == 1 else slice(i, S, dil) for i in range(ST)]
        project_tokens(k, "v", h[:, 0], h[:, 1], h_ready, tiles, keep_v(g))
    qkv = [k.a.now(), k.v.now()]

    m.start, m.done = start, []
    m.stick = fresh(temps[0:6])
    m.turned = fresh(temps[6:8])
    for _ in mixer_b(k, l, m, qk, v, qkv, o[:, 0], o[:, 1]):
        pass
    m.probs = fresh(temps[0:3])
    m.turned = fresh(temps[3:6])
    m.mix_buffers = temps[0:8]
    for _ in mixer_a(k, l, m, qk, v, qkv, o[:, 0], o[:, 1]):
        pass

    attended = now(k)
    merged = place(k, tag + "merged", AT_WORK, [2, DC, S], F32R)
    gates = {"gate_a": [place(k, f"{tag}ga{i}", AT_WORK + 32 + 2 * i, [S]) for i in range(2)],
             "gate_b": [place(k, f"{tag}gb{i}", AT_WORK + 36 + 2 * i, [S]) for i in range(2)]}
    branch = fresh([place(k, f"{tag}br{i}", AT_WORK + 40 + 2 * i, [S]) for i in range(4)])
    gate_ready, gate_free, half, merged_ready = {}, {}, {}, []

    def gate(name, base):
        def evacuate(chunk, banks, done):
            slot = gates[name][chunk % 2]
            mark = k.a.go([done] + k.m_vecs + attended + gate_free.get((name, chunk % 2), []), nc.scalar.activation,
                          slot[:], banks[0][0], ACT.Sigmoid, bias=k.vec("b_gate", 16 * l + base + chunk))
            gate_ready[name, chunk] = mark
            return [mark]
        return evacuate

    def merge(chunk, part, banks, done):
        name = "gate_a" if part == 0 else "gate_b"
        t = branch.take()
        mark = k.v.go([done, gate_ready[name, chunk]] + t.free, nc.vector.tensor_tensor, t.ap[:], banks[0][0],
                      gates[name][chunk % 2][:], ALU.mult)
        gate_free[name, chunk % 2] = [mark]
        if part == 0:
            half[chunk] = t
            return [mark]
        a = half.pop(chunk)
        total = k.v.go([mark], nc.vector.tensor_tensor, a.ap[:], a.ap[:], t.ap[:], ALU.add)
        t.free = [total]
        a.free = split_into(k, [total] + attended, merged[:, 0, chunk, :], merged[:, 1, chunk, :], a.ap[:])
        merged_ready[:] = a.free
        return [mark]

    for j in range(D // SLAB_F):
        for _ in project(k, "gate_a", 1, h[:, 0], h[:, 1], h_ready, SPAN1, gate("gate_a", 0), 2 * j):
            pass
        for _ in project(k, "gate_b", 1, h[:, 0], h[:, 1], h_ready, SPAN1, gate("gate_b", DC), 2 * j):
            pass
        for _ in project(k, "branch", 1, o[:, 0], o[:, 1], m.done, SPAN1, merge, 2 * j, parts=[(0, 2), (2, 4)]):
            pass
    added = []
    for _ in project(k, "w_o", 4, merged[:, 0], merged[:, 1], merged_ready, SPAN1, add_to(k, x, added)):
        pass

    mixed = now(k)
    norm_temps = fresh(temps[0:3])
    h_ready = norm_plain(k, x, added + mixed, lambda c: k.vec("norm2", DC * l + c), h[:, 0], h[:, 1], SPAN1, rstd,
                         norm_temps)
    hidden = place(k, tag + "hidden", AT_WORK, [2, 8, S], F32R)
    conv = fresh([place(k, f"{tag}cv{i}", AT_WORK + 32 + 2 * i, [S]) for i in range(6)])
    acts = {}
    hidden_ready, hidden_free = [], mixed

    def tap(i, c):
        return k.vec("conv_w", (3 * l + i) * FC + c)

    def up_a(chunk, banks, done):
        src, c = banks[0][0], conv.take()
        t = k.a.go([done] + k.m_vecs + c.free, nc.scalar.activation, c.ap[:], src, ACT.Identity, scale=tap(2, chunk),
                   bias=k.vec("conv_b", FC * l + chunk))
        t = k.v.go([t], nc.vector.scalar_tensor_tensor, c.ap[:, 1:S], src[:, 0:S - 1], tap(1, chunk), c.ap[:, 1:S],
                   ALU.mult, ALU.add)
        t = k.v.go([t], nc.vector.scalar_tensor_tensor, c.ap[:, 2:S], src[:, 0:S - 2], tap(0, chunk), c.ap[:, 2:S],
                   ALU.mult, ALU.add)
        acts[chunk] = (c, k.a.go([t], nc.scalar.activation, c.ap[:], c.ap[:], ACT.Gelu))
        return [t]

    def up_v(c0):
        def evacuate(chunk, banks, done):
            c, t = acts.pop(chunk)
            t = k.v.go([done, t], nc.vector.tensor_tensor, c.ap[:], c.ap[:], banks[0][0], ALU.mult)
            c.free = split_into(k, [t] + hidden_free, hidden[:, 0, chunk - c0, :], hidden[:, 1, chunk - c0, :], c.ap[:])
            hidden_ready[:] = c.free
            return [t]
        return evacuate

    for c0, n in FF_PARTS1:
        for c in range(0, n, 2):
            for _ in project(k, "up_a", 1, h[:, 0], h[:, 1], h_ready, SPAN1, up_a, c0 + c):
                pass
            for _ in project(k, "up_v", 1, h[:, 0], h[:, 1], h_ready, SPAN1, up_v(c0), c0 + c):
                pass
        for _ in project(k, "down", 4, hidden[:, 0], hidden[:, 1], hidden_ready, SPAN1, add_to(k, x, added)):
            pass
        hidden_free = [k.pe.now()]
    return added



def transpose_out(k, x, ready, out):
    nc = k.nc
    stage = place(k, "out_rows", AT_WORK, [ST, D])
    stored = []
    for i in range(ST):
        marks = []
        for half in range(2):
            bank = k.banks.take()
            k.pe.wait(ready + bank.free)
            for c in range(4):
                last = nc.tensor.transpose(bank.ap[:, c * P:(c + 1) * P], x[:, 4 * half + c, i * P:(i + 1) * P], k.ident[:])
            marks.append(copy_out(k, [k.pe.mark(last)] + ready, stage[:, i, half * 512:(half + 1) * 512], bank.ap[:, :]))
            k.banks.give(bank, marks[-1:])
        stored.append(k.stores.start(marks, out[i * P:(i + 1) * P, :], stage[:, i, :]))
    k.sp.wait(stored)




IN2 = {"q": 0, "v": 512, "g": 1024, "f": 1536, "b": 2048, "dq": 2560, "dk": 2816, "dv": 3072, "ft": 3328}
FF_PARTS2 = [(0, 6), (6, 6), (12, 5), (17, 5)]
LAT, CTXS = (0, S), (S, T2)


def slab_list(out, name, w, r0, nr, c0, n, split=True):
    for c in range(c0, c0 + n, SLAB_F):
        f = min(SLAB_F, c0 + n - c)
        out.append((name, w[r0:r0 + nr, c:c + f].rearrange("(k p) f -> p k f", p=P), split))


def modulation_slabs(ins):
    out = []
    for l in range(DEPTH):
        slab_list(out, "mod", ins["w_mod_2"][l], 0, D, 0, 6 * D, split=False)
    return out


def second_slabs(ins):
    out = []
    for l in range(DEPTH):
        w = ins["w_in_2"][l]
        for name in ("ft", "dq", "dk", "dv"):
            slab_list(out, name, w, 0, D, IN2[name], 256)
        for pair in range(2):
            for name in ("q", "v", "f", "b", "g"):
                slab_list(out, name, w, 0, D, IN2[name] + 256 * pair, 256)
        slab_list(out, "w_out", ins["w_out_2"][l], 0, D, 0, D)
        for c0, n in FF_PARTS2:
            for c in range(0, n, 2):
                w_ = min(2, n - c) * P
                slab_list(out, "ff_g", ins["w_ffn_in_2"][l], 0, D, (c0 + c) * P, w_)
                slab_list(out, "ff_u", ins["w_ffn_in_2"][l], 0, D, FF + (c0 + c) * P, w_)
            slab_list(out, "ff_out", ins["w_ffn_out_2"][l], c0 * P, n * P, 0, D)
    return out


def second_set_up(k):
    nc, ins = k.nc, k.ins
    v, a = nc.vector, nc.scalar

    def small(name, shape, dtype=F32):
        return nc.alloc_sbuf_tensor(name, [P] + shape, dtype)

    k.cond = small("cond", [DC, 2])
    sig = small("cond_sigmoid", [DC, 2])
    for j, name in enumerate(("c", "c_ctx")):
        t = k.a.go(k.m_vecs, a.activation, sig[:, :, j], k.vec(name, 0, DC), ACT.Sigmoid)
        k.m_cond = [k.v.go([t], v.tensor_tensor, k.cond[:, :, j], sig[:, :, j], k.vec(name, 0, DC), ALU.mult)]
    k.mod = [small(f"mod{l}", [6 * DC, 2]) for l in range(DEPTH)]

    lo = small("lb_logits_e", [2, DEPTH, HGH])
    k.lb, k.lb1 = small("lower_bound", [DEPTH, 2, HGH]), small("one_less_bound", [DEPTH, 2, HGH])
    mx, den = small("lb_max", [2, HGH]), small("lb_den", [2, HGH])
    logits = k.vec("lb", 0, 2 * DEPTH * HGH).rearrange("p (d l c) -> p d l c", d=2, l=DEPTH)
    t = k.v.go(k.m_vecs, v.tensor_tensor, mx[:], logits[:, :, 0, :], logits[:, :, 1, :], ALU.max)
    for l in range(DEPTH):
        u = k.v.go([t], v.tensor_tensor, lo[:, :, l, :], logits[:, :, l, :], mx[:], ALU.subtract)
    u = k.a.go([u], a.activation, lo[:], lo[:], ACT.Exp)
    t = k.v.go([u], v.tensor_tensor, den[:], lo[:, :, 0, :], lo[:, :, 1, :], ALU.add)
    t = k.v.go([t], v.reciprocal, den[:], den[:])
    for l in range(DEPTH):
        u = k.v.go([t], v.tensor_tensor, lo[:, :, l, :], lo[:, :, l, :], den[:], ALU.mult)
    t = k.v.go([u], v.tensor_tensor, mx[:], lo[:, :, 0, :], lo[:, :, 1, :], ALU.add)
    t0 = k.v.go([t], v.tensor_tensor, k.lb[:, 0], lo[:, :, 0, :], lo[:, :, 0, :], ALU.subtract)
    t1 = k.v.go([t], v.tensor_tensor, k.lb[:, 1], mx[:], lo[:, :, 0, :], ALU.subtract)
    k.m_lb = [k.v.go([t0, t1], v.tensor_scalar, k.lb1[:], k.lb[:], -1.0, 1.0, ALU.mult, ALU.add)]

    dl = place(k, "da_lambda", AT_WORK + 70, [DEPTH, 4, 32])
    loaded = k.loads.start([], dl[:], ins["da_lambda_2"].rearrange("l n d -> (l n d)").partition_broadcast(P))
    prod, sums, lam = place(k, "lambda_prod", AT_WORK + 71, [DEPTH, 2, 32]), small("lambda_sum", [DEPTH, 2]), small("minus_lambda", [DEPTH])
    t = k.v.go([loaded], v.tensor_tensor, prod[:], dl[:, :, 0::2, :], dl[:, :, 1::2, :], ALU.mult)
    t = k.v.go([t], v.tensor_reduce, sums[:], prod[:], AX.X, ALU.add)
    t = k.a.go([t], a.activation, sums[:], sums[:], ACT.Exp)
    k.sub = small("subln_gain", [DEPTH])
    for l in range(DEPTH):
        init = lambda_init(l)
        u = k.v.go([t], v.scalar_tensor_tensor, lam[:, l:l + 1], sums[:, l, 1:2], -init, sums[:, l, 0:1], ALU.add, ALU.subtract)
        u = k.v.go(k.m_vecs, v.tensor_scalar, k.sub[:, l:l + 1], k.vec("subln", l), 1.0 - init, None, ALU.mult)
    k.neg_lam, k.m_lam = lam, [u]

    k.resets = nc.alloc_sbuf_tensor("resets", [P, T2 + 1], mybir.dt.bfloat16)
    t = k.v.go([], v.memset, k.resets[:], 1.0)
    k.m_resets = [k.v.go([t], v.memset, k.resets[:, 0:T2 + 1:P], 0.0)]
    k.decays = small("tile_decays", [ST + CT])
    k.gains = [[small(f"gain{l}_{i}", [DC, 2]) for i in range(4)] for l in range(DEPTH)]


def lambda_init(l):
    return 0.8 - 0.6 * math.exp(-0.3 * l)


def modulate(k):
    nc = k.nc
    for l in range(DEPTH):
        for s in range(6 * D // SLAB_F):
            w, _, ready, slots = k.w.take("mod")
            bank = k.banks.take()
            k.pe.wait(ready + k.m_cond + bank.free)
            for j in range(2):
                for kk in range(DC):
                    last = nc.tensor.matmul(bank.ap[:, 2 * j:2 * j + 2], w[:, kk, j * P:(j + 1) * P], k.cond[:, kk, :],
                                            start=kk == 0, stop=kk == DC - 1)
            done = k.pe.mark(last)
            slots[0].free = [done]
            bias = k.vec("b_mod", 6 * DC * l + 2 * s, 2).unsqueeze(2).broadcast_to([P, 2, 2])
            t = k.v.go([done], nc.vector.tensor_tensor, k.mod[l][:, 2 * s:2 * s + 2, :],
                       bank.ap[:, 0:4].rearrange("p (j n) -> p j n", j=2), bias, ALU.add)
            k.banks.give(bank, [t])
            yield
        for i, (m, add) in enumerate(((1, 1.0), (2, 0.0), (4, 1.0), (5, 0.0))):
            for j in range(2):
                k.m_gain = k.v.go([t], nc.vector.scalar_tensor_tensor, k.gains[l][i][:, :, j],
                                  k.mod[l][:, m * DC:(m + 1) * DC, j], add, k.vec("norm_g", (4 * l + i) * DC, DC),
                                  ALU.add, ALU.mult)
        yield


def adaln(k, l, which, x, x_ready, hi, lo, sides, rstd, temps):
    nc = k.nc
    spans = [LAT, CTXS][0:sides]
    end = spans[-1][1]
    ready = inverse_rms(k, x_ready, [x[:, c, :] for c in range(DC)], spans, temps, rstd, D)
    gain, shift = k.gains[l][2 * which], 3 * DC * which
    marks = []
    for c in range(DC):
        t = temps.take()
        marks = []
        for j, (a, b) in enumerate(spans):
            n = k.v.go(ready + t.free + [k.m_gain], nc.vector.scalar_tensor_tensor, t.ap[:, a:b], x[:, c, a:b],
                       gain[:, c, j:j + 1], rstd[:, a:b], ALU.mult, ALU.mult)
            add = k.mod[l][:, shift + c, j:j + 1]
            m_hi = k.a.go([n] + x_ready, nc.scalar.activation, hi[:, c, a:b], t.ap[:, a:b], ACT.Identity, bias=add)
            m_lo = k.v.go([m_hi, n], nc.vector.scalar_tensor_tensor, lo[:, c, a:b], t.ap[:, a:b], add,
                          hi[:, c, a:b].bitcast(F32), ALU.add, ALU.subtract)
            marks += [m_hi, m_lo]
        t.free = marks
    return marks


def add_normed(k, l, which, x, y, y_ready, sides, rstd, temps):
    nc = k.nc
    spans = [LAT, CTXS][0:sides]
    ready = inverse_rms(k, y_ready, [y[:, c, :] for c in range(DC)], spans, temps, rstd, D)
    gain = k.gains[l][2 * which + 1]
    for c in range(DC):
        for j, (a, b) in enumerate(spans):
            n = k.v.go(ready, nc.vector.scalar_tensor_tensor, y[:, c, a:b], y[:, c, a:b], gain[:, c, j:j + 1],
                       rstd[:, a:b], ALU.mult, ALU.mult)
            last = k.g.go([n], nc.gpsimd.tensor_tensor, x[:, c, a:b], x[:, c, a:b], y[:, c, a:b], ALU.add)
    return [last]


def fourier(k, l, h, h_ready, y, start, sides):
    nc = k.nc
    tag = f"b{l}_"
    u = place(k, tag + "u", AT_WORK + 24, [2, T2])
    half = place(k, tag + "half", AT_WORK + 30, [ST + CT, 2, 2, P])
    dl = place(k, tag + "dftl", AT_WORK + 42, [2, ST, S])
    dc = place(k, tag + "dftc", AT_WORK + 58, [2, CT, CTX])
    dft64 = place(k, tag + "dft64", AT_WORK + 62, [2, P])
    m_dl = k.loads.start(start, dl[:], k.ins["c_dftl"])
    m_64 = k.loads.start(start, dft64[:], k.ins["c_dft64"])
    m_dc = k.loads.start(start, dc[:], k.ins["c_dftc"])
    spans = [LAT, CTXS][0:sides]
    ready = []

    def keep(chunk, banks, done):
        ready[:] = ready[-2:] + [copy_out(k, [done] + start, u[:, chunk, a:b], src) for src, a, b in banks]
        return ready[-len(banks):]

    yield from project(k, "ft", 1, h[:, 0], h[:, 1], h_ready, spans, keep)
    ready = [k.a.now(), k.v.now()]
    tiles = ST + CT if sides == 2 else ST
    for i in range(tiles):
        bank = k.banks.take()
        k.pe.wait(ready + [m_64] + bank.free)
        for c in range(2):
            last = nc.tensor.matmul(bank.ap[:, 256 * c:256 * c + 256], u[:, c, i * P:(i + 1) * P],
                                    dft64[:].rearrange("p s f -> p (s f)"), start=True, stop=True)
        mark = copy_out(k, [k.pe.mark(last)] + start, half[:, i].rearrange("p c s f -> p (c s f)"), bank.ap[:, :])
        k.banks.give(bank, [mark])
    ready = [k.a.now(), k.v.now()]
    for c in range(2):
        for (a, b), mat, m_mat, i0, n in ((LAT, dl, m_dl, 0, ST), (CTXS, dc, m_dc, ST, CT))[0:sides]:
            bank = k.banks.take()
            k.pe.wait(ready + [m_mat] + bank.free)
            for i in range(n):
                for s in range(2):
                    last = nc.tensor.matmul(bank.ap[:, 0:b - a], half[:, i0 + i, c, s, :], mat[:, s, i, :],
                                            start=i + s == 0, stop=i == n - 1 and s == 1)
            mark = copy_out(k, [k.pe.mark(last)] + start, y[:, 6 + c, a:b], bank.ap[:, 0:b - a])
            k.banks.give(bank, [mark])
        yield


def diff_attention(k, l, h, h_ready, y, sides):
    nc = k.nc
    tag = f"b{l}_"
    start = now(k)
    at = AT_WORK + 24
    dq, dk = place(k, tag + "dq", at, [2, T2]), place(k, tag + "dk", at + 6, [2, T2])
    dv = place(k, tag + "dv", at + 12, [ST + CT, 256])
    cos, sin = place(k, tag + "cos", at + 18, [S]), place(k, tag + "sin", at + 20, [S])
    probs = Ring([place(k, f"{tag}p{i}", at + 22 + 6 * i, [2, T2]) for i in range(2)])
    turned = Ring([place(k, f"{tag}pt{i}", at + 34 + 3 * i, [ST + CT, P]) for i in range(2)])
    temps = Ring([place(k, f"{tag}dt{i}", at + 40 + 3 * i, [T2]) for i in range(3)])
    stats = Ring([place(k, f"{tag}ds{i}", at + 49 + 0.5 * i, [16]) for i in range(4)])
    for r in (probs, turned, temps, stats):
        for slot in r.slots:
            slot.free = start
    m_cos, m_sin = k.loads.start(start, cos[:], k.ins["c_cos"]), k.loads.start(start, sin[:], k.ins["c_sin"])
    rot = place(k, tag + "rot", at + 51, [P])
    m_rot = k.loads.start(start, rot[:], k.ins["c_rot"])
    scale = 32 ** -0.5

    def keep(dst, spans):
        def evacuate(chunk, banks, done):
            marks = [copy_out(k, [done] + start, dst[:, chunk, a:b], src) for src, a, b in banks]
            bank = k.banks.take()
            k.pe.wait(marks[0:1] + [m_rot] + bank.free)
            done = k.pe.mark(nc.tensor.matmul(bank.ap[:, :], rot[:], dst[:, chunk, 0:S], start=True, stop=True))
            t = temps.take()
            m1 = k.v.go([done, m_sin] + t.free, nc.vector.tensor_tensor, t.ap[:, 0:S], bank.ap[:, :], sin[:], ALU.mult)
            k.banks.give(bank, [m1])
            m2 = k.g.go([done, m_cos], nc.gpsimd.tensor_tensor, dst[:, chunk, 0:S], dst[:, chunk, 0:S], cos[:], ALU.mult)
            t.free = [k.v.go([m1, m2], nc.vector.tensor_tensor, dst[:, chunk, 0:S], dst[:, chunk, 0:S], t.ap[:, 0:S],
                             ALU.add)]
            return marks
        return evacuate

    both = [LAT, CTXS]
    yield from project(k, "dq", 1, h[:, 0], h[:, 1], h_ready, both[0:sides], keep(dq, both[0:sides]))
    yield from project(k, "dk", 1, h[:, 0], h[:, 1], h_ready, both, keep(dk, both))

    def keep_v(i, src, done):
        return [copy_out(k, [done] + start, dv[:, i, :], src)]

    project_tokens(k, "dv", h[:, 0], h[:, 1], h_ready, [slice(i * P, (i + 1) * P) for i in range(ST + CT)], keep_v)
    yield
    ready = [k.a.now(), k.v.now()]
    units = [(c, i, par) for c in range(2) for i in range(ST + CT if sides == 2 else ST) for par in range(2)]
    state, held = {}, {}

    def key_span(i):
        return both if i < ST else both[1:]

    def scores(u):
        c, i, par = u
        p, st = probs.take(), stats.take()
        spans = key_span(i)
        n = len(spans)
        m_exp = []
        banks = {}
        for m in range(2):
            rows = slice(64 * par + 32 * m, 64 * par + 32 * m + 32)
            for j, (a, b) in enumerate(spans):
                bank = banks[m, j] = k.banks.take()
                k.pe.wait(ready + bank.free)
                done = k.pe.mark(nc.tensor.matmul(bank.ap[:, 0:b - a], dq[rows, c, i * P:(i + 1) * P], dk[rows, c, a:b],
                                                  start=True, stop=True, tile_position=(64 * par + 32 * m, 0)))
                t = k.v.go([done] + st.free, nc.vector.tensor_reduce, st.ap[:, 2 * m + j:2 * m + j + 1],
                           bank.ap[:, 0:b - a], AX.X, ALU.max)
        for m in range(2):
            top = st.ap[:, 2 * m:2 * m + 1] if n == 1 else st.ap[:, 2 * m:2 * m + 2]
            t = k.v.go([t], nc.vector.tensor_reduce, st.ap[:, 12 + m:13 + m], top, AX.X, ALU.max)
        t = k.v.go([t], nc.vector.tensor_scalar, st.ap[:, 4:6], st.ap[:, 12:14], -scale, None, ALU.mult)
        for m in range(2):
            for j, (a, b) in enumerate(spans):
                e = k.a.go([t] + p.free, nc.scalar.activation, p.ap[:, m, a:b], banks[m, j].ap[:, 0:b - a], ACT.Exp,
                           bias=st.ap[:, 4 + m:5 + m], scale=scale, accum_out=st.ap[:, 6 + 2 * m + j:7 + 2 * m + j])
                k.banks.give(banks[m, j], [e])
        if n == 2:
            t = k.v.go([e], nc.vector.tensor_tensor, st.ap[:, 10:12], st.ap[:, 6:10:2], st.ap[:, 7:11:2], ALU.add)
        else:
            t = k.v.go([e], nc.vector.tensor_copy, st.ap[:, 10:12], st.ap[:, 6:10:2])
        t = k.v.go([t], nc.vector.reciprocal, st.ap[:, 12:14], st.ap[:, 10:12])
        t = k.v.go([t] + k.m_lam, nc.vector.tensor_tensor, st.ap[:, 14:15], st.ap[:, 13:14], k.neg_lam[:, l:l + 1], ALU.mult)
        a, b = spans[0][0], spans[-1][1]
        t = k.v.go([t], nc.vector.tensor_scalar, p.ap[:, 0, a:b], p.ap[:, 0, a:b], st.ap[:, 12:13], None, ALU.mult)
        t = k.v.go([t], nc.vector.scalar_tensor_tensor, p.ap[:, 0, a:b], p.ap[:, 1, a:b], st.ap[:, 14:15],
                   p.ap[:, 0, a:b], ALU.mult, ALU.add)
        st.free = [t]
        state[u] = (p, t)

    def turn(u):
        c, i, par = u
        p, t = state[u]
        pt = turned.take()
        tiles = range(0 if i < ST else ST, ST + CT)
        marks = []
        for group in (range(0, 3), range(3, 6)) if i < ST else (range(4, 6),):
            bank = k.banks.take()
            k.pe.wait([t] + bank.free)
            for n, b in enumerate(group):
                last = nc.tensor.transpose(bank.ap[:, n * P:(n + 1) * P], p.ap[:, 0, b * P:(b + 1) * P], k.ident[:])
            done = k.pe.mark(last)
            marks.append(copy_out(k, [done] + pt.free, pt.ap[:, group[0]:group[-1] + 1, :].rearrange("p b q -> p (b q)"),
                                  bank.ap[:, 0:len(group) * P]))
            k.banks.give(bank, marks[-1:])
        p.free = [done]
        state[u] = (pt, marks)

    def values(u):
        c, i, par = u
        pt, marks = state.pop(u)
        side = 0 if i < ST else 1
        if (c, side) not in held:
            held[c, side] = k.banks.take()
        bank = held[c, side]
        k.pe.wait(marks + ready + bank.free)
        tiles = list(range(0 if side == 0 else ST, ST + CT))
        q0 = (i - ST * side) * P
        for b in tiles:
            last = nc.tensor.matmul(bank.ap[64 * par:64 * par + 64, q0:q0 + P], dv[:, b, (2 * c + par) * 64:(2 * c + par + 1) * 64],
                                    pt.ap[:, b, :], start=b == tiles[0], stop=b == tiles[-1])
        done = k.pe.mark(last)
        pt.free = [done]
        if par == 1 and i in (ST - 1, ST + CT - 1):
            a, b = both[side]
            m1 = copy_out(k, [done], y[:, 4 + c, a:b], bank.ap[:, 0:b - a])
            k.banks.give(bank, [m1])
            rstd = temps.take()
            k.a.wait(rstd.free)
            root = inverse_rms(k, [m1], [y[:, 4 + c, :]], [(a, b)], temps, rstd.ap, 64, ones=k.pair)
            rstd.free = [k.v.go(root + k.m_lam, nc.vector.scalar_tensor_tensor, y[:, 4 + c, a:b], y[:, 4 + c, a:b],
                                k.sub[:, l:l + 1], rstd.ap[:, a:b], ALU.mult, ALU.mult)]

    yield from pipeline(units, [scores, turn, values])


def recurrent(k, l, h, h_ready, y, sides):
    nc = k.nc
    tag = f"b{l}_"
    at = AT_WORK + 24
    spans = [LAT, CTXS]
    gla = k.nc.alloc_sbuf_tensor_at(tag + "gla", [P, 2, LEVELS + 1, P], U8, offset=ARENA + (at + 51) * 1024)
    wide = place(k, tag + "gla_wide", at, [2, LEVELS + 1, P])
    loaded = k.loads.start(now(k), wide[:], k.ins["c_gla"])
    m_gla = k.g.go(now(k) + [loaded], nc.gpsimd.tensor_copy, gla[:], wide[:])
    for pair in range(2):
        start = now(k)
        nm = f"{tag}r{pair}_"
        q, v = place(k, nm + "q", at, [2, T2]), place(k, nm + "v", at + 6, [ST + CT, 256])
        gates = [place(k, nm + "f", at + 12, [2, T2]), place(k, nm + "b", at + 18, [2, T2])]
        g = place(k, nm + "g", at + 24, [2, T2])
        ex = Ring([place(k, f"{nm}ex{i}", at + 30 + 3 * i, [T2]) for i in range(3)])
        kk, bc, sc = [place(k, nm + n, at + 39 + 3 * i, [T2]) for i, n in enumerate(("k", "bc", "sc"))]
        kdt = place(k, nm + "kdt", at + 48, [ST + CT, P])
        dec = k.decays
        for slot in ex.slots:
            slot.free = start

        def keep_silu(dst):
            def evacuate(chunk, banks, done):
                marks = []
                for src, a, b in banks:
                    t = k.a.go([done] + start, nc.scalar.activation, dst[:, chunk, a:b], src, ACT.Sigmoid)
                    marks.append(k.v.go([t], nc.vector.tensor_tensor, dst[:, chunk, a:b], dst[:, chunk, a:b], src, ALU.mult))
                return marks
            return evacuate

        def keep_gate(d):
            def evacuate(chunk, banks, done):
                marks = []
                hc = 2 * pair + chunk
                for src, a, b in banks:
                    t = k.a.go([done] + start, nc.scalar.activation, gates[d][:, chunk, a:b], src, ACT.Sigmoid)
                    marks.append(t)
                    t = k.v.go([t] + k.m_lb, nc.vector.tensor_scalar, gates[d][:, chunk, a:b], gates[d][:, chunk, a:b],
                               k.lb1[:, l, d, hc:hc + 1], k.lb[:, l, d, hc:hc + 1], ALU.mult, ALU.add)
                return marks
            return evacuate

        def keep_v(i, src, done):
            return [copy_out(k, [done] + start, v[:, i, :], src)]

        yield from project(k, "q", 1, h[:, 0], h[:, 1], h_ready, spans[0:sides], keep_silu(q))
        project_tokens(k, "v", h[:, 0], h[:, 1], h_ready, [slice(i * P, (i + 1) * P) for i in range(ST + CT)], keep_v)
        yield
        yield from project(k, "f", 1, h[:, 0], h[:, 1], h_ready, spans, keep_gate(0))
        yield from project(k, "b", 1, h[:, 0], h[:, 1], h_ready, spans, keep_gate(1))
        yield from project(k, "g", 1, h[:, 0], h[:, 1], h_ready, spans[0:sides], keep_silu(g))
        ready = [k.a.now(), k.v.now()]
        tiles = ST + CT if sides == 2 else ST
        T = tiles * P
        bank_tiles = [(0, ST), (ST, ST + CT)][0:sides]

        for hh in range(2):
            for d in range(2):
                unit = now(k)
                f, qh = gates[d][:, hh, :], q[:, hh, :]
                m_k = k.g.go(unit, nc.gpsimd.tensor_scalar, kk[:], f, -1.0, 1.0, ALU.mult, ALU.add)
                t = k.v.go(unit + [m_k], nc.vector.tensor_scalar, f, f, 2.0 ** -64, None, ALU.max)
                t = k.a.go([t], nc.scalar.activation, f, f, ACT.Ln)
                if d == 0:
                    m_b = k.v.go([t] + k.m_resets, nc.vector.tensor_tensor_scan, bc[:], k.resets[:, 0:T2], f, 0.0,
                                 ALU.mult, ALU.add)
                else:
                    m_b = k.v.go([t] + k.m_resets, nc.vector.tensor_tensor_scan, bc[:, ::-1], k.resets[:, T2:0:-1],
                                 f[:, ::-1], 0.0, ALU.mult, ALU.add)
                m_sc = k.g.go(unit, nc.gpsimd.memset, sc[:, 0:T], 0.0)

                def level(lv):
                    x = ex.take()
                    if lv < LEVELS:
                        m = 1 << lv
                        bp = bc[:, 0:T].rearrange("p (n s m) -> p n s m", s=2, m=m)
                        xp = x.ap[:, 0:T].rearrange("p (n s m) -> p n s m", s=2, m=m)
                        key, query = (0, 1) if d == 0 else (1, 0)
                        edge = bp[:, :, 0, m - 1:m] if d == 0 else bp[:, :, 1, 0:1]
                        edge = edge.broadcast_to([P, T // (2 * m), m])
                        a1 = k.g.go([m_b] + x.free, nc.gpsimd.tensor_tensor, xp[:, :, key, :], edge, bp[:, :, key, :], ALU.subtract)
                        a2 = k.g.go([m_b], nc.gpsimd.tensor_tensor, xp[:, :, query, :], bp[:, :, query, :], edge, ALU.subtract)
                        e = k.a.go([a1, a2], nc.scalar.activation, x.ap[:, 0:T], x.ap[:, 0:T], ACT.Exp)
                        src = lambda ap: ap[:, 0:T].rearrange("p (n s m) -> p n s m", s=2, m=m)
                        k.v.go([e, m_k], nc.vector.tensor_tensor, xp[:, :, key, :], xp[:, :, key, :], src(kk)[:, :, key, :], ALU.mult)
                        e = k.v.go([e], nc.vector.tensor_tensor, xp[:, :, query, :], xp[:, :, query, :], src(qh)[:, :, query, :], ALU.mult)
                        keys, queries = x.ap, x.ap
                    else:
                        keys, queries, e = kk, qh, m_k
                    for i0, i1 in bank_tiles:
                        bank = k.banks.take()
                        k.pe.wait([e, m_k] + ready + bank.free)
                        for i in range(i0, i1):
                            last = nc.tensor.matmul(bank.ap[:, (i - i0) * P:(i - i0 + 1) * P], keys[:, i * P:(i + 1) * P],
                                                    queries[:, i * P:(i + 1) * P], start=True, stop=True)
                        done = k.pe.mark(last)
                        n = i1 - i0
                        mask = gla[:, d, lv, :].unsqueeze(1).broadcast_to([P, n, P])
                        c = k.v.go([done, m_sc, m_gla, k.v.now()], nc.vector.copy_predicated,
                                   sc[:, i0 * P:i1 * P].rearrange("p (n t) -> p n t", n=n), mask,
                                   bank.ap[:, 0:n * P].rearrange("p (n t) -> p n t", n=n))
                        k.banks.give(bank, [c])
                    x.free = [done, e]
                    return c

                for lv in range(LEVELS + 1):
                    m_scores = level(lv)
                    yield

                last_of = bc[:, P - 1::P] if d == 0 else bc[:, 0::P]
                m_dec = k.a.go([m_b] + unit, nc.scalar.activation, dec[:], last_of, ACT.Exp)
                kd, qd, st = ex.take(), ex.take(), ex.take()
                b3 = bc[:].rearrange("p (n t) -> p n t", t=P)
                t = k.g.go([m_b] + kd.free, nc.gpsimd.tensor_tensor, kd.ap[:].rearrange("p (n t) -> p n t", t=P),
                           last_of.unsqueeze(2).broadcast_to([P, ST + CT, P]), b3, ALU.subtract)
                t = k.a.go([t], nc.scalar.activation, kd.ap[:], kd.ap[:], ACT.Exp)
                m_kd = k.v.go([t], nc.vector.tensor_tensor, kd.ap[:], kd.ap[:], kk[:], ALU.mult)
                t = k.a.go([m_b] + qd.free, nc.scalar.activation, qd.ap[:, 0:T], bc[:, 0:T], ACT.Exp)
                m_qd = k.v.go([t], nc.vector.tensor_tensor, qd.ap[:, 0:T], qd.ap[:, 0:T], qh[:, 0:T], ALU.mult)
                order = [4, 5, 0, 1, 2, 3] if d == 0 else [5, 4, 3, 2, 1, 0]
                m_t = []
                for group in (range(0, 3), range(3, 6)):
                    bank = k.banks.take()
                    k.pe.wait([m_kd] + bank.free)
                    for n, i in enumerate(group):
                        last = nc.tensor.transpose(bank.ap[:, n * P:(n + 1) * P], kd.ap[:, i * P:(i + 1) * P], k.ident[:])
                    done = k.pe.mark(last)
                    m_t.append(copy_out(k, [done] + unit, kdt[:, group[0]:group[-1] + 1, :].rearrange("p n k -> p (n k)"),
                                        bank.ap[:, 0:3 * P]))
                    k.banks.give(bank, m_t[-1:])
                kd.free = [done, m_kd]
                sums = [k.banks.take(), k.banks.take()]
                for bank in sums:
                    k.pe.wait(bank.free)
                k.pe.wait(m_t + ready)
                for n, i in enumerate(order[:-1]):
                    last = nc.tensor.matmul(sums[n // 4].ap[:, (n % 4) * P:(n % 4 + 1) * P], kdt[:, i, :],
                                            v[:, i, hh * P:(hh + 1) * P], start=True, stop=True)
                done = k.pe.mark(last)
                states = st.ap[:].rearrange("p (n v) -> p n v", v=P)
                for n, i in enumerate(order[:-1]):
                    part = sums[n // 4].ap[:, (n % 4) * P:(n % 4 + 1) * P]
                    if n == 0:
                        m_st = k.v.go([done] + st.free, nc.vector.tensor_copy, states[:, 1, :], part)
                    else:
                        m_st = k.v.go([m_st, m_dec], nc.vector.scalar_tensor_tensor, states[:, n + 1, :], states[:, n, :],
                                      dec[:, i:i + 1], part, ALU.mult, ALU.add)
                for bank in sums:
                    k.banks.give(bank, [m_st])
                hc = 2 * pair + hh
                for i0, i1 in bank_tiles:
                    bank = k.banks.take()
                    k.pe.wait([m_st, m_qd, m_scores] + bank.free)
                    for i in range(i0, i1):
                        out = bank.ap[:, (i - i0) * P:(i - i0 + 1) * P]
                        n = order.index(i)
                        if n:
                            nc.tensor.matmul(out, states[:, n, :], qd.ap[:, i * P:(i + 1) * P], start=True, stop=False)
                        last = nc.tensor.matmul(out, v[:, i, hh * P:(hh + 1) * P], sc[:, i * P:(i + 1) * P],
                                                start=n == 0, stop=True)
                    done = k.pe.mark(last)
                    a, b = i0 * P, i1 * P
                    if d == 0:
                        m_o = k.v.go([done] + start, nc.vector.tensor_copy, y[:, hc, a:b], bank.ap[:, 0:b - a])
                    else:
                        m_o = k.v.go([done], nc.vector.tensor_tensor, y[:, hc, a:b], y[:, hc, a:b], bank.ap[:, 0:b - a], ALU.add)
                    k.banks.give(bank, [m_o])
                qd.free = st.free = [done]
                yield
            rstd = ex.take()
            k.a.wait(rstd.free)
            for a, b in spans[0:sides]:
                root = inverse_rms(k, [m_o], [y[:, hc, :]], [(a, b)], ex_others(ex, rstd), rstd.ap, HGRN_WIDTH)
                t = k.v.go(root, nc.vector.scalar_tensor_tensor, y[:, hc, a:b], y[:, hc, a:b], k.vec("onorm", l),
                           rstd.ap[:, a:b], ALU.mult, ALU.mult)
                t = k.v.go([t], nc.vector.tensor_tensor, y[:, hc, a:b], y[:, hc, a:b], g[:, hh, a:b], ALU.mult)
            rstd.free = [t]
            yield


HGRN_WIDTH = 128


def ex_others(ring, slot):
    r = Ring([])
    r.slots = [s for s in ring.slots if s is not slot]
    return r


def second_layer(k, l, x, x_ready):
    nc = k.nc
    tag = f"b{l}_"
    sides = 2 if l < DEPTH - 1 else 1
    start = now(k)
    h = place(k, tag + "h", AT_H, [2, DC, T2], F32R)
    y = place(k, tag + "y", AT_WORK, [DC, T2])
    rstd = place(k, tag + "rstd", AT_WORK + 74, [T2])
    norm_buffers = [place(k, f"{tag}n{i}", AT_WORK + 24 + 3 * i, [T2]) for i in range(3)]

    def norm_temps():
        r = Ring(norm_buffers)
        for s in r.slots:
            s.free = now(k)
        return r

    h_ready = adaln(k, l, 0, x, x_ready + start, h[:, 0], h[:, 1], 2, rstd, norm_temps())
    start = now(k)
    yield
    yield from fourier(k, l, h, h_ready, y, start, sides)
    yield from diff_attention(k, l, h, h_ready, y, sides)
    yield from recurrent(k, l, h, h_ready, y, sides)
    mixed = now(k)
    ys = place(k, tag + "ys", AT_H, [2, DC, T2], F32R)
    end = (sides + 1) * 256 if sides == 2 else S
    for c in range(DC):
        y_ready = split_into(k, mixed, ys[:, 0, c, 0:end], ys[:, 1, c, 0:end], y[:, c, 0:end])
    spans = [LAT, CTXS][0:sides]
    out = place(k, tag + "out", AT_WORK + 33, [DC, T2])
    marks = {}

    def keep(chunk, banks, done):
        got = [copy_out(k, [done] + mixed, out[:, chunk, a:b], src) for src, a, b in banks]
        marks[chunk] = got
        return got

    yield from project(k, "w_out", 4, ys[:, 0], ys[:, 1], y_ready, spans, keep)
    x_ready = add_normed(k, l, 0, x, out, [k.a.now(), k.v.now()], sides, rstd, norm_temps())

    start = now(k)
    h_ready = adaln(k, l, 1, x, x_ready + start, h[:, 0], h[:, 1], sides, rstd, norm_temps())
    hidden = place(k, tag + "hidden", AT_WORK + 33, [2, 6, T2], F32R)
    acts_ring = Ring(norm_buffers)
    for s in acts_ring.slots:
        s.free = now(k)
    acts, hidden_ready, hidden_free = {}, [], now(k)
    yield

    def ff_g(chunk, banks, done):
        t = acts_ring.take()
        freed = []
        for src, a, b in banks:
            m = k.a.go([done] + t.free, nc.scalar.activation, t.ap[:, a:b], src, ACT.Sigmoid)
            freed.append(k.v.go([m], nc.vector.tensor_tensor, t.ap[:, a:b], t.ap[:, a:b], src, ALU.mult))
        acts[chunk] = (t, freed)
        return freed

    def ff_u(c0):
        def evacuate(chunk, banks, done):
            t, ms = acts.pop(chunk)
            for src, a, b in banks:
                last = k.v.go([done] + ms, nc.vector.tensor_tensor, t.ap[:, a:b], t.ap[:, a:b], src, ALU.mult)
            end = banks[-1][2]
            t.free = split_into(k, [last] + hidden_free, hidden[:, 0, chunk - c0, 0:end], hidden[:, 1, chunk - c0, 0:end],
                                t.ap[:, 0:end])
            hidden_ready[:] = t.free
            return [last]
        return evacuate

    def down(first):
        def evacuate(chunk, banks, done):
            if first:
                return [copy_out(k, [done] + hidden_free, y[:, chunk, a:b], src) for src, a, b in banks]
            return [k.v.go([done, k.a.now()], nc.vector.tensor_tensor, y[:, chunk, a:b], y[:, chunk, a:b], src, ALU.add)
                    for src, a, b in banks]
        return evacuate

    for c0, n in FF_PARTS2:
        for c in range(0, n, 2):
            yield from project(k, "ff_g", 1, h[:, 0], h[:, 1], h_ready, spans, ff_g, c0 + c)
            yield from project(k, "ff_u", 1, h[:, 0], h[:, 1], h_ready, spans, ff_u(c0), c0 + c)
        yield from project(k, "ff_out", 4, hidden[:, 0], hidden[:, 1], hidden_ready, spans, down(c0 == 0))
        hidden_free = [k.pe.now()]
    k.x_ready = add_normed(k, l, 1, x, y, [k.a.now(), k.v.now()], sides, rstd, norm_temps())


def program(nc, ins, out):
    k = set_up(nc, ins)
    stage = place(k, "vector_rows", AT_WORK, [4 * P])
    load_vectors(k, stage)
    second_set_up(k)
    slabs = first_slabs(ins) + modulation_slabs(ins) + second_slabs(ins)
    k.w = Weights(k, slabs)
    x = place(k, "x", AT_X, [DC, T2])
    rows = place(k, "x_rows", AT_WORK + 16, [ST, D])
    rows_ctx = place(k, "ctx_rows", AT_WORK + 32, [CT, D])
    x_ready = transpose_in(k, ins["x"][0], ST, x[:, :, 0:S], rows, [])
    ctx_ready = transpose_in(k, ins["ctx_2"][0], CT, x[:, :, S:T2], rows_ctx, [])
    x1 = x[:, :, 0:S]
    x_ready = x_ready + ctx_ready
    for l in range(DEPTH):
        x_ready = first_layer(k, l, x1, x_ready)
    rstd = place(k, "f_rstd", AT_WORK + 74, [S])
    temps = Ring([place(k, f"f_t{i}", AT_WORK + 24 + 3 * i, [S]) for i in range(3)])
    for s in temps.slots:
        s.free = now(k)
    x_ready = norm_plain(k, x1, x_ready + now(k), lambda c: k.vec("norm_f", c), None, None, SPAN1, rstd, temps, out=x1)
    for _ in modulate(k):
        pass
    for l in range(DEPTH):
        for _ in second_layer(k, l, x, x_ready):
            pass
        x_ready = k.x_ready
    transpose_out(k, x, now(k), out[0])


INPUTS = ("x", "norm1", "w_in", "b_gate", "w_br", "w_o", "norm2", "w_up", "conv_w", "conv_b", "w_down", "norm_f",
          "c_2", "ctx_2", "c_ctx_2", "w_mod_2", "b_mod_2", "norm_g_2", "w_in_2", "w_out_2", "hg_lb_logits_2",
          "hg_onorm_2", "da_lambda_2", "da_subln_2", "w_ffn_in_2", "w_ffn_out_2")


def kernel(**inputs):
    import concourse.bacc as bacc
    from concourse.bass_utils import run_bass_kernel_spmd

    nc = bacc.Bacc("TRN2", target_bir_lowering=False, num_devices=1)
    arrays = {name: np.ascontiguousarray(inputs[name]) for name in INPUTS}
    arrays.update(constants())
    ins = {name: nc.dram_tensor(name, a.shape, mybir.dt.from_np(a.dtype), kind="ExternalInput").ap()
           for name, a in arrays.items()}
    out = nc.dram_tensor("y_out", (1, S, D), F32, kind="ExternalOutput").ap()
    program(nc, ins, out[0:1])
    return run_bass_kernel_spmd(nc, [arrays], core_ids=[0]).results[0]["y_out"]
```

```python
import math

import numpy as np

import concourse.bass as bass
from concourse import mybir

F32 = mybir.dt.float32
F32R = mybir.dt.float32r
U8 = mybir.dt.uint8
ACT = mybir.ActivationFunctionType
ALU = mybir.AluOpType
AX = mybir.AxisListType

P = 128
D = 1024
DC = D // P
S = 512
ST = S // P
CTX = 256
CT = CTX // P
T2 = S + CTX
FF = 2816
FC = FF // P
DEPTH = 2
EPS = 1e-6

HD = 64
GROUPS = ((128, 1), (512, 4), (2048, 16))
ORDER = (1, 4, 4)
GH = 4
W_A = GH * len(GROUPS) * HD
W_B = 256
GATE0 = 3 * W_A + 3 * W_B
SLOPES = [float(np.float32(2.0 ** (-8.0 * n / 12))) for n in range(1, 13)]
FAR = 1e32

HGH = 4
LEVELS = 7
DAH = 4
GRID_W = 64

SLAB_K, SLAB_F = 8, 256



def distances(kind):
    window, dil = GROUPS[kind]
    q = np.arange(P)[:, None]
    if kind == 0:
        k = np.arange(2 * P)[None, :]
        delta = q + P - k
        ok = (delta >= 0) & (delta <= window)
    else:
        k = np.arange(P)[None, :]
        delta = (q - k) * ORDER[kind]
        ok = (delta >= 0) & (delta % dil == 0) & (delta <= window)
    return np.where(ok, -delta, -FAR).astype(np.float32)


def gla_masks():
    s, t = np.arange(P)[:, None], np.arange(P)[None, :]
    out = np.zeros((2, LEVELS + 1, P, P), np.float32)
    for lv in range(LEVELS):
        m = 1 << lv
        same = s // (2 * m) == t // (2 * m)
        out[0, lv] = same & (s // m % 2 == 0) & (t // m % 2 == 1)
        out[1, lv] = same & (s // m % 2 == 1) & (t // m % 2 == 0)
    out[:, LEVELS] = s == t
    return out


def constants():
    j = np.arange(P)
    c = {}
    c["c_ident"] = np.eye(P, dtype=np.float32)
    c["c_ones"] = np.ones((P, P), np.float32)
    c["c_pair"] = (j[:, None] // HD == j[None, :] // HD).astype(np.float32)
    c["c_dist0"], c["c_dist1"], c["c_dist2"] = distances(0), distances(1), distances(2)
    before = j[None, :] < j[:, None]
    c["c_causal"] = before.astype(np.float32)
    c["c_causal_neg"] = np.where(before, 0.0, -1e30).astype(np.float32)
    c["c_gla"] = np.ascontiguousarray(gla_masks().transpose(2, 0, 1, 3))
    f32 = np.float32
    inv = f32(1.0) / (f32(10000.0) ** (np.arange(0, 16, 2, dtype=f32) / f32(16)))
    t = np.arange(S)
    pos = np.stack([t // GRID_W, t % GRID_W]).astype(f32)
    feat = j % 32
    ang = pos[feat // 16, :] * inv[feat % 8][:, None].astype(f32)
    c["c_cos"], c["c_sin"] = np.cos(ang).astype(f32), np.sin(ang).astype(f32)
    rot = np.zeros((P, P), f32)
    for f in range(P):
        if f // 8 % 2 == 0:
            rot[f + 8, f] = -1.0
        else:
            rot[f - 8, f] = 1.0
    c["c_rot"] = rot
    a = 2 * np.pi * np.outer(np.arange(64), np.arange(64)) / 64
    d64 = np.zeros((P, 2, P))
    for g in range(2):
        d64[64 * g:64 * g + 64, 0, 64 * g:64 * g + 64] = np.cos(a)
        d64[64 * g:64 * g + 64, 1, 64 * g:64 * g + 64] = -np.sin(a)
    c["c_dft64"] = d64.astype(f32)
    for name, n in (("c_dftl", S), ("c_dftc", CTX)):
        a = 2 * np.pi * (np.outer(np.arange(n), np.arange(n)) % n) / n
        w = np.stack([np.cos(a), np.sin(a)]) / math.sqrt(n * 64)
        c[name] = np.ascontiguousarray(w.reshape(2, n // P, P, n).transpose(2, 0, 1, 3)).astype(f32)
    return c



class Stream:

    def __init__(self, nc, engine, name):
        self.engine, self.sem = engine, nc.alloc_semaphore(f"{name}_done")
        self.count, self.seen = 0, {}


    def wait(self, marks):
        for sem, value in marks:
            if self.seen.get(sem.name, 0) < value:
                self.engine.wait_ge(sem, value)
                self.seen[sem.name] = value

    def mark(self, instruction):
        instruction.then_inc(self.sem, 1)
        self.count += 1
        return (self.sem, self.count)

    def now(self):
        return (self.sem, self.count)

    def go(self, after, op, *args, **kw):
        self.wait(after)
        return self.mark(op(*args, **kw))


class ScalarStream(Stream):

    BOTH = (ACT.Exp, ACT.Ln)
    ANY = (ACT.Copy, ACT.Identity, ACT.Square, ACT.Abs)
    table = None

    def go(self, after, op, out, in_, func, **kw):
        if func in self.BOTH:
            if self.table != "both":
                self.engine.preload_act_table_set("natural_log_exp_and_others")
            self.table = "both"
        elif func not in self.ANY:
            self.table = func
        return super().go(after, op, out, in_, func, **kw)


class Slot:

    def __init__(self, ap):
        self.ap, self.free = ap, []


class Ring:
    def __init__(self, aps):
        self.slots, self.at = [Slot(a) for a in aps], 0

    def take(self):
        s = self.slots[self.at % len(self.slots)]
        self.at += 1
        return s


class Banks:

    def __init__(self, banks):
        self.idle = [Slot(b) for b in banks]

    def take(self):
        return self.idle.pop(0)

    def give(self, slot, marks):
        slot.free = list(marks)
        self.idle.append(slot)


class DmaQueue:

    def __init__(self, nc, stream, name, n):
        self.stream, self.sems, self.at = stream, [nc.alloc_semaphore(f"{name}{i}") for i in range(n)], 0
        self.used = [0] * n

    def start(self, after, dst, src):
        i = self.at % len(self.sems)
        self.at += 1
        if self.used[i]:
            self.stream.wait([(self.sems[i], self.used[i])])
        self.stream.wait(after)
        self.stream.engine.dma_start(dst, src).then_inc(self.sems[i], 16)
        self.used[i] += 16
        return (self.sems[i], self.used[i])


def weave(main, filler, steps):
    owed = 0.0
    for _ in main:
        owed += steps
        while owed >= 1:
            owed -= 1
            next(filler, None)
        yield
    yield from filler


def pipeline(units, stages):
    for step in range(len(units) + len(stages) - 1):
        for k in reversed(range(len(stages))):
            if 0 <= step - k < len(units):
                stages[k](units[step - k])
        yield



class Core:
    pass






SBUF_END = 229344
ARENA_KB = 149
ARENA = SBUF_END - int(ARENA_KB * 1024)
AT_X = 0
AT_H = 24
AT_WORK = 72


def place(k, name, kb, shape, dtype=F32):
    size = 4 * int(np.prod(shape))
    assert kb * 1024 + size <= ARENA_KB * 1024, name
    return k.nc.alloc_sbuf_tensor_at(name, [P] + list(shape), dtype, offset=int(ARENA + kb * 1024))


def set_up(nc, ins):
    k = Core()
    k.nc, k.ins = nc, ins
    k.pe, k.v = Stream(nc, nc.tensor, "pe"), Stream(nc, nc.vector, "dve")
    k.a, k.g = ScalarStream(nc, nc.scalar, "act"), Stream(nc, nc.gpsimd, "pool")
    k.sp = Stream(nc, nc.sync, "sp")
    k.weights = DmaQueue(nc, k.sp, "weights_in", 4)
    k.loads = DmaQueue(nc, k.a, "loads", 8)
    k.rows = DmaQueue(nc, k.sp, "rows_in", 4)
    k.stores = DmaQueue(nc, k.sp, "stores", 4)
    k.turn = 0

    k.banks = Banks([nc.alloc_psum_tensor(f"bank{i}", [P, 512], F32) for i in range(8)])
    SLAB = SLAB_K * SLAB_F
    k.raw = Ring([nc.alloc_sbuf_tensor(f"w_raw{i}", [P, SLAB], F32) for i in range(2)])
    k.whi = Ring([nc.alloc_sbuf_tensor(f"w_hi{i}", [P, SLAB], F32R) for i in range(2)])
    k.wlo = Ring([nc.alloc_sbuf_tensor(f"w_lo{i}", [P, SLAB], F32R) for i in range(2)])

    return k


def load_constants(k):
    nc, ins = k.nc, k.ins

    def const(name, shape, dtype=F32):
        t = nc.alloc_sbuf_tensor(name[2:] + "_c", [P] + shape, dtype)
        m = k.loads.start([], t[:], ins[name])
        return t, m

    k.ident, k.m_ident = const("c_ident", [P])
    k.ones, k.m_ones = const("c_ones", [P])
    k.pair, k.m_pair = const("c_pair", [P])
    k.dist, k.m_dist = zip(const("c_dist0", [2 * P]), const("c_dist1", [P]), const("c_dist2", [P]))
    k.causal, k.m_causal = const("c_causal", [P])
    k.causal_neg, k.m_causal_neg = const("c_causal_neg", [P])
    k.zeros = nc.alloc_sbuf_tensor("zeros", [P, 1], F32)
    k.m_zeros = k.v.go([], nc.vector.memset, k.zeros[:], 0.0)
    k.eps = nc.alloc_sbuf_tensor("eps", [P, 1], F32)
    k.m_eps = k.v.go([], nc.vector.memset, k.eps[:], EPS)



def now(k):
    return [k.pe.now(), k.v.now(), k.a.now(), k.g.now()]


def copy_out(k, after, out, in_, scale=None):
    k.turn += 1
    if k.turn % 2:
        return k.a.go(after, k.nc.scalar.activation, out, in_, ACT.Copy, scale=1.0 if scale is None else scale)
    if scale is None:
        return k.v.go(after, k.nc.vector.tensor_copy, out, in_)
    return k.v.go(after, k.nc.vector.tensor_scalar, out, in_, scale, None, ALU.mult)


def load_vectors(k, stage):
    nc, ins = k.nc, k.ins

    def rows(name, pattern, **kw):
        return ins[name].rearrange(pattern, p=P, **kw)

    lists = [
        ("norm1", rows("norm1", "l (c p) -> (l c) p")), ("b_gate", rows("b_gate", "l (c p) -> (l c) p")),
        ("norm2", rows("norm2", "l (c p) -> (l c) p")), ("conv_w", rows("conv_w", "l w (c p) -> (l w c) p")),
        ("conv_b", rows("conv_b", "l (c p) -> (l c) p")), ("norm_f", rows("norm_f", "(c p) -> c p")),
        ("b_mod", rows("b_mod_2", "l (c p) -> (l c) p")), ("norm_g", rows("norm_g_2", "l n (c p) -> (l n c) p")),
        ("lb", rows("hg_lb_logits_2", "d l (c p) -> (d l c) p")), ("onorm", ins["hg_onorm_2"]),
        ("c", rows("c_2", "o (c p) -> (o c) p")), ("c_ctx", rows("c_ctx_2", "(c p) -> c p")),
        ("subln", None),
    ]
    at, base, loaded = 0, {}, []
    for name, src in lists:
        base[name] = at
        n = DEPTH if src is None else src.shape[0]
        done = 0
        while done < n:
            row, tile = (at + done) % P, (at + done) // P
            m = min(n - done, P - row)
            dst = stage[row:row + m, tile * P:(tile + 1) * P]
            if src is None:
                for h in range(2):
                    loaded.append(k.loads.start([], dst[:, 64 * h:64 * h + 64], ins["da_subln_2"][done:done + m, :]))
            else:
                loaded.append(k.loads.start([], dst, src[done:done + m, :]))
            done += m
        at += n
    k.vecs = nc.alloc_sbuf_tensor("vectors", [P, at], F32)
    bank, k.m_vecs = k.banks.take(), []
    for tile in range(-(-at // P)):
        n = min(P, at - tile * P)
        k.pe.wait(loaded + [k.m_ident])
        done = k.pe.mark(nc.tensor.transpose(bank.ap[:, tile * P:tile * P + n], stage[0:n, tile * P:(tile + 1) * P],
                                             k.ident[0:n, 0:n]))
    k.m_vecs = [k.v.go([done], nc.vector.tensor_copy, k.vecs[:], bank.ap[:, 0:at])]
    k.banks.give(bank, k.m_vecs)
    k.vec = lambda name, i, n=1: k.vecs[:, base[name] + i:base[name] + i + n]



LO_ON_DVE = ("mod",)


class Weights:

    def __init__(self, k, slabs, order):
        self.k, self.ready, self.used = k, [], []
        self.order = list(order) if order else None
        self.by_name = {}
        for name, src in slabs:
            self.by_name.setdefault(name, []).append(src)

    def prepare(self, name):
        k, nc = self.k, self.k.nc
        src = self.by_name[name].pop(0)
        nk, nf = src.shape[1], src.shape[2]
        raw, hi, lo = k.raw.take(), k.whi.take(), k.wlo.take()
        view = lambda t: t[:, 0:nk * nf].rearrange("p (k f) -> p k f", k=nk)
        flat = slice(0, nk * nf)
        loaded = k.weights.start(raw.free, view(raw.ap), src)
        m_hi = k.a.go([loaded] + hi.free, nc.scalar.activation, hi.ap[:, flat], raw.ap[:, flat], ACT.Copy)
        lo_by, subtract = (k.v, nc.vector.tensor_tensor) if name in LO_ON_DVE else (k.g, nc.gpsimd.tensor_tensor)
        m_lo = lo_by.go([loaded, m_hi] + lo.free, subtract, lo.ap[:, flat], raw.ap[:, flat],
                      hi.ap[:, flat].bitcast(F32), ALU.subtract)
        raw.free = [m_lo]
        self.ready.append((name, view(hi.ap), view(lo.ap), [m_hi, m_lo], (hi, lo)))

    def take(self, name):
        if self.order is None:
            self.prepare(name)
        while self.order and len(self.ready) < 2:
            self.prepare(self.order.pop(0))
        got = self.ready.pop(0)
        assert got[0] == name, (got[0], name)
        self.used.append(name)
        return got[1:]


def products(pe, nc, out, w_hi, w_lo, x_hi, x_lo, first, last):
    nc.tensor.matmul(out, w_hi, x_hi, start=first, stop=False)
    nc.tensor.matmul(out, w_hi, x_lo, start=False, stop=False)
    return nc.tensor.matmul(out, w_lo, x_hi, start=False, stop=last)


def project(k, name, n_slabs, x_hi, x_lo, x_ready, spans, evacuate, chunk0=0, parts=None):
    nc = k.nc
    chunk = chunk0
    for s in range(n_slabs):
        w_hi, w_lo, w_ready, slots = k.w.take(name)
        nk, nf = w_hi.shape[1], w_hi.shape[2]
        for j in range(nf // P):
            cols = slice(j * P, (j + 1) * P)
            for part in parts or [(0, nk)]:
                banks = [k.banks.take() for _ in spans]
                k.pe.wait(w_ready)
                for bank in banks:
                    k.pe.wait(bank.free)
                for kk in range(*part):
                    k.pe.wait(x_ready[kk])
                    for (t0, t1), bank in zip(spans, banks):
                        last = products(k.pe, nc, bank.ap[:, 0:t1 - t0], w_hi[:, kk, cols], w_lo[:, kk, cols],
                                        x_hi[:, kk, t0:t1], x_lo[:, kk, t0:t1],
                                        kk == part[0], kk == part[1] - 1)
                done = k.pe.mark(last)
                args = (chunk, part[0]) if parts else (chunk,)
                freed = evacuate(*args, [(b.ap[:, 0:t1 - t0], t0, t1) for (t0, t1), b in zip(spans, banks)], done)
                for bank in banks:
                    k.banks.give(bank, freed)
            chunk += 1
            if j == nf // P - 1:
                for slot in slots:
                    slot.free = [done]
            yield


def project_tokens(k, name, x_hi, x_lo, x_ready, tiles, evacuate):
    nc = k.nc
    w_hi, w_lo, w_ready, slots = k.w.take(name)
    nk, nf = w_hi.shape[1], w_hi.shape[2]
    for i, tokens in enumerate(tiles):
        bank = k.banks.take()
        k.pe.wait(w_ready + bank.free)
        for kk in range(nk):
            k.pe.wait(x_ready[kk])
            last = products(k.pe, nc, bank.ap[:, 0:nf], x_hi[:, kk, tokens], x_lo[:, kk, tokens],
                            w_hi[:, kk, :], w_lo[:, kk, :], kk == 0, kk == nk - 1)
        done = k.pe.mark(last)
        k.banks.give(bank, evacuate(i, bank.ap[:, 0:nf], done))
        if i == len(tiles) - 1:
            for slot in slots:
                slot.free = [done]
        if i % 2:
            yield


def split_into(k, after, hi, lo, value):
    m_hi = k.a.go(after, k.nc.scalar.activation, hi, value, ACT.Copy)
    m_lo = k.v.go([m_hi] + list(after), k.nc.vector.tensor_tensor, lo, value, hi.bitcast(F32), ALU.subtract)
    return [m_hi, m_lo]


def without(ring, slot):
    r = Ring([])
    r.slots = [s for s in ring.slots if s is not slot]
    return r


def inverse_rms(k, ready, chunks, spans, temps, out, out_free, width, ones=None):
    nc = k.nc
    ones = k.ones if ones is None else ones
    t0, t1 = spans[0][0], spans[-1][1]
    n = t1 - t0
    total = temps.take()
    others = without(temps, total)
    m = k.a.go(ready[0] + total.free, nc.scalar.activation, total.ap[:, 0:n], chunks[0][:, t0:t1], ACT.Square)
    for c, x in list(enumerate(chunks))[1:]:
        t = others.take()
        sq = k.a.go(ready[c] + t.free, nc.scalar.activation, t.ap[:, 0:n], x[:, t0:t1], ACT.Square)
        m = k.v.go([sq, m], nc.vector.tensor_tensor, total.ap[:, 0:n], total.ap[:, 0:n], t.ap[:, 0:n], ALU.add)
        t.free = [m]
    marks = []
    for a, b in spans:
        bank = k.banks.take()
        k.pe.wait([m, k.m_ones, k.m_pair] + bank.free)
        done = k.pe.mark(nc.tensor.matmul(bank.ap[:, 0:b - a], ones[:], total.ap[:, a - t0:b - t0], start=True, stop=True))
        total.free = [done]
        ln = k.a.go([done, k.m_eps] + out_free, nc.scalar.activation, out[:, a:b], bank.ap[:, 0:b - a], ACT.Ln,
                    scale=1.0 / width, bias=k.eps[:])
        k.banks.give(bank, [ln])
        marks.append(k.a.go([ln], nc.scalar.activation, out[:, a:b], out[:, a:b], ACT.Exp, scale=-0.5))
    return marks



def load_rows(k, src, tiles, stage, after):
    return [k.rows.start(after, stage[:, i, :], src[i * P:(i + 1) * P, :]) for i in range(tiles)]


def transpose_in(k, loaded, tiles, x, stage):
    nc = k.nc
    marks = []
    for c in range(DC):
        bank = k.banks.take()
        k.pe.wait(loaded + [k.m_ident] + bank.free)
        for i in range(tiles):
            last = nc.tensor.transpose(bank.ap[:, i * P:(i + 1) * P], stage[:, i, c * P:(c + 1) * P], k.ident[:])
        marks.append([copy_out(k, [k.pe.mark(last)], x[:, c, :], bank.ap[:, 0:tiles * P])])
        k.banks.give(bank, marks[-1])
    return marks


def norm_plain(k, x, x_ready, before, gain, hi, lo, spans, rstd, temps, out=None):
    nc = k.nc
    t0, t1 = spans[0][0], spans[-1][1]
    root = inverse_rms(k, x_ready, [x[:, c, :] for c in range(DC)], spans, temps, rstd, before, D)
    marks = []
    for c in range(DC):
        if out is not None:
            marks.append([k.v.go(root + k.m_vecs, nc.vector.scalar_tensor_tensor, out[:, c, t0:t1], x[:, c, t0:t1],
                                 gain(c), rstd[:, t0:t1], ALU.mult, ALU.mult)])
            continue
        t = temps.take()
        n = k.v.go(root + k.m_vecs + t.free, nc.vector.scalar_tensor_tensor, t.ap[:, t0:t1], x[:, c, t0:t1],
                   gain(c), rstd[:, t0:t1], ALU.mult, ALU.mult)
        marks.append(split_into(k, [n] + before, hi[:, c, t0:t1], lo[:, c, t0:t1], t.ap[:, t0:t1]))
        t.free = marks[-1]
    return marks


def by_residue(ap, dil):
    return ap.rearrange("p (l r) -> p r l", r=dil)


def mixer_a(k, l, m, qk, v, qkv_ready, o_hi, o_lo):
    nc = k.nc
    stats = m.stats
    units = [(g, i, par) for g in range(3) for i in range(ST) for par in range(2)]
    state, held, evac = {}, {}, {}

    def keys(g, i):
        return 2 * P if g == 0 and i > 0 else P

    def scores(u):
        g, i, par = u
        n = keys(g, i)
        bank = k.banks.take()
        k.pe.wait(qkv_ready + bank.free)
        for j in range(2):
            rows = slice(HD * par, HD * par + HD)
            last = nc.tensor.matmul(bank.ap[:, j * n:(j + 1) * n], qk[rows, 2 * g + j, i * P:(i + 1) * P],
                                    qk[rows, 6 + 2 * g + j, (i + 1) * P - n:(i + 1) * P], start=True, stop=True)
        done = k.pe.mark(last)
        sb = m.probs.take()
        dist = k.dist[g]
        off = 2 * P - n if g == 0 else 0
        for j in range(2):
            slope = SLOPES[GH * g + 2 * j + par]
            last = k.v.go([done, k.m_dist[g]] + sb.free, nc.vector.scalar_tensor_tensor, sb.ap[:, j * n:(j + 1) * n],
                          dist[:, off:off + n], slope, bank.ap[:, j * n:(j + 1) * n], ALU.mult, ALU.add)
        k.banks.give(bank, [last])
        both = sb.ap[:, 0:2 * n].rearrange("p (j n) -> p j n", j=2)
        neg = stats[:, 0, g, i, par:par + 3:2]
        negmax = k.v.go([last], nc.vector.tensor_reduce, neg, both, AX.X, ALU.max, negate=True)
        for j in range(2):
            h = par + 2 * j
            e = k.a.go([negmax], nc.scalar.activation, both[:, j, :], both[:, j, :], ACT.Exp,
                       bias=stats[:, 0, g, i, h:h + 1], accum_out=stats[:, 1, g, i, h:h + 1])
        state[u] = (sb, e)

    def turn(u):
        g, i, par = u
        n = keys(g, i)
        sb, e = state[u]
        bank = k.banks.take()
        k.pe.wait([e, k.m_ident] + bank.free)
        for b in range(2 * n // P):
            last = nc.tensor.transpose(bank.ap[:, b * P:(b + 1) * P], sb.ap[:, b * P:(b + 1) * P], k.ident[:])
        done = k.pe.mark(last)
        sb.free = [done]
        pt = m.turned.take()
        copied = copy_out(k, [done] + pt.free, pt.ap[:, 0:2 * n], bank.ap[:, 0:2 * n])
        k.banks.give(bank, [copied])
        state[u] = (pt, copied)

    def values(u):
        g, i, par = u
        n = keys(g, i)
        pt, copied = state.pop(u)
        for j in range(2):
            if (g, j) not in held:
                held[g, j] = k.banks.take()
            bank = held[g, j]
            k.pe.wait([copied] + qkv_ready + bank.free)
            h = par + 2 * j
            for b in range(n // P):
                tile = i - (n // P - 1) + b
                last = nc.tensor.matmul(bank.ap[HD * par:HD * par + HD, i * P:(i + 1) * P],
                                        v[:, tile, g * 256 + h * HD:g * 256 + (h + 1) * HD],
                                        pt.ap[:, j * n + b * P:j * n + (b + 1) * P],
                                        start=b == 0, stop=b == n // P - 1)
        done = k.pe.mark(last)
        pt.free = [done]
        if i == ST - 1 and par == 1:
            dil = ORDER[g]
            for j in range(2):
                bank = held[g, j]
                src = bank.ap[:, :] if dil == 1 else bank.ap[:, :].rearrange("p (r l) -> p l r", r=dil)
                dst = m.oa[:, g, j, :] if dil == 1 else m.oa[:, g, j, :].rearrange("p (l r) -> p l r", r=dil)
                evac[g, j] = copy_out(k, [done] + m.start, dst, src)
                k.banks.give(bank, [evac[g, j]])

    yield from pipeline(units, [scores, turn, values])
    m.evacuated = evac


def mixture(k, m, o_hi, o_lo):
    nc = k.nc
    stats, evac = m.stats, m.evacuated
    def spread(which, g, c):
        bank = k.banks.take()
        k.pe.wait(bank.free + [k.a.now(), k.v.now()])
        for i in range(ST):
            for j in range(2):
                col = stats[:, which, g, i, 2 * c + j:2 * c + j + 1].broadcast_to([P, HD])
                last = nc.tensor.matmul(bank.ap[HD * j:HD * j + HD, i * P:(i + 1) * P], col, k.ident[:],
                                        start=True, stop=True)
        dil = ORDER[g]
        src = bank.ap[:, :] if dil == 1 else bank.ap[:, :].rearrange("p (r l) -> p l r", r=dil)
        return bank, src, [k.pe.mark(last)]

    def natural(t, dil):
        return t if dil == 1 else t.rearrange("p (l r) -> p l r", r=dil)

    mix = Ring(m.mix_buffers)
    for slot in mix.slots:
        slot.free = now(k)
    for c in range(2):
        n = [mix.take() for _ in range(3)]
        marks = []
        for g in range(3):
            bank, src, done = spread(0, g, c)
            marks.append(k.a.go(done + n[g].free, nc.scalar.activation, natural(n[g].ap[:, 0:S], ORDER[g]), src, ACT.Copy))
            k.banks.give(bank, marks[-1:])
        least = mix.take()
        t = k.v.go(marks + least.free, nc.vector.tensor_tensor, least.ap[:, 0:S], n[0].ap[:, 0:S], n[1].ap[:, 0:S], ALU.min)
        t = k.v.go([t], nc.vector.tensor_tensor, least.ap[:, 0:S], least.ap[:, 0:S], n[2].ap[:, 0:S], ALU.min)
        total = mix.take()
        for g in range(3):
            t1 = k.g.go([t], nc.gpsimd.tensor_tensor, n[g].ap[:, 0:S], least.ap[:, 0:S], n[g].ap[:, 0:S], ALU.subtract)
            e = k.a.go([t1], nc.scalar.activation, n[g].ap[:, 0:S], n[g].ap[:, 0:S], ACT.Exp)
            bank, src, done = spread(1, g, c)
            den = mix.take() if g else total
            mul = k.v.go([e] + done + den.free, nc.vector.tensor_tensor, natural(den.ap[:, 0:S], ORDER[g]),
                         natural(n[g].ap[:, 0:S], ORDER[g]), src, ALU.mult)
            k.banks.give(bank, [mul])
            if g:
                mul = k.v.go([mul], nc.vector.tensor_tensor, total.ap[:, 0:S], total.ap[:, 0:S], den.ap[:, 0:S], ALU.add)
                den.free = [mul]
            yield
        r = k.v.go([mul], nc.vector.reciprocal, total.ap[:, 0:S], total.ap[:, 0:S])
        for g in range(3):
            p = k.g.go([e, mul, evac[g, c]], nc.gpsimd.tensor_tensor, n[g].ap[:, 0:S], n[g].ap[:, 0:S], m.oa[:, g, c, :], ALU.mult)
        s1 = k.g.go([p], nc.gpsimd.tensor_tensor, n[0].ap[:, 0:S], n[0].ap[:, 0:S], n[1].ap[:, 0:S], ALU.add)
        s2 = k.g.go([s1], nc.gpsimd.tensor_tensor, n[0].ap[:, 0:S], n[0].ap[:, 0:S], n[2].ap[:, 0:S], ALU.add)
        f = k.v.go([s2, r], nc.vector.tensor_tensor, least.ap[:, 0:S], n[0].ap[:, 0:S], total.ap[:, 0:S], ALU.mult)
        marks = split_into(k, [f] + m.start, o_hi[:, c, :], o_lo[:, c, :], least.ap[:, 0:S])
        for slot in n + [least, total]:
            slot.free = marks + [f]
        m.done[c] = marks
        yield


def mixer_b(k, l, m, qk, v, qkv_ready, o_hi, o_lo):
    nc = k.nc
    units = [(c, i, par) for c in range(2) for i in range(ST) for par in range(2)]
    state, held = {}, {}

    def scores(u):
        c, i, par = u
        n = (i + 1) * P
        bank = k.banks.take()
        rows = slice(HD * par, HD * par + HD)
        k.pe.wait(qkv_ready + bank.free)
        done = k.pe.mark(nc.tensor.matmul(bank.ap[:, 0:n], qk[rows, 12 + c, i * P:n], qk[rows, 14 + c, 0:n],
                                          start=True, stop=True))
        z, sp = m.stick.take(), m.stick.take()
        t = k.v.go([done] + z.free, nc.vector.tensor_copy, z.ap[:, 0:n], bank.ap[:, 0:n])
        k.banks.give(bank, [t])
        t = k.a.go([t] + sp.free, nc.scalar.activation, sp.ap[:, 0:n], z.ap[:, 0:n], ACT.Abs)
        t = k.a.go([t], nc.scalar.activation, sp.ap[:, 0:n], sp.ap[:, 0:n], ACT.Exp, scale=-1.0)
        t = k.a.go([t], nc.scalar.activation, sp.ap[:, 0:n], sp.ap[:, 0:n], ACT.Ln, bias=1.0)
        state[u] = (z, sp, t)

    def sums(u):
        c, i, par = u
        n = (i + 1) * P
        z, sp, t = state[u]
        own = slice(i * P, n)
        t = k.v.go([t], nc.vector.scalar_tensor_tensor, sp.ap[:, 0:n], z.ap[:, 0:n], 0.0, sp.ap[:, 0:n], ALU.max, ALU.add)
        t = k.v.go([t, k.m_causal], nc.vector.tensor_tensor, sp.ap[:, own], sp.ap[:, own], k.causal[:], ALU.mult)
        neg = k.g.go([t, k.m_causal_neg], nc.gpsimd.tensor_tensor, z.ap[:, own], z.ap[:, own], k.causal_neg[:], ALU.add)
        back = sp.ap[:, n - 1::-1] if n == S else sp.ap[:, 0:n][:, ::-1]
        t = k.v.go([t, k.m_zeros], nc.vector.tensor_tensor_scan, back, back, k.zeros[:, 0:1].broadcast_to([P, n]), 0.0,
                   ALU.add, ALU.add)
        t = k.v.go([t, neg], nc.vector.tensor_tensor, z.ap[:, 0:n], z.ap[:, 0:n], sp.ap[:, 0:n], ALU.subtract)
        sp.free = [t]
        t = k.a.go([t], nc.scalar.activation, z.ap[:, 0:n], z.ap[:, 0:n], ACT.Exp)
        state[u] = (z, t)

    def turn(u):
        c, i, par = u
        z, t = state[u]
        bank = k.banks.take()
        k.pe.wait([t, k.m_ident] + bank.free)
        for b in range(i + 1):
            last = nc.tensor.transpose(bank.ap[:, b * P:(b + 1) * P], z.ap[:, b * P:(b + 1) * P], k.ident[:])
        done = k.pe.mark(last)
        z.free = [done]
        pt = m.turned.take()
        copied = copy_out(k, [done] + pt.free, pt.ap[:, 0:(i + 1) * P], bank.ap[:, 0:(i + 1) * P])
        k.banks.give(bank, [copied])
        state[u] = (pt, copied)

    def values(u):
        c, i, par = u
        pt, copied = state.pop(u)
        if c not in held:
            held[c] = k.banks.take()
        bank = held[c]
        k.pe.wait([copied] + qkv_ready + bank.free)
        col = 3 * 256 + (2 * c + par) * HD
        for b in range(i + 1):
            last = nc.tensor.matmul(bank.ap[HD * par:HD * par + HD, i * P:(i + 1) * P], v[:, b, col:col + HD],
                                    pt.ap[:, b * P:(b + 1) * P], start=b == 0, stop=b == i)
        done = k.pe.mark(last)
        pt.free = [done]
        if i == ST - 1 and par == 1:
            marks = split_into(k, [done] + m.start, o_hi[:, 2 + c, :], o_lo[:, 2 + c, :], bank.ap[:, :])
            k.banks.give(bank, marks)
            m.done[2 + c] = marks

    yield from pipeline(units, [scores, sums, turn, values])


SPAN1 = [(0, S)]


def slab_list(out, name, w, r0, nr, c0, n, step=SLAB_F):
    for c in range(c0, c0 + n, step):
        f = min(step, c0 + n - c)
        out.append((name, w[r0:r0 + nr, c:c + f].rearrange("(k p) f -> p k f", p=P)))


def first_slabs(ins):
    out = []
    for l in range(DEPTH):
        w = ins["w_in"][l]
        slab_list(out, "qk_a", w, 0, D, 0, 2 * W_A)
        slab_list(out, "v_a", w, 0, D, 2 * W_A, W_A)
        slab_list(out, "qk_b", w, 0, D, 3 * W_A, 2 * W_B)
        slab_list(out, "v_b", w, 0, D, 3 * W_A + 2 * W_B, W_B)
        slab_list(out, "gate_a", w, 0, D, GATE0, D)
        slab_list(out, "gate_b", w, 0, D, GATE0 + D, D)
        slab_list(out, "branch", ins["w_br"][l], 0, 2 * W_B, 0, D)
        slab_list(out, "w_o", ins["w_o"][l], 0, D, 0, D)
        for c0, n in FF_PARTS1:
            slab_list(out, "up_a", ins["w_up"][l], 0, D, c0 * P, n * P)
            slab_list(out, "up_v", ins["w_up"][l], 0, D, FF + c0 * P, n * P)
            slab_list(out, "down", ins["w_down"][l], c0 * P, n * P, 0, D)
    return out


FF_PARTS1 = [(0, 8), (8, 8), (16, 6)]


def add_to(k, x, marks):
    def evacuate(chunk, banks, done):
        src, t0, t1 = banks[0]
        marks[chunk] = [k.v.go([done], k.nc.vector.tensor_tensor, x[:, chunk, t0:t1], x[:, chunk, t0:t1], src, ALU.add)]
        return marks[chunk]
    return evacuate


def fresh(aps, free):
    r = Ring(aps)
    for s in r.slots:
        s.free = list(free)
    return r


def first_layer(k, l, x, spare, x_ready, before):
    nc = k.nc
    m = Core()
    tag = f"a{l}_"
    h = place(k, tag + "h", AT_H, [2, DC, S], F32R)
    o = place(k, tag + "o", AT_H + 32, [2, 4, S], F32R)
    qk = place(k, tag + "qk", AT_WORK, [16, S])
    v = place(k, tag + "v", AT_WORK + 32, [ST, W_A + W_B])
    m.oa = place(k, tag + "oa", AT_WORK + 48, [3, 2, S])
    temps = [place(k, f"{tag}t{i}", AT_WORK + 60 + 2 * i, [S]) for i in range(8)]
    m.stats = place(k, tag + "stats", AT_WORK + 76, [2, 3, ST, GH])
    rstd = temps[7]

    h_ready = norm_plain(k, x, x_ready, before, lambda c: k.vec("norm1", DC * l + c), h[:, 0], h[:, 1], SPAN1, rstd,
                         fresh(temps[3:6], before))
    start = now(k)

    def keep_qk(chunk, banks, done):
        src = banks[0][0]
        dst = qk[:, chunk, :]
        query = chunk < 6 or chunk in (12, 13)
        dil = ORDER[chunk % 6 // 2] if chunk < 12 else 1
        if dil > 1:
            src, dst = by_residue(src, dil), dst.rearrange("p (r l) -> p r l", r=dil)
        return [copy_out(k, [done] + start, dst, src, HD ** -0.5 if query else None)]

    def keep_v(g):
        def evacuate(i, src, done):
            return [copy_out(k, [done] + start, v[:, i, g * 256:(g + 1) * 256], src)]
        return evacuate

    def project_v(name, g):
        dil = ORDER[g] if g < 3 else 1
        tiles = [slice(i * P, (i + 1) * P) if dil == 1 else slice(i, S, dil) for i in range(ST)]
        return project_tokens(k, name, h[:, 0], h[:, 1], h_ready, tiles, keep_v(g))

    def project_a():
        yield from project(k, "qk_a", 6, h[:, 0], h[:, 1], h_ready, SPAN1, keep_qk)
        for g in range(3):
            yield from project_v("v_a", g)

    for _ in project(k, "qk_b", 2, h[:, 0], h[:, 1], h_ready, SPAN1, keep_qk, 12):
        pass
    for _ in project_v("v_b", 3):
        pass
    m.start, m.done = start, [None] * 4
    m.stick = fresh(temps[0:6], now(k))
    m.turned = fresh(temps[6:8], now(k))
    for _ in weave(mixer_b(k, l, m, qk, v, [k.a.now(), k.v.now()], o[:, 0], o[:, 1]), project_a(), 1.0):
        pass

    gates = [None] * (2 * DC)
    gate_ready = {}

    def gate(base, buffers, after):
        def evacuate(chunk, banks, done):
            gates[base + chunk] = buffers[chunk]
            src = banks[0][0]
            if len(buffers[chunk].shape) == 3:
                src = src.rearrange("p (a b) -> p a b", a=2)
            gate_ready[base + chunk] = k.a.go([done] + k.m_vecs + after, nc.scalar.activation, buffers[chunk], src,
                                              ACT.Sigmoid, bias=k.vec("b_gate", 16 * l + base + chunk))
            return [gate_ready[base + chunk]]
        return evacuate

    def gates_a(after):
        buffers = [qk[:, 12 + c, :] for c in range(4)] + [spare[:, 2 * c:2 * c + 2, :] for c in range(4)]
        yield from project(k, "gate_a", 4, h[:, 0], h[:, 1], h_ready, SPAN1, gate(0, buffers, after))

    def gates_b(after):
        buffers = [qk[:, c, :] for c in range(DC)]
        yield from project(k, "gate_b", 4, h[:, 0], h[:, 1], h_ready, SPAN1, gate(DC, buffers, after))

    def both(*parts):
        for p in parts:
            yield from p

    m.probs = fresh(temps[0:3], now(k))
    m.turned = fresh(temps[3:6], now(k))
    m.mix_buffers = temps[0:8]
    mod_rows = fresh([temps[6][:, 0:SLAB_F], temps[6][:, SLAB_F:2 * SLAB_F]], now(k))
    for _ in weave(mixer_a(k, l, m, qk, v, [k.a.now(), k.v.now()], o[:, 0], o[:, 1]),
                   both(gates_a(now(k)), modulate(k, l, mod_rows)), 1.3):
        pass
    for _ in weave(mixture(k, m, o[:, 0], o[:, 1]), gates_b(now(k)), 1.0):
        pass

    attended = now(k)
    merged = place(k, tag + "merged", AT_WORK + 32, [2, DC, S], F32R)
    branch = fresh([place(k, f"{tag}br{i}", AT_WORK + 64 + 2 * i, [S]) for i in range(4)], attended)
    half, merged_ready = {}, [None] * DC

    def merge(chunk, part, banks, done):
        i = chunk if part == 0 else DC + chunk
        t = branch.take()
        g, src, dst = gates[i], banks[0][0], t.ap[:]
        if len(g.shape) == 3:
            src, dst = src.rearrange("p (a b) -> p a b", a=2), dst.rearrange("p (a b) -> p a b", a=2)
        mark = k.v.go([done, gate_ready[i]] + t.free, nc.vector.tensor_tensor, dst, src, g, ALU.mult)
        if part == 0:
            half[chunk] = t
            return [mark]
        a = half.pop(chunk)
        total = k.v.go([mark], nc.vector.tensor_tensor, a.ap[:], a.ap[:], t.ap[:], ALU.add)
        t.free = [total]
        a.free = merged_ready[chunk] = split_into(k, [total] + attended, merged[:, 0, chunk, :], merged[:, 1, chunk, :],
                                                  a.ap[:])
        return [mark]

    for _ in project(k, "branch", 4, o[:, 0], o[:, 1], m.done, SPAN1, merge, parts=[(0, 2), (2, 4)]):
        pass
    added = [None] * DC
    before = now(k)
    for _ in project(k, "w_o", 4, merged[:, 0], merged[:, 1], merged_ready, SPAN1, add_to(k, x, added)):
        pass

    h_ready = norm_plain(k, x, added, before, lambda c: k.vec("norm2", DC * l + c), h[:, 0], h[:, 1], SPAN1, rstd,
                         fresh(temps[3:6], before))
    mixed = now(k)
    hidden = place(k, tag + "hidden", AT_WORK, [2, 8, S], F32R)
    conv = fresh([place(k, f"{tag}cv{i}", AT_WORK + 32 + 2 * i, [S]) for i in range(6)], mixed)
    acts = {}
    hidden_ready, hidden_free = [None] * 8, mixed

    def tap(i, c):
        return k.vec("conv_w", (3 * l + i) * FC + c)

    def up_a(chunk, banks, done):
        src, c = banks[0][0], conv.take()
        t = k.a.go([done] + k.m_vecs + c.free, nc.scalar.activation, c.ap[:], src, ACT.Identity, scale=tap(2, chunk),
                   bias=k.vec("conv_b", FC * l + chunk))
        t = k.v.go([t], nc.vector.scalar_tensor_tensor, c.ap[:, 1:S], src[:, 0:S - 1], tap(1, chunk), c.ap[:, 1:S],
                   ALU.mult, ALU.add)
        t = k.v.go([t], nc.vector.scalar_tensor_tensor, c.ap[:, 2:S], src[:, 0:S - 2], tap(0, chunk), c.ap[:, 2:S],
                   ALU.mult, ALU.add)
        acts[chunk] = (c, k.a.go([t], nc.scalar.activation, c.ap[:], c.ap[:], ACT.Gelu))
        return [t]

    def up_v(c0):
        def evacuate(chunk, banks, done):
            c, t = acts.pop(chunk)
            t = k.v.go([done, t], nc.vector.tensor_tensor, c.ap[:], c.ap[:], banks[0][0], ALU.mult)
            c.free = split_into(k, [t] + hidden_free, hidden[:, 0, chunk - c0, :], hidden[:, 1, chunk - c0, :], c.ap[:])
            hidden_ready[chunk - c0] = c.free
            return [t]
        return evacuate

    for c0, n in FF_PARTS1:
        for c in range(0, n, 2):
            for _ in project(k, "up_a", 1, h[:, 0], h[:, 1], h_ready, SPAN1, up_a, c0 + c):
                pass
            for _ in project(k, "up_v", 1, h[:, 0], h[:, 1], h_ready, SPAN1, up_v(c0), c0 + c):
                pass
        before = now(k)
        for _ in project(k, "down", 4, hidden[:, 0], hidden[:, 1], hidden_ready, SPAN1, add_to(k, x, added)):
            pass
        hidden_free = [k.pe.now()]
    return added, before



def transpose_out(k, x, ready, out):
    nc = k.nc
    stage = place(k, "out_rows", AT_WORK + 33, [ST, D])
    before = now(k)
    stored = []
    for i in range(ST):
        marks = []
        for half in range(2):
            bank = k.banks.take()
            for c in range(4):
                k.pe.wait(ready[4 * half + c])
            k.pe.wait(bank.free)
            for c in range(4):
                last = nc.tensor.transpose(bank.ap[:, c * P:(c + 1) * P], x[:, 4 * half + c, i * P:(i + 1) * P], k.ident[:])
            marks.append(copy_out(k, [k.pe.mark(last)] + before, stage[:, i, half * 512:(half + 1) * 512], bank.ap[:, :]))
            k.banks.give(bank, marks[-1:])
        stored.append(k.stores.start(marks, out[i * P:(i + 1) * P, :], stage[:, i, :]))
    k.sp.wait(stored)




IN2 = {"q": 0, "v": 512, "g": 1024, "f": 1536, "b": 2048, "dq": 2560, "dk": 2816, "dv": 3072, "ft": 3328}
FF_PARTS2 = [(0, 6), (6, 6), (12, 5), (17, 5)]
LAT, CTXS = (0, S), (S, T2)


def modulation_slabs(ins):
    out = []
    for l in range(DEPTH):
        slab_list(out, "mod", ins["w_mod_2"][l], 0, D, 0, 6 * D)
    return out


def second_slabs(ins):
    out = []
    for l in range(DEPTH):
        w = ins["w_in_2"][l]
        for name in ("ft", "dq", "dk", "dv"):
            slab_list(out, name, w, 0, D, IN2[name], 256)
        for name in ("q", "v", "f", "b", "g"):
            slab_list(out, name, w, 0, D, IN2[name], HGH * P, step=P)
        slab_list(out, "w_out", ins["w_out_2"][l], 0, D, 0, D)
        for c0, n in FF_PARTS2:
            slab_list(out, "ff_g", ins["w_ffn_in_2"][l], 0, D, c0 * P, n * P)
            slab_list(out, "ff_u", ins["w_ffn_in_2"][l], 0, D, FF + c0 * P, n * P)
            slab_list(out, "ff_out", ins["w_ffn_out_2"][l], c0 * P, n * P, 0, D)
    return out


def second_set_up(k):
    nc, ins = k.nc, k.ins
    v, a = nc.vector, nc.scalar

    def small(name, shape, dtype=F32):
        return nc.alloc_sbuf_tensor(name, [P] + shape, dtype)

    k.cond, value = small("cond", [DC, 4], F32R), small("cond_value", [DC, 2])
    sig = small("cond_sigmoid", [DC, 2])
    for j, name in enumerate(("c", "c_ctx")):
        t = k.a.go(k.m_vecs, a.activation, sig[:, :, j], k.vec(name, 0, DC), ACT.Sigmoid)
        t = k.v.go([t], v.tensor_tensor, value[:, :, j], sig[:, :, j], k.vec(name, 0, DC), ALU.mult)
    k.m_cond = split_into(k, [t], k.cond[:, :, 0:2], k.cond[:, :, 2:4], value[:])
    k.fold = small("fold", [2])
    k.m_fold = [k.v.go([k.m_ident], v.tensor_tensor, k.fold[0:4, :], k.ident[0:4, 0:2], k.ident[0:4, 2:4], ALU.add)]
    k.mod = [small(f"mod{l}", [6 * DC, 2]) for l in range(DEPTH)]

    lo = small("lb_logits_e", [2, DEPTH, HGH])
    k.lb, k.lb1 = small("lower_bound", [DEPTH, 2, HGH]), small("one_less_bound", [DEPTH, 2, HGH])
    mx, den = small("lb_max", [2, HGH]), small("lb_den", [2, HGH])
    logits = k.vec("lb", 0, 2 * DEPTH * HGH).rearrange("p (d l c) -> p d l c", d=2, l=DEPTH)
    t = k.v.go(k.m_vecs, v.tensor_tensor, mx[:], logits[:, :, 0, :], logits[:, :, 1, :], ALU.max)
    for l in range(DEPTH):
        u = k.v.go([t], v.tensor_tensor, lo[:, :, l, :], logits[:, :, l, :], mx[:], ALU.subtract)
    u = k.a.go([u], a.activation, lo[:], lo[:], ACT.Exp)
    t = k.v.go([u], v.tensor_tensor, den[:], lo[:, :, 0, :], lo[:, :, 1, :], ALU.add)
    t = k.v.go([t], v.reciprocal, den[:], den[:])
    for l in range(DEPTH):
        u = k.v.go([t], v.tensor_tensor, lo[:, :, l, :], lo[:, :, l, :], den[:], ALU.mult)
    t = k.v.go([u], v.tensor_tensor, mx[:], lo[:, :, 0, :], lo[:, :, 1, :], ALU.add)
    t0 = k.v.go([t], v.tensor_tensor, k.lb[:, 0], lo[:, :, 0, :], lo[:, :, 0, :], ALU.subtract)
    t1 = k.v.go([t], v.tensor_tensor, k.lb[:, 1], mx[:], lo[:, :, 0, :], ALU.subtract)
    k.m_lb = [k.v.go([t0, t1], v.tensor_scalar, k.lb1[:], k.lb[:], -1.0, 1.0, ALU.mult, ALU.add)]

    dl = place(k, "da_lambda", AT_WORK + 70, [DEPTH, 4, 32])
    loaded = k.loads.start([], dl[:], ins["da_lambda_2"].rearrange("l n d -> (l n d)").partition_broadcast(P))
    prod, sums, lam = place(k, "lambda_prod", AT_WORK + 71, [DEPTH, 2, 32]), small("lambda_sum", [DEPTH, 2]), small("minus_lambda", [DEPTH])
    t = k.v.go([loaded], v.tensor_tensor, prod[:], dl[:, :, 0::2, :], dl[:, :, 1::2, :], ALU.mult)
    t = k.v.go([t], v.tensor_reduce, sums[:], prod[:], AX.X, ALU.add)
    t = k.a.go([t], a.activation, sums[:], sums[:], ACT.Exp)
    k.sub = small("subln_gain", [DEPTH])
    for l in range(DEPTH):
        init = lambda_init(l)
        u = k.v.go([t], v.scalar_tensor_tensor, lam[:, l:l + 1], sums[:, l, 1:2], -init, sums[:, l, 0:1], ALU.add, ALU.subtract)
        u = k.v.go(k.m_vecs, v.tensor_scalar, k.sub[:, l:l + 1], k.vec("subln", l), 1.0 - init, None, ALU.mult)
    k.neg_lam, k.m_lam = lam, [u]

    k.resets = nc.alloc_sbuf_tensor("resets", [P, T2 + 1], mybir.dt.bfloat16)
    t = k.v.go([], v.memset, k.resets[:], 1.0)
    k.m_resets = [k.v.go([t], v.memset, k.resets[:, 0:T2 + 1:P], 0.0)]
    k.decays = small("tile_decays", [ST + CT])
    k.gains = [[small(f"gain{l}_{i}", [DC, 2]) for i in range(4)] for l in range(DEPTH)]


def lambda_init(l):
    return 0.8 - 0.6 * math.exp(-0.3 * l)


def modulate(k, l, row_buffers):
    nc = k.nc
    n_slabs = 6 * D // SLAB_F
    rows = {}

    def products_of(s):
        w_hi, w_lo, ready, slots = k.w.take("mod")
        bank = k.banks.take()
        k.pe.wait(ready + k.m_cond + bank.free)
        for kk in range(DC):
            for w in (w_hi, w_lo):
                last = nc.tensor.matmul(bank.ap[0:4, 0:SLAB_F], k.cond[:, kk, :], w[:, kk, :],
                                        start=kk == 0 and w is w_hi, stop=kk == DC - 1 and w is w_lo)
        done = k.pe.mark(last)
        for slot in slots:
            slot.free = [done]
        row = row_buffers.take()
        rows[s] = (row, k.v.go([done] + row.free, nc.vector.tensor_copy, row.ap[0:4, :], bank.ap[0:4, 0:SLAB_F]))
        k.banks.give(bank, [rows[s][1]])

    def columns_of(s):
        row, ready = rows.pop(s)
        bank = k.banks.take()
        k.pe.wait([ready] + k.m_fold + bank.free)
        for j in range(2):
            last = nc.tensor.matmul(bank.ap[:, 2 * j:2 * j + 2], row.ap[0:4, j * P:(j + 1) * P], k.fold[0:4, :],
                                    start=True, stop=True)
        done = k.pe.mark(last)
        row.free = [done]
        bias = k.vec("b_mod", 6 * DC * l + 2 * s, 2).unsqueeze(2).broadcast_to([P, 2, 2])
        t = k.v.go([done] + k.m_vecs, nc.vector.tensor_tensor, k.mod[l][:, 2 * s:2 * s + 2, :],
                   bank.ap[:, 0:4].rearrange("p (j n) -> p j n", j=2), bias, ALU.add)
        k.banks.give(bank, [t])
        return t

    for s in range(n_slabs):
        products_of(s)
        if s:
            columns_of(s - 1)
        yield
    t = columns_of(n_slabs - 1)
    for i, (m, add) in enumerate(((1, 1.0), (2, 0.0), (4, 1.0), (5, 0.0))):
        for j in range(2):
            k.m_gain = k.v.go([t], nc.vector.scalar_tensor_tensor, k.gains[l][i][:, :, j],
                              k.mod[l][:, m * DC:(m + 1) * DC, j], add, k.vec("norm_g", (4 * l + i) * DC, DC),
                              ALU.add, ALU.mult)
    yield


def adaln(k, l, which, x, x_ready, before, hi, lo, sides, rstd, temps):
    nc = k.nc
    spans = [LAT, CTXS][0:sides]
    root = inverse_rms(k, x_ready, [x[:, c, :] for c in range(DC)], spans, temps, rstd, before, D)
    gain, shift = k.gains[l][2 * which], 3 * DC * which
    marks = []
    for c in range(DC):
        t = temps.take()
        marks.append([])
        for j, (a, b) in enumerate(spans):
            n = k.v.go(root + t.free + [k.m_gain], nc.vector.scalar_tensor_tensor, t.ap[:, a:b], x[:, c, a:b],
                       gain[:, c, j:j + 1], rstd[:, a:b], ALU.mult, ALU.mult)
            add = k.mod[l][:, shift + c, j:j + 1]
            m_hi = k.a.go([n] + before, nc.scalar.activation, hi[:, c, a:b], t.ap[:, a:b], ACT.Identity, bias=add)
            m_lo = k.v.go([m_hi, n] + before, nc.vector.scalar_tensor_tensor, lo[:, c, a:b], t.ap[:, a:b], add,
                          hi[:, c, a:b].bitcast(F32), ALU.add, ALU.subtract)
            marks[-1] += [m_hi, m_lo]
        t.free = marks[-1]
    return marks


def add_normed(k, l, which, x, y, y_ready, before, sides, rstd, temps):
    nc = k.nc
    spans = [LAT, CTXS][0:sides]
    root = inverse_rms(k, y_ready, [y[:, c, :] for c in range(DC)], spans, temps, rstd, before, D)
    gain = k.gains[l][2 * which + 1]
    marks = []
    for c in range(DC):
        marks.append([])
        for j, (a, b) in enumerate(spans):
            n = k.v.go(root + y_ready[c], nc.vector.scalar_tensor_tensor, y[:, c, a:b], y[:, c, a:b], gain[:, c, j:j + 1],
                       rstd[:, a:b], ALU.mult, ALU.mult)
            stream, op = (k.g, nc.gpsimd.tensor_tensor) if c % 2 else (k.v, nc.vector.tensor_tensor)
            marks[-1].append(stream.go([n], op, x[:, c, a:b], x[:, c, a:b], y[:, c, a:b], ALU.add))
    return marks


def fourier_matrices(k, l):
    tag, start = f"b{l}_", now(k)
    m = Core()
    m.dl = place(k, tag + "dftl", AT_WORK + 42, [2, ST, S])
    m.dc = place(k, tag + "dftc", AT_WORK + 58, [2, CT, CTX])
    m.d64 = place(k, tag + "dft64", AT_WORK + 62, [2, P])
    m.m_64 = k.rows.start(start, m.d64[:], k.ins["c_dft64"])
    m.m_dl = k.rows.start(start, m.dl[:], k.ins["c_dftl"])
    m.m_dc = k.rows.start(start, m.dc[:], k.ins["c_dftc"])
    return m


def fourier(k, l, h, h_ready, y, start, sides, mats):
    nc = k.nc
    tag = f"b{l}_"
    u = place(k, tag + "u", AT_WORK + 24, [2, T2])
    half = place(k, tag + "half", AT_WORK + 30, [ST + CT, 2, 2, P])
    dl, dc, dft64, m_dl, m_dc, m_64 = mats.dl, mats.dc, mats.d64, mats.m_dl, mats.m_dc, mats.m_64
    spans = [LAT, CTXS][0:sides]
    ready = []

    def keep(chunk, banks, done):
        ready[:] = ready[-2:] + [copy_out(k, [done] + start, u[:, chunk, a:b], src) for src, a, b in banks]
        return ready[-len(banks):]

    yield from project(k, "ft", 1, h[:, 0], h[:, 1], h_ready, spans, keep)
    ready = [k.a.now(), k.v.now()]
    tiles = ST + CT if sides == 2 else ST
    for i in range(tiles):
        bank = k.banks.take()
        k.pe.wait(ready + [m_64] + bank.free)
        for c in range(2):
            last = nc.tensor.matmul(bank.ap[:, 256 * c:256 * c + 256], u[:, c, i * P:(i + 1) * P],
                                    dft64[:].rearrange("p s f -> p (s f)"), start=True, stop=True)
        mark = copy_out(k, [k.pe.mark(last)] + start, half[:, i].rearrange("p c s f -> p (c s f)"), bank.ap[:, :])
        k.banks.give(bank, [mark])
    ready = [k.a.now(), k.v.now()]
    for c in range(2):
        for (a, b), mat, m_mat, i0, n in ((LAT, dl, m_dl, 0, ST), (CTXS, dc, m_dc, ST, CT))[0:sides]:
            bank = k.banks.take()
            k.pe.wait(ready + [m_mat] + bank.free)
            for i in range(n):
                for s in range(2):
                    last = nc.tensor.matmul(bank.ap[:, 0:b - a], half[:, i0 + i, c, s, :], mat[:, s, i, :],
                                            start=i + s == 0, stop=i == n - 1 and s == 1)
            mark = copy_out(k, [k.pe.mark(last)] + start, y[:, 6 + c, a:b], bank.ap[:, 0:b - a])
            k.banks.give(bank, [mark])
        yield


def diff_attention(k, l, h, h_ready, y, sides):
    nc = k.nc
    tag = f"b{l}_"
    start = now(k)
    at = AT_WORK + 39
    dq, dk = place(k, tag + "dq", at, [2, T2]), place(k, tag + "dk", at + 6, [2, T2])
    dv = place(k, tag + "dv", at + 12, [ST + CT, 256])
    cos, sin = place(k, tag + "cos", at + 18, [S]), place(k, tag + "sin", at + 20, [S])
    probs = Ring([place(k, f"{tag}p{i}", AT_WORK + 6 * i, [2, T2]) for i in range(2)])
    turned = Ring([place(k, f"{tag}pt{i}", at + 22 + 3 * i, [ST + CT, P]) for i in range(2)])
    temps = Ring([place(k, f"{tag}dt{i}", at + 28 + 3 * i, [T2]) for i in range(2)])
    stats = Ring([place(k, f"{tag}ds{i}", at + 34 + 0.5 * i, [16]) for i in range(4)])
    for r in (probs, turned, temps, stats):
        for slot in r.slots:
            slot.free = start
    rot = place(k, tag + "rot", at + 36, [P])
    m_cos, m_sin = k.rows.start(start, cos[:], k.ins["c_cos"]), k.rows.start(start, sin[:], k.ins["c_sin"])
    m_rot = k.rows.start(start, rot[:], k.ins["c_rot"])
    scale = 32 ** -0.5

    def keep(dst, spans):
        def evacuate(chunk, banks, done):
            marks = [copy_out(k, [done] + start, dst[:, chunk, a:b], src) for src, a, b in banks]
            bank = k.banks.take()
            k.pe.wait(marks[0:1] + [m_rot] + bank.free)
            done = k.pe.mark(nc.tensor.matmul(bank.ap[:, :], rot[:], dst[:, chunk, 0:S], start=True, stop=True))
            t = temps.take()
            m1 = k.v.go([done, m_sin] + t.free, nc.vector.tensor_tensor, t.ap[:, 0:S], bank.ap[:, :], sin[:], ALU.mult)
            k.banks.give(bank, [m1])
            m2 = k.g.go([done, m_cos], nc.gpsimd.tensor_tensor, dst[:, chunk, 0:S], dst[:, chunk, 0:S], cos[:], ALU.mult)
            t.free = [k.v.go([m1, m2], nc.vector.tensor_tensor, dst[:, chunk, 0:S], dst[:, chunk, 0:S], t.ap[:, 0:S],
                             ALU.add)]
            return marks
        return evacuate

    both = [LAT, CTXS]
    for _ in project(k, "dq", 1, h[:, 0], h[:, 1], h_ready, both[0:sides], keep(dq, both[0:sides])):
        pass
    for _ in project(k, "dk", 1, h[:, 0], h[:, 1], h_ready, both, keep(dk, both)):
        pass

    def keep_v(i, src, done):
        return [copy_out(k, [done] + start, dv[:, i, :], src)]

    for _ in project_tokens(k, "dv", h[:, 0], h[:, 1], h_ready, [slice(i * P, (i + 1) * P) for i in range(ST + CT)],
                            keep_v):
        pass
    ready = [k.a.now(), k.v.now()]
    units = [(c, i, par, mp) for c in range(2) for i in range(ST + CT if sides == 2 else ST) for par in range(2)
             for mp in range(2)]
    state, held = {}, {}

    def key_span(i):
        return both if i < ST else both[1:]

    def scores(u):
        c, i, par, mp = u
        if mp == 0:
            state[c, i, par] = (probs.take(), stats.take())
        p, st = state[c, i, par]
        at = 64 * par + 32 * mp
        banks = []
        for j, (a, b) in enumerate(key_span(i)):
            bank = k.banks.take()
            k.pe.wait(ready + bank.free)
            done = k.pe.mark(nc.tensor.matmul(bank.ap[:, 0:b - a], dq[at:at + 32, c, i * P:(i + 1) * P],
                                              dk[at:at + 32, c, a:b], start=True, stop=True, tile_position=(at, 0)))
            t = k.v.go([done] + st.free, nc.vector.tensor_reduce, st.ap[:, 2 * mp + j:2 * mp + j + 1],
                       bank.ap[:, 0:b - a], AX.X, ALU.max)
            banks.append(bank)
        if len(banks) == 2:
            t = k.v.go([t], nc.vector.tensor_reduce, st.ap[:, 12 + mp:13 + mp], st.ap[:, 2 * mp:2 * mp + 2], AX.X, ALU.max)
            top = 12 + mp
        else:
            top = 2 * mp
        t = k.v.go([t], nc.vector.tensor_scalar, st.ap[:, 4 + mp:5 + mp], st.ap[:, top:top + 1], -scale, None, ALU.mult)
        state[u] = (banks, t)

    def soft(u):
        c, i, par, mp = u
        banks, t = state.pop(u)
        p, st = state[c, i, par]
        spans = key_span(i)
        for j, (a, b) in enumerate(spans):
            e = k.a.go([t] + p.free, nc.scalar.activation, p.ap[:, mp, a:b], banks[j].ap[:, 0:b - a], ACT.Exp,
                       bias=st.ap[:, 4 + mp:5 + mp], scale=scale, accum_out=st.ap[:, 6 + 2 * mp + j:7 + 2 * mp + j])
            k.banks.give(banks[j], [e])
        if mp == 0:
            return
        if len(spans) == 2:
            t = k.v.go([e], nc.vector.tensor_tensor, st.ap[:, 10:12], st.ap[:, 6:10:2], st.ap[:, 7:11:2], ALU.add)
        else:
            t = k.v.go([e], nc.vector.tensor_copy, st.ap[:, 10:12], st.ap[:, 6:10:2])
        t = k.v.go([t], nc.vector.reciprocal, st.ap[:, 12:14], st.ap[:, 10:12])
        t = k.v.go([t] + k.m_lam, nc.vector.tensor_tensor, st.ap[:, 14:15], st.ap[:, 13:14], k.neg_lam[:, l:l + 1], ALU.mult)
        a, b = spans[0][0], spans[-1][1]
        t = k.v.go([t], nc.vector.tensor_scalar, p.ap[:, 0, a:b], p.ap[:, 0, a:b], st.ap[:, 12:13], None, ALU.mult)
        t = k.v.go([t], nc.vector.scalar_tensor_tensor, p.ap[:, 0, a:b], p.ap[:, 1, a:b], st.ap[:, 14:15],
                   p.ap[:, 0, a:b], ALU.mult, ALU.add)
        st.free = [t]
        state[c, i, par] = (p, t)

    def turn(u):
        c, i, par, mp = u
        if mp == 0:
            return
        p, t = state[c, i, par]
        pt = turned.take()
        marks = []
        for group in (range(0, 3), range(3, 6)) if i < ST else (range(4, 6),):
            bank = k.banks.take()
            k.pe.wait([t] + bank.free)
            for n, b in enumerate(group):
                last = nc.tensor.transpose(bank.ap[:, n * P:(n + 1) * P], p.ap[:, 0, b * P:(b + 1) * P], k.ident[:])
            done = k.pe.mark(last)
            marks.append(copy_out(k, [done] + pt.free, pt.ap[:, group[0]:group[-1] + 1, :].rearrange("p b q -> p (b q)"),
                                  bank.ap[:, 0:len(group) * P]))
            k.banks.give(bank, marks[-1:])
        p.free = [done]
        state[c, i, par] = (pt, marks)

    def values(u):
        c, i, par, mp = u
        if mp == 0:
            return
        pt, marks = state.pop((c, i, par))
        side = 0 if i < ST else 1
        if (c, side) not in held:
            held[c, side] = k.banks.take()
        bank = held[c, side]
        k.pe.wait(marks + ready + bank.free)
        tiles = list(range(0 if side == 0 else ST, ST + CT))
        q0 = (i - ST * side) * P
        for b in tiles:
            last = nc.tensor.matmul(bank.ap[64 * par:64 * par + 64, q0:q0 + P], dv[:, b, (2 * c + par) * 64:(2 * c + par + 1) * 64],
                                    pt.ap[:, b, :], start=b == tiles[0], stop=b == tiles[-1])
        done = k.pe.mark(last)
        pt.free = [done]
        if par == 1 and i in (ST - 1, ST + CT - 1):
            a, b = both[side]
            m1 = copy_out(k, [done], y[:, 4 + c, a:b], bank.ap[:, 0:b - a])
            k.banks.give(bank, [m1])
            rstd = temps.take()
            root = inverse_rms(k, [[m1]], [y[:, 4 + c, :]], [(a, b)], without(temps, rstd), rstd.ap, rstd.free, 64,
                               ones=k.pair)
            rstd.free = [k.v.go(root + k.m_lam, nc.vector.scalar_tensor_tensor, y[:, 4 + c, a:b], y[:, 4 + c, a:b],
                                k.sub[:, l:l + 1], rstd.ap[:, a:b], ALU.mult, ALU.mult)]

    return pipeline(units, [scores, soft, turn, values])


class Recurrent:

    def __init__(self, k, l, h, h_ready, y, sides):
        self.k, self.l, self.h, self.h_ready, self.y, self.sides = k, l, h, h_ready, y, sides
        self.heads = {}

    def project(self, hc):
        k, l, nc = self.k, self.l, self.k.nc
        at, start = AT_WORK + 24 + 15 * (hc % 2), now(k)
        nm = f"b{l}_r{hc}_"
        m = self.heads[hc] = Core()
        m.q, m.v, m.f, m.b, m.g = [place(k, nm + n, at + 3 * i, [T2]) for i, n in enumerate("qvfbg")]
        m.ready = []
        spans = [LAT, CTXS]

        def keep_silu(dst):
            def evacuate(chunk, banks, done):
                marks = []
                for src, a, b in banks:
                    t = k.a.go([done] + start, nc.scalar.activation, dst[:, a:b], src, ACT.Sigmoid)
                    marks.append(k.v.go([t], nc.vector.tensor_tensor, dst[:, a:b], dst[:, a:b], src, ALU.mult))
                m.ready += marks
                return marks
            return evacuate

        def keep_gate(d, dst):
            def evacuate(chunk, banks, done):
                marks = []
                for src, a, b in banks:
                    t = k.a.go([done] + start, nc.scalar.activation, dst[:, a:b], src, ACT.Sigmoid)
                    marks.append(t)
                    m.ready.append(k.v.go([t] + k.m_lb, nc.vector.tensor_scalar, dst[:, a:b], dst[:, a:b],
                                          k.lb1[:, l, d, hc:hc + 1], k.lb[:, l, d, hc:hc + 1], ALU.mult, ALU.add))
                return marks
            return evacuate

        def keep_v(i, src, done):
            m.ready.append(copy_out(k, [done] + start, m.v[:, i * P:(i + 1) * P], src))
            return m.ready[-1:]

        def feature_major(name, sp, evacuate):
            return project(k, name, 1, self.h[:, 0], self.h[:, 1], self.h_ready, sp, evacuate)

        yield from feature_major("q", spans[0:self.sides], keep_silu(m.q))
        yield from feature_major("f", spans, keep_gate(0, m.f))
        yield from feature_major("b", spans, keep_gate(1, m.b))
        yield from feature_major("g", spans[0:self.sides], keep_silu(m.g))
        yield from project_tokens(k, "v", self.h[:, 0], self.h[:, 1], self.h_ready,
                                  [slice(i * P, (i + 1) * P) for i in range(ST + CT)], keep_v)

    def units(self, hc):
        k, l, nc, y, sides = self.k, self.l, self.k.nc, self.y, self.sides
        at, nm = AT_WORK + 54, f"b{l}_u{hc}_"
        spans = [LAT, CTXS]
        m = self.heads[hc]
        q, v, g, ready = m.q, m.v, m.g, m.ready
        if hc == 0:
            self.start = now(k)
            self.gla = nc.alloc_sbuf_tensor_at(f"b{l}_gla", [P, 2, LEVELS + 1, P], U8, offset=ARENA + (at + 21) * 1024)
            wide = place(k, f"b{l}_gla_wide", at, [2, LEVELS + 1, P])
            loaded = k.rows.start(self.start, wide[:], k.ins["c_gla"])
            self.m_gla = k.g.go([loaded] + self.start, nc.gpsimd.tensor_copy, self.gla[:], wide[:])
            self.start = self.start + [self.m_gla]
        gla, m_gla, start = self.gla, self.m_gla, self.start
        ex = fresh([place(k, f"{nm}ex{i}", at + 3 * i, [T2]) for i in range(3)], now(k) + start)
        kk, bc, sc = [place(k, nm + n, at + 9 + 3 * i, [T2]) for i, n in enumerate(("k", "bc", "sc"))]
        kdt = place(k, nm + "kdt", at + 18, [ST + CT, P])
        dec = k.decays
        tiles = ST + CT if sides == 2 else ST
        T = tiles * P
        bank_tiles = [(0, ST), (ST, ST + CT)][0:sides]

        for d in range(2):
            unit = ready + now(k)
            f, qh = (m.f, m.b)[d][:], q[:]
            m_k = k.g.go(unit, nc.gpsimd.tensor_scalar, kk[:], f, -1.0, 1.0, ALU.mult, ALU.add)
            t = k.v.go(unit + [m_k], nc.vector.tensor_scalar, f, f, 2.0 ** -64, None, ALU.max)
            t = k.a.go([t], nc.scalar.activation, f, f, ACT.Ln)
            if d == 0:
                m_b = k.v.go([t] + k.m_resets, nc.vector.tensor_tensor_scan, bc[:], k.resets[:, 0:T2], f, 0.0,
                             ALU.mult, ALU.add)
            else:
                m_b = k.v.go([t] + k.m_resets, nc.vector.tensor_tensor_scan, bc[:, ::-1], k.resets[:, T2:0:-1],
                             f[:, ::-1], 0.0, ALU.mult, ALU.add)
            m_sc = k.g.go(unit, nc.gpsimd.memset, sc[:, 0:T], 0.0)

            work = {}

            def decays(lv):
                if lv == LEVELS:
                    return
                x = ex.take()
                n = 1 << lv
                bp = bc[:, 0:T].rearrange("p (n s m) -> p n s m", s=2, m=n)
                xp = x.ap[:, 0:T].rearrange("p (n s m) -> p n s m", s=2, m=n)
                key, query = (0, 1) if d == 0 else (1, 0)
                edge = bp[:, :, 0, n - 1:n] if d == 0 else bp[:, :, 1, 0:1]
                edge = edge.broadcast_to([P, T // (2 * n), n])
                a1 = k.g.go([m_b] + x.free, nc.gpsimd.tensor_tensor, xp[:, :, key, :], edge, bp[:, :, key, :], ALU.subtract)
                a2 = k.v.go([m_b] + x.free, nc.vector.tensor_tensor, xp[:, :, query, :], bp[:, :, query, :], edge, ALU.subtract)
                e = k.a.go([a1, a2], nc.scalar.activation, x.ap[:, 0:T], x.ap[:, 0:T], ACT.Exp)
                work[lv] = (x, xp, key, query, n, e)

            def scores(lv):
                if lv < LEVELS:
                    x, xp, key, query, n, e = work[lv]
                    parts = lambda ap: ap[:, 0:T].rearrange("p (n s m) -> p n s m", s=2, m=n)
                    e1 = k.g.go([e, m_k], nc.gpsimd.tensor_tensor, xp[:, :, key, :], xp[:, :, key, :],
                                parts(kk)[:, :, key, :], ALU.mult)
                    e2 = k.v.go([e] + ready, nc.vector.tensor_tensor, xp[:, :, query, :], xp[:, :, query, :],
                                parts(qh)[:, :, query, :], ALU.mult)
                    keys, queries, e = x.ap, x.ap, [e1, e2]
                else:
                    keys, queries, e = kk, qh, [m_k] + ready
                banks = []
                for i0, i1 in bank_tiles:
                    bank = k.banks.take()
                    k.pe.wait(e + bank.free)
                    for i in range(i0, i1):
                        last = nc.tensor.matmul(bank.ap[:, (i - i0) * P:(i - i0 + 1) * P], keys[:, i * P:(i + 1) * P],
                                                queries[:, i * P:(i + 1) * P], start=True, stop=True)
                    banks.append((bank, i0, i1, k.pe.mark(last)))
                if lv < LEVELS:
                    x.free = [banks[-1][3]]
                work[lv] = banks

            def masked(lv):
                for bank, i0, i1, done in work.pop(lv):
                    n = i1 - i0
                    mask = gla[:, d, lv, :].unsqueeze(1).broadcast_to([P, n, P])
                    c = k.v.go([done, m_sc, m_gla, m_last[0]], nc.vector.copy_predicated,
                               sc[:, i0 * P:i1 * P].rearrange("p (n t) -> p n t", n=n), mask,
                               bank.ap[:, 0:n * P].rearrange("p (n t) -> p n t", n=n))
                    k.banks.give(bank, [c])
                    m_last[0] = c

            m_last = [m_sc]
            yield from pipeline(range(LEVELS + 1), [decays, scores, masked])
            m_scores = m_last[0]

            last_of = bc[:, P - 1::P] if d == 0 else bc[:, 0::P]
            m_dec = k.a.go([m_b] + unit, nc.scalar.activation, dec[:], last_of, ACT.Exp)
            kd, qd, st = ex.take(), ex.take(), ex.take()
            b3 = bc[:].rearrange("p (n t) -> p n t", t=P)
            t = k.g.go([m_b] + kd.free, nc.gpsimd.tensor_tensor, kd.ap[:].rearrange("p (n t) -> p n t", t=P),
                       last_of.unsqueeze(2).broadcast_to([P, ST + CT, P]), b3, ALU.subtract)
            t = k.a.go([t], nc.scalar.activation, kd.ap[:], kd.ap[:], ACT.Exp)
            m_kd = k.v.go([t], nc.vector.tensor_tensor, kd.ap[:], kd.ap[:], kk[:], ALU.mult)
            t = k.a.go([m_b] + qd.free, nc.scalar.activation, qd.ap[:, 0:T], bc[:, 0:T], ACT.Exp)
            m_qd = k.v.go([t], nc.vector.tensor_tensor, qd.ap[:, 0:T], qd.ap[:, 0:T], qh[:, 0:T], ALU.mult)
            order = [4, 5, 0, 1, 2, 3] if d == 0 else [5, 4, 3, 2, 1, 0]
            m_t = []
            for group in (range(0, 3), range(3, 6)):
                bank = k.banks.take()
                k.pe.wait([m_kd] + bank.free)
                for n, i in enumerate(group):
                    last = nc.tensor.transpose(bank.ap[:, n * P:(n + 1) * P], kd.ap[:, i * P:(i + 1) * P], k.ident[:])
                done = k.pe.mark(last)
                m_t.append(copy_out(k, [done] + unit, kdt[:, group[0]:group[-1] + 1, :].rearrange("p n k -> p (n k)"),
                                    bank.ap[:, 0:3 * P]))
                k.banks.give(bank, m_t[-1:])
            kd.free = [done, m_kd]
            sums = [k.banks.take(), k.banks.take()]
            for bank in sums:
                k.pe.wait(bank.free)
            k.pe.wait(m_t + ready)
            for n, i in enumerate(order[:-1]):
                last = nc.tensor.matmul(sums[n // 4].ap[:, (n % 4) * P:(n % 4 + 1) * P], kdt[:, i, :],
                                        v[:, i * P:(i + 1) * P], start=True, stop=True)
            done = k.pe.mark(last)
            states = st.ap[:].rearrange("p (n v) -> p n v", v=P)
            for n, i in enumerate(order[:-1]):
                part = sums[n // 4].ap[:, (n % 4) * P:(n % 4 + 1) * P]
                if n == 0:
                    m_st = k.v.go([done] + st.free, nc.vector.tensor_copy, states[:, 1, :], part)
                else:
                    m_st = k.v.go([m_st, m_dec], nc.vector.scalar_tensor_tensor, states[:, n + 1, :], states[:, n, :],
                                  dec[:, i:i + 1], part, ALU.mult, ALU.add)
            for bank in sums:
                k.banks.give(bank, [m_st])
            for i0, i1 in bank_tiles:
                bank = k.banks.take()
                k.pe.wait([m_st, m_qd, m_scores] + bank.free)
                for i in range(i0, i1):
                    out = bank.ap[:, (i - i0) * P:(i - i0 + 1) * P]
                    n = order.index(i)
                    if n:
                        nc.tensor.matmul(out, states[:, n, :], qd.ap[:, i * P:(i + 1) * P], start=True, stop=False)
                    last = nc.tensor.matmul(out, v[:, i * P:(i + 1) * P], sc[:, i * P:(i + 1) * P],
                                            start=n == 0, stop=True)
                done = k.pe.mark(last)
                a, b = i0 * P, i1 * P
                if d == 0:
                    m_o = k.v.go([done] + start, nc.vector.tensor_copy, y[:, hc, a:b], bank.ap[:, 0:b - a])
                else:
                    m_o = k.v.go([done], nc.vector.tensor_tensor, y[:, hc, a:b], y[:, hc, a:b], bank.ap[:, 0:b - a], ALU.add)
                k.banks.give(bank, [m_o])
            qd.free = st.free = [done]
            yield
        rstd = ex.take()
        for a, b in spans[0:sides]:
            root = inverse_rms(k, [[m_o]], [y[:, hc, :]], [(a, b)], without(ex, rstd), rstd.ap, rstd.free, P)
            t = k.v.go(root, nc.vector.scalar_tensor_tensor, y[:, hc, a:b], y[:, hc, a:b], k.vec("onorm", l),
                       rstd.ap[:, a:b], ALU.mult, ALU.mult)
            t = k.v.go([t], nc.vector.tensor_tensor, y[:, hc, a:b], y[:, hc, a:b], g[:, a:b], ALU.mult)
        rstd.free = [t]
        yield


def second_layer(k, l, x, x_ready, before):
    nc = k.nc
    tag = f"b{l}_"
    sides = 2 if l < DEPTH - 1 else 1
    start = now(k)
    h = place(k, tag + "h", AT_H, [2, DC, T2], F32R)
    y = place(k, tag + "y", AT_WORK, [DC, T2])
    rstd = place(k, tag + "rstd", AT_WORK + 74, [T2])
    norm_buffers = [place(k, f"{tag}n{i}", AT_WORK + 24 + 3 * i, [T2]) for i in range(3)]

    mats = fourier_matrices(k, l)
    h_ready = adaln(k, l, 0, x, x_ready, before + [k.v.now()], h[:, 0], h[:, 1], 2, rstd, fresh(norm_buffers, start))
    start = now(k)
    for _ in fourier(k, l, h, h_ready, y, start, sides, mats):
        pass
    rec = Recurrent(k, l, h, h_ready, y, sides)
    attention = diff_attention(k, l, h, h_ready, y, sides)
    for _ in weave(attention, rec.project(0), 7 / (48 if sides == 2 else 32)):
        pass
    for hc in range(HGH):
        for _ in weave(rec.units(hc), rec.project(hc + 1) if hc + 1 < HGH else iter(()), 7 / 22):
            pass
    mixed = now(k)
    ys = place(k, tag + "ys", AT_H, [2, DC, T2], F32R)
    end = T2 if sides == 2 else S
    ys_ready = [split_into(k, mixed, ys[:, 0, c, 0:end], ys[:, 1, c, 0:end], y[:, c, 0:end]) for c in range(DC)]
    spans = [LAT, CTXS][0:sides]
    out = place(k, tag + "out", AT_WORK + 33, [DC, T2])
    out_ready = [None] * DC

    def keep(chunk, banks, done):
        out_ready[chunk] = [copy_out(k, [done] + mixed, out[:, chunk, a:b], src) for src, a, b in banks]
        return out_ready[chunk]

    for _ in project(k, "w_out", 4, ys[:, 0], ys[:, 1], ys_ready, spans, keep):
        pass
    temps = fresh(norm_buffers, mixed)
    x_ready = add_normed(k, l, 0, x, out, out_ready, mixed, sides, rstd, temps)

    h_ready = adaln(k, l, 1, x, x_ready, [k.pe.now(), k.v.now()], h[:, 0], h[:, 1], sides, rstd, temps)
    hidden = place(k, tag + "hidden", AT_WORK + 33, [2, 6, T2], F32R)
    acts_ring = temps
    acts, hidden_ready, hidden_free = {}, [None] * 6, now(k)

    def ff_g(chunk, banks, done):
        t = acts_ring.take()
        freed = []
        for src, a, b in banks:
            m = k.a.go([done] + t.free, nc.scalar.activation, t.ap[:, a:b], src, ACT.Sigmoid)
            freed.append(k.v.go([m], nc.vector.tensor_tensor, t.ap[:, a:b], t.ap[:, a:b], src, ALU.mult))
        acts[chunk] = (t, freed)
        return freed

    def ff_u(c0):
        def evacuate(chunk, banks, done):
            t, ms = acts.pop(chunk)
            for src, a, b in banks:
                last = k.v.go([done] + ms, nc.vector.tensor_tensor, t.ap[:, a:b], t.ap[:, a:b], src, ALU.mult)
            end = banks[-1][2]
            t.free = split_into(k, [last] + hidden_free, hidden[:, 0, chunk - c0, 0:end], hidden[:, 1, chunk - c0, 0:end],
                                t.ap[:, 0:end])
            hidden_ready[chunk - c0] = t.free
            return [last]
        return evacuate

    def down(first):
        def evacuate(chunk, banks, done):
            if first:
                y_ready[chunk] = [copy_out(k, [done] + hidden_free, y[:, chunk, a:b], src) for src, a, b in banks]
            else:
                y_ready[chunk] = [k.v.go([done] + y_ready[chunk], nc.vector.tensor_tensor, y[:, chunk, a:b],
                                         y[:, chunk, a:b], src, ALU.add) for src, a, b in banks]
            return y_ready[chunk]
        return evacuate

    y_ready = [None] * DC
    for c0, n in FF_PARTS2:
        for c in range(0, n, 2):
            for _ in project(k, "ff_g", 1, h[:, 0], h[:, 1], h_ready, spans, ff_g, c0 + c):
                pass
            for _ in project(k, "ff_u", 1, h[:, 0], h[:, 1], h_ready, spans, ff_u(c0), c0 + c):
                pass
        before = now(k)
        for _ in project(k, "ff_out", 4, hidden[:, 0], hidden[:, 1], hidden_ready, spans, down(c0 == 0)):
            pass
        hidden_free = [k.pe.now()]
    x_ready = add_normed(k, l, 1, x, y, y_ready, before, sides, rstd, temps)
    return x_ready, before


def program(nc, ins, out, order=None):
    k = set_up(nc, ins)
    x = place(k, "x", AT_X, [DC, T2])
    rows = place(k, "x_rows", AT_WORK + 16, [ST, D])
    rows_ctx = place(k, "ctx_rows", AT_WORK + 32, [CT, D])
    loaded = load_rows(k, ins["x"][0], ST, rows, [])
    load_constants(k)
    stage = place(k, "vector_rows", AT_WORK, [4 * P])
    load_vectors(k, stage)
    k.w = Weights(k, first_slabs(ins) + modulation_slabs(ins) + second_slabs(ins), order)
    x1 = x[:, :, 0:S]
    x_ready = transpose_in(k, loaded, ST, x1, rows)
    second_set_up(k)
    before = now(k)
    for l in range(DEPTH):
        x_ready, before = first_layer(k, l, x1, x[:, :, S:T2], x_ready, before)
    rstd = place(k, "f_rstd", AT_WORK + 74, [S])
    temps = fresh([place(k, f"f_t{i}", AT_WORK + 64 + 2 * i, [S]) for i in range(3)], before)
    loaded = load_rows(k, ins["ctx_2"][0], CT, rows_ctx, now(k))
    x_ready = norm_plain(k, x1, x_ready, before, lambda c: k.vec("norm_f", c), None, None, SPAN1, rstd, temps, out=x1)
    ctx_ready = transpose_in(k, loaded, CT, x[:, :, S:T2], rows_ctx)
    x_ready = [a + b for a, b in zip(x_ready, ctx_ready)]
    for l in range(DEPTH):
        x_ready, before = second_layer(k, l, x, x_ready, before)
    transpose_out(k, x, x_ready, out[0])
    return k.w.used


INPUTS = ("x", "norm1", "w_in", "b_gate", "w_br", "w_o", "norm2", "w_up", "conv_w", "conv_b", "w_down", "norm_f",
          "c_2", "ctx_2", "c_ctx_2", "w_mod_2", "b_mod_2", "norm_g_2", "w_in_2", "w_out_2", "hg_lb_logits_2",
          "hg_onorm_2", "da_lambda_2", "da_subln_2", "w_ffn_in_2", "w_ffn_out_2")


def kernel(**inputs):
    import concourse.bacc as bacc
    from concourse.bass_utils import run_bass_kernel_spmd

    arrays = {name: np.ascontiguousarray(inputs[name]) for name in INPUTS}
    arrays.update(constants())
    order = None
    for _ in range(2):
        nc = bacc.Bacc("TRN2", target_bir_lowering=False, num_devices=1)
        ins = {name: nc.dram_tensor(name, a.shape, mybir.dt.from_np(a.dtype), kind="ExternalInput").ap()
               for name, a in arrays.items()}
        out = nc.dram_tensor("y_out", (1, S, D), F32, kind="ExternalOutput").ap()
        order = program(nc, ins, out, order)
    return run_bass_kernel_spmd(nc, [arrays], core_ids=[0]).results[0]["y_out"]
```

```python
import math

import numpy as np

import concourse.bass as bass
from concourse import mybir

F32 = mybir.dt.float32
F32R = mybir.dt.float32r
U8 = mybir.dt.uint8
ACT = mybir.ActivationFunctionType
ALU = mybir.AluOpType
AX = mybir.AxisListType

P = 128
D = 1024
DC = D // P
S = 512
ST = S // P
CTX = 256
CT = CTX // P
T2 = S + CTX
FF = 2816
FC = FF // P
DEPTH = 2
EPS = 1e-6

HD = 64
GROUPS = ((128, 1), (512, 4), (2048, 16))
ORDER = (1, 4, 4)
GH = 4
W_A = GH * len(GROUPS) * HD
W_B = 256
GATE0 = 3 * W_A + 3 * W_B
SLOPES = [float(np.float32(2.0 ** (-8.0 * n / 12))) for n in range(1, 13)]
FAR = 1e32

HGH = 4
LEVELS = 7
DAH = 4
GRID_W = 64

SLAB_K, SLAB_F = 8, 256



def distances(kind):
    window, dil = GROUPS[kind]
    q = np.arange(P)[:, None]
    if kind == 0:
        k = np.arange(2 * P)[None, :]
        delta = q + P - k
        ok = (delta >= 0) & (delta <= window)
    else:
        k = np.arange(P)[None, :]
        delta = (q - k) * ORDER[kind]
        ok = (delta >= 0) & (delta % dil == 0) & (delta <= window)
    return np.where(ok, -delta, -FAR).astype(np.float32)


def gla_masks():
    s, t = np.arange(P)[:, None], np.arange(P)[None, :]
    out = np.zeros((2, LEVELS + 1, P, P), np.float32)
    for lv in range(LEVELS):
        m = 1 << lv
        same = s // (2 * m) == t // (2 * m)
        out[0, lv] = same & (s // m % 2 == 0) & (t // m % 2 == 1)
        out[1, lv] = same & (s // m % 2 == 1) & (t // m % 2 == 0)
    out[:, LEVELS] = s == t
    return out


def constants():
    j = np.arange(P)
    c = {}
    c["c_ident"] = np.eye(P, dtype=np.float32)
    c["c_ones"] = np.ones((P, P), np.float32)
    c["c_pair"] = (j[:, None] // HD == j[None, :] // HD).astype(np.float32)
    c["c_dist0"], c["c_dist1"], c["c_dist2"] = distances(0), distances(1), distances(2)
    before = j[None, :] < j[:, None]
    c["c_causal"] = before.astype(np.float32)
    c["c_causal_neg"] = np.where(before, 0.0, -1e30).astype(np.float32)
    c["c_gla"] = np.ascontiguousarray(gla_masks().transpose(2, 0, 1, 3))
    f32 = np.float32
    inv = f32(1.0) / (f32(10000.0) ** (np.arange(0, 16, 2, dtype=f32) / f32(16)))
    t = np.arange(S)
    pos = np.stack([t // GRID_W, t % GRID_W]).astype(f32)
    feat = j % 32
    ang = pos[feat // 16, :] * inv[feat % 8][:, None].astype(f32)
    c["c_cos"], c["c_sin"] = np.cos(ang).astype(f32), np.sin(ang).astype(f32)
    rot = np.zeros((P, P), f32)
    for f in range(P):
        if f // 8 % 2 == 0:
            rot[f + 8, f] = -1.0
        else:
            rot[f - 8, f] = 1.0
    c["c_rot"] = rot
    a = 2 * np.pi * np.outer(np.arange(64), np.arange(64)) / 64
    d64 = np.zeros((P, 2, P))
    for g in range(2):
        d64[64 * g:64 * g + 64, 0, 64 * g:64 * g + 64] = np.cos(a)
        d64[64 * g:64 * g + 64, 1, 64 * g:64 * g + 64] = -np.sin(a)
    c["c_dft64"] = d64.astype(f32)
    for name, n in (("c_dftl", S), ("c_dftc", CTX)):
        a = 2 * np.pi * (np.outer(np.arange(n), np.arange(n)) % n) / n
        w = np.stack([np.cos(a), np.sin(a)]) / math.sqrt(n * 64)
        c[name] = np.ascontiguousarray(w.reshape(2, n // P, P, n).transpose(2, 0, 1, 3)).astype(f32)
    return c



class Stream:

    def __init__(self, nc, engine, name):
        self.engine, self.sem = engine, nc.alloc_semaphore(f"{name}_done")
        self.count, self.seen = 0, {}


    def wait(self, marks):
        for sem, value in marks:
            if self.seen.get(sem.name, 0) < value:
                self.engine.wait_ge(sem, value)
                self.seen[sem.name] = value

    def mark(self, instruction):
        instruction.then_inc(self.sem, 1)
        self.count += 1
        return (self.sem, self.count)

    def now(self):
        return (self.sem, self.count)

    def go(self, after, op, *args, **kw):
        self.wait(after)
        return self.mark(op(*args, **kw))


class ScalarStream(Stream):

    BOTH = (ACT.Exp, ACT.Ln)
    ANY = (ACT.Copy, ACT.Identity, ACT.Square, ACT.Abs)
    table = None

    def go(self, after, op, out, in_, func, **kw):
        if func in self.BOTH:
            if self.table != "both":
                self.engine.preload_act_table_set("natural_log_exp_and_others")
            self.table = "both"
        elif func not in self.ANY:
            self.table = func
        return super().go(after, op, out, in_, func, **kw)


class Slot:

    def __init__(self, ap):
        self.ap, self.free = ap, []


class Ring:
    def __init__(self, aps):
        self.slots, self.at = [Slot(a) for a in aps], 0

    def take(self):
        s = self.slots[self.at % len(self.slots)]
        self.at += 1
        return s


class Shared:

    def __init__(self, banks):
        self.idle = [Slot(b) for b in banks]

    def take(self):
        return self.idle.pop(0)

    def give(self, slot, marks):
        slot.free = list(marks)
        self.idle.append(slot)


class DmaQueue:

    def __init__(self, nc, stream, name, n):
        self.stream, self.sems, self.at = stream, [nc.alloc_semaphore(f"{name}{i}") for i in range(n)], 0
        self.used = [0] * n

    def start(self, after, dst, src):
        i = self.at % len(self.sems)
        self.at += 1
        if self.used[i]:
            self.stream.wait([(self.sems[i], self.used[i])])
        self.stream.wait(after)
        self.stream.engine.dma_start(dst, src).then_inc(self.sems[i], 16)
        self.used[i] += 16
        return (self.sems[i], self.used[i])


def weave(main, filler, steps):
    owed = 0.0
    for _ in main:
        owed += steps
        while owed >= 1:
            owed -= 1
            next(filler, None)
        yield
    yield from filler


def pipeline(units, stages):
    for step in range(len(units) + len(stages) - 1):
        for k in reversed(range(len(stages))):
            if 0 <= step - k < len(units):
                stages[k](units[step - k])
        yield



class Core:
    pass






SBUF_END = 229344
ARENA_KB = 149
ARENA = SBUF_END - int(ARENA_KB * 1024)
AT_X = 0
AT_H = 24
AT_WORK = 72


def place(k, name, kb, shape, dtype=F32):
    size = 4 * int(np.prod(shape))
    assert kb * 1024 + size <= ARENA_KB * 1024, name
    return k.nc.alloc_sbuf_tensor_at(name, [P] + list(shape), dtype, offset=int(ARENA + kb * 1024))


def set_up(nc, ins):
    k = Core()
    k.nc, k.ins = nc, ins
    k.pe, k.v = Stream(nc, nc.tensor, "pe"), Stream(nc, nc.vector, "dve")
    k.a, k.g = ScalarStream(nc, nc.scalar, "act"), Stream(nc, nc.gpsimd, "pool")
    k.sp = Stream(nc, nc.sync, "sp")
    k.weights = DmaQueue(nc, k.sp, "weights_in", 4)
    k.loads = DmaQueue(nc, k.a, "loads", 8)
    k.rows = DmaQueue(nc, k.sp, "rows_in", 4)
    k.stores = DmaQueue(nc, k.sp, "stores", 4)
    k.turn = 0

    k.banks = Shared([nc.alloc_psum_tensor(f"bank{i}", [P, 512], F32) for i in range(8)])
    SLAB = SLAB_K * SLAB_F
    k.raw = Ring([nc.alloc_sbuf_tensor(f"w_raw{i}", [P, SLAB], F32) for i in range(2)])
    k.whi = Ring([nc.alloc_sbuf_tensor(f"w_hi{i}", [P, SLAB], F32R) for i in range(2)])
    k.wlo = Ring([nc.alloc_sbuf_tensor(f"w_lo{i}", [P, SLAB], F32R) for i in range(2)])

    return k


def load_constants(k):
    nc, ins = k.nc, k.ins

    def const(name, shape, dtype=F32):
        t = nc.alloc_sbuf_tensor(name[2:] + "_c", [P] + shape, dtype)
        m = k.loads.start([], t[:], ins[name])
        return t, m

    k.ident, k.m_ident = const("c_ident", [P])
    k.ones, k.m_ones = const("c_ones", [P])
    k.pair, k.m_pair = const("c_pair", [P])
    k.dist, k.m_dist = zip(const("c_dist0", [2 * P]), const("c_dist1", [P]), const("c_dist2", [P]))
    k.causal, k.m_causal = const("c_causal", [P])
    k.causal_neg, k.m_causal_neg = const("c_causal_neg", [P])
    k.zeros = nc.alloc_sbuf_tensor("zeros", [P, 1], F32)
    k.m_zeros = k.v.go([], nc.vector.memset, k.zeros[:], 0.0)
    k.eps = nc.alloc_sbuf_tensor("eps", [P, 1], F32)
    k.m_eps = k.v.go([], nc.vector.memset, k.eps[:], EPS)



def now(k):
    return [k.pe.now(), k.v.now(), k.a.now(), k.g.now()]


def copy_out(k, after, out, in_, scale=None):
    k.turn += 1
    if k.turn % 2:
        return k.a.go(after, k.nc.scalar.activation, out, in_, ACT.Copy, scale=1.0 if scale is None else scale)
    if scale is None:
        return k.v.go(after, k.nc.vector.tensor_copy, out, in_)
    return k.v.go(after, k.nc.vector.tensor_scalar, out, in_, scale, None, ALU.mult)


def load_vectors(k, stage):
    nc, ins = k.nc, k.ins

    def rows(name, pattern, **kw):
        return ins[name].rearrange(pattern, p=P, **kw)

    lists = [
        ("norm1", rows("norm1", "l (c p) -> (l c) p")), ("b_gate", rows("b_gate", "l (c p) -> (l c) p")),
        ("norm2", rows("norm2", "l (c p) -> (l c) p")), ("conv_w", rows("conv_w", "l w (c p) -> (l w c) p")),
        ("conv_b", rows("conv_b", "l (c p) -> (l c) p")), ("norm_f", rows("norm_f", "(c p) -> c p")),
        ("b_mod", rows("b_mod_2", "l (c p) -> (l c) p")), ("norm_g", rows("norm_g_2", "l n (c p) -> (l n c) p")),
        ("lb", rows("hg_lb_logits_2", "d l (c p) -> (d l c) p")), ("onorm", ins["hg_onorm_2"]),
        ("c", rows("c_2", "o (c p) -> (o c) p")), ("c_ctx", rows("c_ctx_2", "(c p) -> c p")),
        ("subln", None),
    ]
    at, base, loaded = 0, {}, []
    for name, src in lists:
        base[name] = at
        n = DEPTH if src is None else src.shape[0]
        done = 0
        while done < n:
            row, tile = (at + done) % P, (at + done) // P
            m = min(n - done, P - row)
            dst = stage[row:row + m, tile * P:(tile + 1) * P]
            if src is None:
                for h in range(2):
                    loaded.append(k.loads.start([], dst[:, 64 * h:64 * h + 64], ins["da_subln_2"][done:done + m, :]))
            else:
                loaded.append(k.loads.start([], dst, src[done:done + m, :]))
            done += m
        at += n
    k.vecs = nc.alloc_sbuf_tensor("vectors", [P, at], F32)
    bank, k.m_vecs = k.banks.take(), []
    for tile in range(-(-at // P)):
        n = min(P, at - tile * P)
        k.pe.wait(loaded + [k.m_ident])
        done = k.pe.mark(nc.tensor.transpose(bank.ap[:, tile * P:tile * P + n], stage[0:n, tile * P:(tile + 1) * P],
                                             k.ident[0:n, 0:n]))
    k.m_vecs = [k.v.go([done], nc.vector.tensor_copy, k.vecs[:], bank.ap[:, 0:at])]
    k.banks.give(bank, k.m_vecs)
    k.vec = lambda name, i, n=1: k.vecs[:, base[name] + i:base[name] + i + n]



MOD_SLABS = 6 * D // SLAB_F
WHOLE = ("mod",)


class Weights:

    def __init__(self, k, slabs, order):
        self.k, self.ready, self.used = k, [], []
        self.order = list(order) if order else None
        self.by_name = {}
        for name, src in slabs:
            self.by_name.setdefault(name, []).append(src)

    def prepare(self, name):
        k, nc = self.k, self.k.nc
        src = self.by_name[name].pop(0)
        nk, nf = src.shape[1], src.shape[2]
        raw = k.raw.take()
        view = lambda t: t[:, 0:nk * nf].rearrange("p (k f) -> p k f", k=nk)
        flat = slice(0, nk * nf)
        loaded = k.weights.start(raw.free, view(raw.ap), src)
        if name in WHOLE:
            self.ready.append((name, view(raw.ap), None, [loaded], (raw,)))
            return
        hi, lo = k.whi.take(), k.wlo.take()
        m_hi = k.a.go([loaded] + hi.free, nc.scalar.activation, hi.ap[:, flat], raw.ap[:, flat], ACT.Copy)
        m_lo = k.g.go([loaded, m_hi] + lo.free, nc.gpsimd.tensor_tensor, lo.ap[:, flat], raw.ap[:, flat],
                      hi.ap[:, flat].bitcast(F32), ALU.subtract)
        raw.free = [m_lo]
        self.ready.append((name, view(hi.ap), view(lo.ap), [m_hi, m_lo], (hi, lo)))

    def prefetch(self):
        while self.order and len(self.ready) < 2:
            self.prepare(self.order.pop(0))

    def take(self, name):
        if self.order is None:
            self.prepare(name)
        self.prefetch()
        got = self.ready.pop(0)
        assert got[0] == name, (got[0], name)
        self.used.append(name)
        return got[1:]


def products(pe, nc, out, w_hi, w_lo, x_hi, x_lo, first, last):
    nc.tensor.matmul(out, w_hi, x_hi, start=first, stop=False)
    nc.tensor.matmul(out, w_hi, x_lo, start=False, stop=False)
    return nc.tensor.matmul(out, w_lo, x_hi, start=False, stop=last)


def project(k, name, n_slabs, x_hi, x_lo, x_ready, spans, evacuate, chunk0=0, parts=None):
    nc = k.nc
    chunk = chunk0
    for s in range(n_slabs):
        w_hi, w_lo, w_ready, slots = k.w.take(name)
        nk, nf = w_hi.shape[1], w_hi.shape[2]
        for j in range(nf // P):
            cols = slice(j * P, (j + 1) * P)
            for part in parts or [(0, nk)]:
                banks = [k.banks.take() for _ in spans]
                k.pe.wait(w_ready)
                for bank in banks:
                    k.pe.wait(bank.free)
                for kk in range(*part):
                    if kk == (part[0] + part[1]) // 2:
                        yield
                    k.pe.wait(x_ready[kk])
                    for (t0, t1), bank in zip(spans, banks):
                        last = products(k.pe, nc, bank.ap[:, 0:t1 - t0], w_hi[:, kk, cols], w_lo[:, kk, cols],
                                        x_hi[:, kk, t0:t1], x_lo[:, kk, t0:t1],
                                        kk == part[0], kk == part[1] - 1)
                done = k.pe.mark(last)
                if j == nf // P - 1 and part[1] == nk:
                    for slot in slots:
                        slot.free = [done]
                yield
                args = (chunk, part[0]) if parts else (chunk,)
                freed = evacuate(*args, [(b.ap[:, 0:t1 - t0], t0, t1) for (t0, t1), b in zip(spans, banks)], done)
                for bank in banks:
                    k.banks.give(bank, freed)
            chunk += 1


def project_tokens(k, name, x_hi, x_lo, x_ready, tiles, evacuate):
    nc = k.nc
    w_hi, w_lo, w_ready, slots = k.w.take(name)
    nk, nf = w_hi.shape[1], w_hi.shape[2]
    for i, tokens in enumerate(tiles):
        bank = k.banks.take()
        k.pe.wait(w_ready + bank.free)
        for kk in range(nk):
            k.pe.wait(x_ready[kk])
            last = products(k.pe, nc, bank.ap[:, 0:nf], x_hi[:, kk, tokens], x_lo[:, kk, tokens],
                            w_hi[:, kk, :], w_lo[:, kk, :], kk == 0, kk == nk - 1)
        done = k.pe.mark(last)
        if i == len(tiles) - 1:
            for slot in slots:
                slot.free = [done]
        yield
        k.banks.give(bank, evacuate(i, bank.ap[:, 0:nf], done))


def split_into(k, after, hi, lo, value):
    m_hi = k.a.go(after, k.nc.scalar.activation, hi, value, ACT.Copy)
    m_lo = k.v.go([m_hi] + list(after), k.nc.vector.tensor_tensor, lo, value, hi.bitcast(F32), ALU.subtract)
    return [m_hi, m_lo]


def without(ring, slot):
    r = Ring([])
    r.slots = [s for s in ring.slots if s is not slot]
    return r


def inverse_rms(k, ready, chunks, spans, temps, out, out_free, width, ones=None):
    nc = k.nc
    ones = k.ones if ones is None else ones
    t0, t1 = spans[0][0], spans[-1][1]
    n = t1 - t0
    total = temps.take()
    others = without(temps, total)
    m = k.a.go(ready[0] + total.free, nc.scalar.activation, total.ap[:, 0:n], chunks[0][:, t0:t1], ACT.Square)
    for c, x in list(enumerate(chunks))[1:]:
        t = others.take()
        sq = k.a.go(ready[c] + t.free, nc.scalar.activation, t.ap[:, 0:n], x[:, t0:t1], ACT.Square)
        m = k.v.go([sq, m], nc.vector.tensor_tensor, total.ap[:, 0:n], total.ap[:, 0:n], t.ap[:, 0:n], ALU.add)
        t.free = [m]
    marks = []
    for a, b in spans:
        bank = k.banks.take()
        k.pe.wait([m, k.m_ones, k.m_pair] + bank.free)
        done = k.pe.mark(nc.tensor.matmul(bank.ap[:, 0:b - a], ones[:], total.ap[:, a - t0:b - t0], start=True, stop=True))
        total.free = [done]
        ln = k.a.go([done, k.m_eps] + out_free, nc.scalar.activation, out[:, a:b], bank.ap[:, 0:b - a], ACT.Ln,
                    scale=1.0 / width, bias=k.eps[:])
        k.banks.give(bank, [ln])
        marks.append(k.a.go([ln], nc.scalar.activation, out[:, a:b], out[:, a:b], ACT.Exp, scale=-0.5))
    return marks



def load_rows(k, src, tiles, stage, after):
    return [k.rows.start(after, stage[:, i, :], src[i * P:(i + 1) * P, :]) for i in range(tiles)]


def transpose_in(k, loaded, tiles, x, stage):
    nc = k.nc
    marks = []
    for c in range(DC):
        bank = k.banks.take()
        k.pe.wait(loaded + [k.m_ident] + bank.free)
        for i in range(tiles):
            last = nc.tensor.transpose(bank.ap[:, i * P:(i + 1) * P], stage[:, i, c * P:(c + 1) * P], k.ident[:])
        marks.append([copy_out(k, [k.pe.mark(last)], x[:, c, :], bank.ap[:, 0:tiles * P])])
        k.banks.give(bank, marks[-1])
    return marks


def norm_plain(k, x, x_ready, before, gain, hi, lo, spans, rstd, temps, out=None):
    nc = k.nc
    t0, t1 = spans[0][0], spans[-1][1]
    root = inverse_rms(k, x_ready, [x[:, c, :] for c in range(DC)], spans, temps, rstd, before, D)
    if out is not None:
        return [[k.v.go(root + k.m_vecs, nc.vector.scalar_tensor_tensor, out[:, c, t0:t1], x[:, c, t0:t1],
                        gain(c), rstd[:, t0:t1], ALU.mult, ALU.mult)] for c in range(DC)]
    marks, work = [], {}

    def normed(c):
        t = temps.take()
        n = k.v.go(root + k.m_vecs + t.free, nc.vector.scalar_tensor_tensor, t.ap[:, t0:t1], x[:, c, t0:t1],
                   gain(c), rstd[:, t0:t1], ALU.mult, ALU.mult)
        work[c] = (t, n, k.a.go([n] + before, nc.scalar.activation, hi[:, c, t0:t1], t.ap[:, t0:t1], ACT.Copy))

    def rest(c):
        t, n, m_hi = work.pop(c)
        m_lo = k.v.go([m_hi, n] + before, nc.vector.tensor_tensor, lo[:, c, t0:t1], t.ap[:, t0:t1],
                      hi[:, c, t0:t1].bitcast(F32), ALU.subtract)
        t.free = [m_hi, m_lo]
        marks.append(t.free)

    ahead(DC, normed, rest)
    return marks


def ahead(n, first, second):
    for c in range(n + 1):
        if c < n:
            first(c)
        if c:
            second(c - 1)


def by_residue(ap, dil):
    return ap.rearrange("p (l r) -> p r l", r=dil)


def mixer_a(k, l, m, qk, v, qkv_ready, o_hi, o_lo):
    nc = k.nc
    stats = m.stats
    units = [(g, i, par) for g in range(3) for i in range(ST) for par in range(2)]
    state, held, evac = {}, {}, {}

    def keys(g, i):
        return 2 * P if g == 0 and i > 0 else P

    def scores(u):
        g, i, par = u
        n = keys(g, i)
        bank = k.banks.take()
        k.pe.wait(qkv_ready + bank.free)
        for j in range(2):
            rows = slice(HD * par, HD * par + HD)
            last = nc.tensor.matmul(bank.ap[:, j * n:(j + 1) * n], qk[rows, 2 * g + j, i * P:(i + 1) * P],
                                    qk[rows, 6 + 2 * g + j, (i + 1) * P - n:(i + 1) * P], start=True, stop=True)
        done = k.pe.mark(last)
        sb = m.probs.take()
        dist = k.dist[g]
        off = 2 * P - n if g == 0 else 0
        for j in range(2):
            slope = SLOPES[GH * g + 2 * j + par]
            last = k.v.go([done, k.m_dist[g]] + sb.free, nc.vector.scalar_tensor_tensor, sb.ap[:, j * n:(j + 1) * n],
                          dist[:, off:off + n], slope, bank.ap[:, j * n:(j + 1) * n], ALU.mult, ALU.add)
        k.banks.give(bank, [last])
        both = sb.ap[:, 0:2 * n].rearrange("p (j n) -> p j n", j=2)
        neg = stats[:, 0, g, i, par:par + 3:2]
        negmax = k.v.go([last], nc.vector.tensor_reduce, neg, both, AX.X, ALU.max, negate=True)
        for j in range(2):
            h = par + 2 * j
            e = k.a.go([negmax], nc.scalar.activation, both[:, j, :], both[:, j, :], ACT.Exp,
                       bias=stats[:, 0, g, i, h:h + 1], accum_out=stats[:, 1, g, i, h:h + 1])
        state[u] = (sb, e)

    def turn(u):
        g, i, par = u
        n = keys(g, i)
        sb, e = state[u]
        bank = k.banks.take()
        k.pe.wait([e, k.m_ident] + bank.free)
        for b in range(2 * n // P):
            last = nc.tensor.transpose(bank.ap[:, b * P:(b + 1) * P], sb.ap[:, b * P:(b + 1) * P], k.ident[:])
        done = k.pe.mark(last)
        sb.free = [done]
        pt = m.turned.take()
        copied = copy_out(k, [done] + pt.free, pt.ap[:, 0:2 * n], bank.ap[:, 0:2 * n])
        k.banks.give(bank, [copied])
        state[u] = (pt, copied)

    def values(u):
        g, i, par = u
        n = keys(g, i)
        pt, copied = state.pop(u)
        for j in range(2):
            if (g, j) not in held:
                held[g, j] = k.banks.take()
            bank = held[g, j]
            k.pe.wait([copied] + qkv_ready + bank.free)
            h = par + 2 * j
            for b in range(n // P):
                tile = i - (n // P - 1) + b
                last = nc.tensor.matmul(bank.ap[HD * par:HD * par + HD, i * P:(i + 1) * P],
                                        v[:, tile, g * 256 + h * HD:g * 256 + (h + 1) * HD],
                                        pt.ap[:, j * n + b * P:j * n + (b + 1) * P],
                                        start=b == 0, stop=b == n // P - 1)
        done = k.pe.mark(last)
        pt.free = [done]
        if i == ST - 1 and par == 1:
            dil = ORDER[g]
            for j in range(2):
                bank = held[g, j]
                src = bank.ap[:, :] if dil == 1 else bank.ap[:, :].rearrange("p (r l) -> p l r", r=dil)
                dst = m.oa[:, g, j, :] if dil == 1 else m.oa[:, g, j, :].rearrange("p (l r) -> p l r", r=dil)
                evac[g, j] = copy_out(k, [done] + m.start, dst, src)
                k.banks.give(bank, [evac[g, j]])

    yield from pipeline(units, [scores, turn, values])
    m.evacuated, m.stats_ready = evac, [k.a.now(), k.v.now()]


def mixture(k, m, o_hi, o_lo):
    nc = k.nc
    stats, evac = m.stats, m.evacuated
    def spread(which, g, c):
        bank = k.banks.take()
        k.pe.wait(bank.free + m.stats_ready)
        for i in range(ST):
            for j in range(2):
                col = stats[:, which, g, i, 2 * c + j:2 * c + j + 1].broadcast_to([P, HD])
                last = nc.tensor.matmul(bank.ap[HD * j:HD * j + HD, i * P:(i + 1) * P], col, k.ident[:],
                                        start=True, stop=True)
        dil = ORDER[g]
        src = bank.ap[:, :] if dil == 1 else bank.ap[:, :].rearrange("p (r l) -> p l r", r=dil)
        return bank, src, [k.pe.mark(last)]

    def natural(t, dil):
        return t if dil == 1 else t.rearrange("p (l r) -> p l r", r=dil)

    mix = Ring(m.mix_buffers)
    for slot in mix.slots:
        slot.free = now(k)
    for c in range(2):
        n = [mix.take() for _ in range(3)]
        marks = []
        for g in range(3):
            bank, src, done = spread(0, g, c)
            marks.append(k.a.go(done + n[g].free, nc.scalar.activation, natural(n[g].ap[:, 0:S], ORDER[g]), src, ACT.Copy))
            k.banks.give(bank, marks[-1:])
        least = mix.take()
        t = k.v.go(marks + least.free, nc.vector.tensor_tensor, least.ap[:, 0:S], n[0].ap[:, 0:S], n[1].ap[:, 0:S], ALU.min)
        t = k.v.go([t], nc.vector.tensor_tensor, least.ap[:, 0:S], least.ap[:, 0:S], n[2].ap[:, 0:S], ALU.min)
        total = mix.take()
        for g in range(3):
            t1 = k.g.go([t], nc.gpsimd.tensor_tensor, n[g].ap[:, 0:S], least.ap[:, 0:S], n[g].ap[:, 0:S], ALU.subtract)
            e = k.a.go([t1], nc.scalar.activation, n[g].ap[:, 0:S], n[g].ap[:, 0:S], ACT.Exp)
            bank, src, done = spread(1, g, c)
            den = mix.take() if g else total
            mul = k.v.go([e] + done + den.free, nc.vector.tensor_tensor, natural(den.ap[:, 0:S], ORDER[g]),
                         natural(n[g].ap[:, 0:S], ORDER[g]), src, ALU.mult)
            k.banks.give(bank, [mul])
            if g:
                mul = k.v.go([mul], nc.vector.tensor_tensor, total.ap[:, 0:S], total.ap[:, 0:S], den.ap[:, 0:S], ALU.add)
                den.free = [mul]
            yield
        r = k.v.go([mul], nc.vector.reciprocal, total.ap[:, 0:S], total.ap[:, 0:S])
        for g in range(3):
            p = k.g.go([e, mul, evac[g, c]], nc.gpsimd.tensor_tensor, n[g].ap[:, 0:S], n[g].ap[:, 0:S], m.oa[:, g, c, :], ALU.mult)
        s1 = k.g.go([p], nc.gpsimd.tensor_tensor, n[0].ap[:, 0:S], n[0].ap[:, 0:S], n[1].ap[:, 0:S], ALU.add)
        s2 = k.g.go([s1], nc.gpsimd.tensor_tensor, n[0].ap[:, 0:S], n[0].ap[:, 0:S], n[2].ap[:, 0:S], ALU.add)
        f = k.v.go([s2, r], nc.vector.tensor_tensor, least.ap[:, 0:S], n[0].ap[:, 0:S], total.ap[:, 0:S], ALU.mult)
        marks = split_into(k, [f] + m.start, o_hi[:, c, :], o_lo[:, c, :], least.ap[:, 0:S])
        for slot in n + [least, total]:
            slot.free = marks + [f]
        m.done[c] = marks
        yield


def mixer_b(k, l, m, qk, v, qkv_ready, o_hi, o_lo):
    nc = k.nc
    units = [(c, i, par) for c in range(2) for i in range(ST) for par in range(2)]
    state, held = {}, {}

    def scores(u):
        c, i, par = u
        n = (i + 1) * P
        bank = k.banks.take()
        rows = slice(HD * par, HD * par + HD)
        k.pe.wait(qkv_ready + bank.free)
        done = k.pe.mark(nc.tensor.matmul(bank.ap[:, 0:n], qk[rows, 12 + c, i * P:n], qk[rows, 14 + c, 0:n],
                                          start=True, stop=True))
        z, sp = m.stick.take(), m.stick.take()
        t = k.v.go([done] + z.free, nc.vector.tensor_copy, z.ap[:, 0:n], bank.ap[:, 0:n])
        k.banks.give(bank, [t])
        t = k.a.go([t] + sp.free, nc.scalar.activation, sp.ap[:, 0:n], z.ap[:, 0:n], ACT.Abs)
        t = k.a.go([t], nc.scalar.activation, sp.ap[:, 0:n], sp.ap[:, 0:n], ACT.Exp, scale=-1.0)
        t = k.a.go([t], nc.scalar.activation, sp.ap[:, 0:n], sp.ap[:, 0:n], ACT.Ln, bias=1.0)
        state[u] = (z, sp, t)

    def sums(u):
        c, i, par = u
        n = (i + 1) * P
        z, sp, t = state[u]
        own = slice(i * P, n)
        t = k.v.go([t], nc.vector.scalar_tensor_tensor, sp.ap[:, 0:n], z.ap[:, 0:n], 0.0, sp.ap[:, 0:n], ALU.max, ALU.add)
        t = k.v.go([t, k.m_causal], nc.vector.tensor_tensor, sp.ap[:, own], sp.ap[:, own], k.causal[:], ALU.mult)
        neg = k.g.go([t, k.m_causal_neg], nc.gpsimd.tensor_tensor, z.ap[:, own], z.ap[:, own], k.causal_neg[:], ALU.add)
        back = sp.ap[:, n - 1::-1] if n == S else sp.ap[:, 0:n][:, ::-1]
        t = k.v.go([t, k.m_zeros], nc.vector.tensor_tensor_scan, back, back, k.zeros[:, 0:1].broadcast_to([P, n]), 0.0,
                   ALU.add, ALU.add)
        t = k.v.go([t, neg], nc.vector.tensor_tensor, z.ap[:, 0:n], z.ap[:, 0:n], sp.ap[:, 0:n], ALU.subtract)
        sp.free = [t]
        t = k.a.go([t], nc.scalar.activation, z.ap[:, 0:n], z.ap[:, 0:n], ACT.Exp)
        state[u] = (z, t)

    def turn(u):
        c, i, par = u
        z, t = state[u]
        bank = k.banks.take()
        k.pe.wait([t, k.m_ident] + bank.free)
        for b in range(i + 1):
            last = nc.tensor.transpose(bank.ap[:, b * P:(b + 1) * P], z.ap[:, b * P:(b + 1) * P], k.ident[:])
        done = k.pe.mark(last)
        z.free = [done]
        pt = m.turned.take()
        copied = copy_out(k, [done] + pt.free, pt.ap[:, 0:(i + 1) * P], bank.ap[:, 0:(i + 1) * P])
        k.banks.give(bank, [copied])
        state[u] = (pt, copied)

    def values(u):
        c, i, par = u
        pt, copied = state.pop(u)
        if c not in held:
            held[c] = k.banks.take()
        bank = held[c]
        k.pe.wait([copied] + qkv_ready + bank.free)
        col = 3 * 256 + (2 * c + par) * HD
        for b in range(i + 1):
            last = nc.tensor.matmul(bank.ap[HD * par:HD * par + HD, i * P:(i + 1) * P], v[:, b, col:col + HD],
                                    pt.ap[:, b * P:(b + 1) * P], start=b == 0, stop=b == i)
        done = k.pe.mark(last)
        pt.free = [done]
        if i == ST - 1 and par == 1:
            marks = split_into(k, [done] + m.start, o_hi[:, 2 + c, :], o_lo[:, 2 + c, :], bank.ap[:, :])
            k.banks.give(bank, marks)
            m.done[2 + c] = marks

    yield from pipeline(units, [scores, sums, lambda u: None, turn, values])


SPAN1 = [(0, S)]


def slab_list(out, name, w, r0, nr, c0, n, step=SLAB_F):
    for c in range(c0, c0 + n, step):
        f = min(step, c0 + n - c)
        out.append((name, w[r0:r0 + nr, c:c + f].rearrange("(k p) f -> p k f", p=P)))


def first_slabs(ins):
    out = []
    for l in range(DEPTH):
        w = ins["w_in"][l]
        slab_list(out, "qk_a", w, 0, D, 0, 2 * W_A)
        slab_list(out, "v_a", w, 0, D, 2 * W_A, W_A)
        slab_list(out, "qk_b", w, 0, D, 3 * W_A, 2 * W_B)
        slab_list(out, "v_b", w, 0, D, 3 * W_A + 2 * W_B, W_B)
        slab_list(out, "gate_a", w, 0, D, GATE0, D)
        slab_list(out, "gate_b", w, 0, D, GATE0 + D, D)
        slab_list(out, "branch", ins["w_br"][l], 0, 2 * W_B, 0, D)
        slab_list(out, "w_o", ins["w_o"][l], 0, D, 0, D)
        for c0, n in FF_PARTS1:
            slab_list(out, "up_a", ins["w_up"][l], 0, D, c0 * P, n * P)
            slab_list(out, "up_v", ins["w_up"][l], 0, D, FF + c0 * P, n * P)
            slab_list(out, "down", ins["w_down"][l], c0 * P, n * P, 0, D)
    return out


FF_PARTS1 = [(0, 8), (8, 8), (16, 6)]


def add_to(k, x, marks):
    def evacuate(chunk, banks, done):
        src, t0, t1 = banks[0]
        marks[chunk] = [k.v.go([done], k.nc.vector.tensor_tensor, x[:, chunk, t0:t1], x[:, chunk, t0:t1], src, ALU.add)]
        return marks[chunk]
    return evacuate


def fresh(aps, free):
    r = Ring(aps)
    for s in r.slots:
        s.free = list(free)
    return r


def first_layer(k, l, x, spare, x_ready, before):
    nc = k.nc
    m = Core()
    tag = f"a{l}_"
    h = place(k, tag + "h", AT_H, [2, DC, S], F32R)
    o = place(k, tag + "o", AT_H + 32, [2, 4, S], F32R)
    qk = place(k, tag + "qk", AT_WORK, [16, S])
    v = place(k, tag + "v", AT_WORK + 32, [ST, W_A + W_B])
    m.oa = place(k, tag + "oa", AT_WORK + 48, [3, 2, S])
    temps = [place(k, f"{tag}t{i}", AT_WORK + 60 + 2 * i, [S]) for i in range(8)]
    m.stats = place(k, tag + "stats", AT_WORK + 76, [2, 3, ST, GH])
    rstd = temps[7]

    h_ready = norm_plain(k, x, x_ready, before, lambda c: k.vec("norm1", DC * l + c), h[:, 0], h[:, 1], SPAN1, rstd,
                         fresh(temps[3:6], before))
    start = now(k)
    if l == 0:
        second_set_up(k)

    def keep_qk(chunk, banks, done):
        src = banks[0][0]
        dst = qk[:, chunk, :]
        query = chunk < 6 or chunk in (12, 13)
        dil = ORDER[chunk % 6 // 2] if chunk < 12 else 1
        if dil > 1:
            src, dst = by_residue(src, dil), dst.rearrange("p (r l) -> p r l", r=dil)
        return [copy_out(k, [done] + start, dst, src, HD ** -0.5 if query else None)]

    def keep_v(g):
        def evacuate(i, src, done):
            return [copy_out(k, [done] + start, v[:, i, g * 256:(g + 1) * 256], src)]
        return evacuate

    def project_v(name, g):
        dil = ORDER[g] if g < 3 else 1
        tiles = [slice(i * P, (i + 1) * P) if dil == 1 else slice(i, S, dil) for i in range(ST)]
        return project_tokens(k, name, h[:, 0], h[:, 1], h_ready, tiles, keep_v(g))

    def project_a():
        yield from project(k, "qk_a", 6, h[:, 0], h[:, 1], h_ready, SPAN1, keep_qk)
        for g in range(3):
            yield from project_v("v_a", g)

    for _ in project(k, "qk_b", 2, h[:, 0], h[:, 1], h_ready, SPAN1, keep_qk, 12):
        pass
    for _ in project_v("v_b", 3):
        pass
    m.start, m.done = start, [None] * 4
    m.stick = fresh(temps[0:6], now(k))
    m.turned = fresh(temps[6:8], now(k))
    for _ in weave(mixer_b(k, l, m, qk, v, [k.a.now(), k.v.now()], o[:, 0], o[:, 1]), project_a(), 1.8):
        pass

    gates = [None] * (2 * DC)
    gate_ready = {}

    def gate(base, buffers, after):
        def evacuate(chunk, banks, done):
            gates[base + chunk] = buffers[chunk]
            src = banks[0][0]
            if len(buffers[chunk].shape) == 3:
                src = src.rearrange("p (a b) -> p a b", a=2)
            gate_ready[base + chunk] = k.a.go([done] + k.m_vecs + after, nc.scalar.activation, buffers[chunk], src,
                                              ACT.Sigmoid, bias=k.vec("b_gate", 16 * l + base + chunk))
            return [gate_ready[base + chunk]]
        return evacuate

    def gates_a(after, rows):
        buffers = [qk[:, 12 + c, :] for c in range(4)] + [spare[:, 2 * c:2 * c + 2, :] for c in range(4)]
        for s in range(4):
            yield from project(k, "gate_a", 1, h[:, 0], h[:, 1], h_ready, SPAN1, gate(0, buffers, after), 2 * s)
            yield from k.modulation.steps(MOD_SLABS // 8, rows)

    def gates_b(after):
        buffers = [qk[:, c, :] for c in range(DC)]
        yield from project(k, "gate_b", 4, h[:, 0], h[:, 1], h_ready, SPAN1, gate(DC, buffers, after))

    m.probs = fresh(temps[0:3], now(k))
    m.turned = fresh(temps[3:6], now(k))
    m.mix_buffers = temps[0:8]
    mod_rows = fresh([temps[6][:, 0:SLAB_F], temps[6][:, SLAB_F:2 * SLAB_F]], now(k))
    for _ in weave(mixer_a(k, l, m, qk, v, [k.a.now(), k.v.now()], o[:, 0], o[:, 1]),
                   gates_a(now(k), mod_rows), 28 / 26):
        pass
    for _ in weave(mixture(k, m, o[:, 0], o[:, 1]), gates_b(now(k)), 2.0):
        pass

    attended = now(k)
    merged = place(k, tag + "merged", AT_WORK + 32, [2, DC, S], F32R)
    branch = fresh([place(k, f"{tag}br{i}", AT_WORK + 64 + 2 * i, [S]) for i in range(4)], attended)
    half, merged_ready = {}, [None] * DC

    def merge(chunk, part, banks, done):
        i = chunk if part == 0 else DC + chunk
        t = branch.take()
        g, src, dst = gates[i], banks[0][0], t.ap[:]
        if len(g.shape) == 3:
            src, dst = src.rearrange("p (a b) -> p a b", a=2), dst.rearrange("p (a b) -> p a b", a=2)
        mark = k.v.go([done, gate_ready[i]] + t.free, nc.vector.tensor_tensor, dst, src, g, ALU.mult)
        if part == 0:
            half[chunk] = t
            return [mark]
        a = half.pop(chunk)
        total = k.v.go([mark], nc.vector.tensor_tensor, a.ap[:], a.ap[:], t.ap[:], ALU.add)
        t.free = [total]
        a.free = merged_ready[chunk] = split_into(k, [total] + attended, merged[:, 0, chunk, :], merged[:, 1, chunk, :],
                                                  a.ap[:])
        return [mark]

    for _ in project(k, "branch", 4, o[:, 0], o[:, 1], m.done, SPAN1, merge, parts=[(0, 2), (2, 4)]):
        pass
    added = [None] * DC
    before = now(k)
    for _ in project(k, "w_o", 4, merged[:, 0], merged[:, 1], merged_ready, SPAN1, add_to(k, x, added)):
        pass

    h_ready = norm_plain(k, x, added, before, lambda c: k.vec("norm2", DC * l + c), h[:, 0], h[:, 1], SPAN1, rstd,
                         fresh(temps[3:6], before))
    mixed = now(k)
    hidden = place(k, tag + "hidden", AT_WORK, [2, 8, S], F32R)
    conv = fresh([place(k, f"{tag}cv{i}", AT_WORK + 32 + 2 * i, [S]) for i in range(6)], mixed)
    acts = {}
    hidden_ready, hidden_free = [None] * 8, mixed

    def tap(i, c):
        return k.vec("conv_w", (3 * l + i) * FC + c)

    def up_a(chunk, banks, done):
        src, c = banks[0][0], conv.take()
        t = k.a.go([done] + k.m_vecs + c.free, nc.scalar.activation, c.ap[:], src, ACT.Identity, scale=tap(2, chunk),
                   bias=k.vec("conv_b", FC * l + chunk))
        t = k.v.go([t], nc.vector.scalar_tensor_tensor, c.ap[:, 1:S], src[:, 0:S - 1], tap(1, chunk), c.ap[:, 1:S],
                   ALU.mult, ALU.add)
        t = k.v.go([t], nc.vector.scalar_tensor_tensor, c.ap[:, 2:S], src[:, 0:S - 2], tap(0, chunk), c.ap[:, 2:S],
                   ALU.mult, ALU.add)
        acts[chunk] = (c, k.a.go([t], nc.scalar.activation, c.ap[:], c.ap[:], ACT.Gelu))
        return [t]

    def up_v(c0):
        def evacuate(chunk, banks, done):
            c, t = acts.pop(chunk)
            t = k.v.go([done, t], nc.vector.tensor_tensor, c.ap[:], c.ap[:], banks[0][0], ALU.mult)
            c.free = split_into(k, [t] + hidden_free, hidden[:, 0, chunk - c0, :], hidden[:, 1, chunk - c0, :], c.ap[:])
            hidden_ready[chunk - c0] = c.free
            return [t]
        return evacuate

    for c0, n in FF_PARTS1:
        for c in range(0, n, 2):
            for _ in project(k, "up_a", 1, h[:, 0], h[:, 1], h_ready, SPAN1, up_a, c0 + c):
                pass
            for _ in project(k, "up_v", 1, h[:, 0], h[:, 1], h_ready, SPAN1, up_v(c0), c0 + c):
                pass
        before = now(k)
        for _ in project(k, "down", 4, hidden[:, 0], hidden[:, 1], hidden_ready, SPAN1, add_to(k, x, added)):
            pass
        hidden_free = [k.pe.now()]
    return added, before



def transpose_out(k, x, ready, out):
    nc = k.nc
    stage = place(k, "out_rows", AT_WORK + 33, [ST, D])
    before = now(k)
    stored = []
    for i in range(ST):
        marks = []
        for half in range(2):
            bank = k.banks.take()
            for c in range(4):
                k.pe.wait(ready[4 * half + c])
            k.pe.wait(bank.free)
            for c in range(4):
                last = nc.tensor.transpose(bank.ap[:, c * P:(c + 1) * P], x[:, 4 * half + c, i * P:(i + 1) * P], k.ident[:])
            marks.append(copy_out(k, [k.pe.mark(last)] + before, stage[:, i, half * 512:(half + 1) * 512], bank.ap[:, :]))
            k.banks.give(bank, marks[-1:])
        stored.append(k.stores.start(marks, out[i * P:(i + 1) * P, :], stage[:, i, :]))
    k.sp.wait(stored)




IN2 = {"q": 0, "v": 512, "g": 1024, "f": 1536, "b": 2048, "dq": 2560, "dk": 2816, "dv": 3072, "ft": 3328}
FF_PARTS2 = [(0, 6), (6, 6), (12, 5), (17, 5)]
LAT, CTXS = (0, S), (S, T2)


def modulation_slabs(ins):
    out = []
    for l in range(DEPTH):
        slab_list(out, "mod", ins["w_mod_2"][l], 0, D, 0, 6 * D)
    return out


def second_slabs(ins):
    out = []
    for l in range(DEPTH):
        w = ins["w_in_2"][l]
        for name in ("ft", "dq", "dk", "dv"):
            slab_list(out, name, w, 0, D, IN2[name], 256)
        for name in ("q", "v", "f", "b", "g"):
            slab_list(out, name, w, 0, D, IN2[name], HGH * P, step=P)
        slab_list(out, "w_out", ins["w_out_2"][l], 0, D, 0, D)
        for c0, n in FF_PARTS2:
            slab_list(out, "ff_g", ins["w_ffn_in_2"][l], 0, D, c0 * P, n * P)
            slab_list(out, "ff_u", ins["w_ffn_in_2"][l], 0, D, FF + c0 * P, n * P)
            slab_list(out, "ff_out", ins["w_ffn_out_2"][l], c0 * P, n * P, 0, D)
    return out


def second_set_up(k):
    nc, ins = k.nc, k.ins
    v, a = nc.vector, nc.scalar

    def small(name, shape, dtype=F32):
        return nc.alloc_sbuf_tensor(name, [P] + shape, dtype)

    k.cond = small("cond", [DC, 2])
    sig = small("cond_sigmoid", [DC, 2])
    for j, name in enumerate(("c", "c_ctx")):
        t = k.a.go(k.m_vecs, a.activation, sig[:, :, j], k.vec(name, 0, DC), ACT.Sigmoid)
        t = k.v.go([t], v.tensor_tensor, k.cond[:, :, j], sig[:, :, j], k.vec(name, 0, DC), ALU.mult)
    k.modulation = Modulation(k)
    k.m_cond = [t]
    k.mod = [small(f"mod{l}", [6 * DC, 2]) for l in range(DEPTH)]

    lo = small("lb_logits_e", [2, DEPTH, HGH])
    k.lb, k.lb1 = small("lower_bound", [DEPTH, 2, HGH]), small("one_less_bound", [DEPTH, 2, HGH])
    mx, den = small("lb_max", [2, HGH]), small("lb_den", [2, HGH])
    logits = k.vec("lb", 0, 2 * DEPTH * HGH).rearrange("p (d l c) -> p d l c", d=2, l=DEPTH)
    t = k.v.go(k.m_vecs, v.tensor_tensor, mx[:], logits[:, :, 0, :], logits[:, :, 1, :], ALU.max)
    for l in range(DEPTH):
        u = k.v.go([t], v.tensor_tensor, lo[:, :, l, :], logits[:, :, l, :], mx[:], ALU.subtract)
    u = k.a.go([u], a.activation, lo[:], lo[:], ACT.Exp)
    t = k.v.go([u], v.tensor_tensor, den[:], lo[:, :, 0, :], lo[:, :, 1, :], ALU.add)
    t = k.v.go([t], v.reciprocal, den[:], den[:])
    for l in range(DEPTH):
        u = k.v.go([t], v.tensor_tensor, lo[:, :, l, :], lo[:, :, l, :], den[:], ALU.mult)
    t = k.v.go([u], v.tensor_tensor, mx[:], lo[:, :, 0, :], lo[:, :, 1, :], ALU.add)
    t0 = k.v.go([t], v.tensor_tensor, k.lb[:, 0], lo[:, :, 0, :], lo[:, :, 0, :], ALU.subtract)
    t1 = k.v.go([t], v.tensor_tensor, k.lb[:, 1], mx[:], lo[:, :, 0, :], ALU.subtract)
    k.m_lb = [k.v.go([t0, t1], v.tensor_scalar, k.lb1[:], k.lb[:], -1.0, 1.0, ALU.mult, ALU.add)]

    dl = place(k, "da_lambda", AT_WORK + 70, [DEPTH, 4, 32])
    loaded = k.loads.start([], dl[:], ins["da_lambda_2"].rearrange("l n d -> (l n d)").partition_broadcast(P))
    prod, sums, lam = place(k, "lambda_prod", AT_WORK + 71, [DEPTH, 2, 32]), small("lambda_sum", [DEPTH, 2]), small("minus_lambda", [DEPTH])
    t = k.v.go([loaded], v.tensor_tensor, prod[:], dl[:, :, 0::2, :], dl[:, :, 1::2, :], ALU.mult)
    t = k.v.go([t], v.tensor_reduce, sums[:], prod[:], AX.X, ALU.add)
    t = k.a.go([t], a.activation, sums[:], sums[:], ACT.Exp)
    k.sub = small("subln_gain", [DEPTH])
    for l in range(DEPTH):
        init = lambda_init(l)
        u = k.v.go([t], v.scalar_tensor_tensor, lam[:, l:l + 1], sums[:, l, 1:2], -init, sums[:, l, 0:1], ALU.add, ALU.subtract)
        u = k.v.go(k.m_vecs, v.tensor_scalar, k.sub[:, l:l + 1], k.vec("subln", l), 1.0 - init, None, ALU.mult)
    k.neg_lam, k.m_lam = lam, [u]

    k.resets = nc.alloc_sbuf_tensor("resets", [P, T2 + 1], mybir.dt.bfloat16)
    t = k.v.go([], v.memset, k.resets[:], 1.0)
    k.m_resets = [k.v.go([t], v.memset, k.resets[:, 0:T2 + 1:P], 0.0)]
    k.decays = small("tile_decays", [ST + CT])
    k.gains = [[small(f"gain{l}_{i}", [DC, 2]) for i in range(4)] for l in range(DEPTH)]


def lambda_init(l):
    return 0.8 - 0.6 * math.exp(-0.3 * l)


class Modulation:

    def __init__(self, k):
        self.k, self.at = k, 0

    def columns(self, row, ready):
        k, nc, (l, s) = self.k, self.k.nc, divmod(self.at, MOD_SLABS)
        bank = k.banks.take()
        k.pe.wait([ready] + bank.free)
        for j in range(2):
            last = nc.tensor.transpose(bank.ap[:, 2 * j:2 * j + 2], row.ap[0:2, j * P:(j + 1) * P], k.ident[0:2, 0:2])
        done = k.pe.mark(last)
        row.free = [done]
        bias = k.vec("b_mod", 6 * DC * l + 2 * s, 2).unsqueeze(2).broadcast_to([P, 2, 2])
        t = k.v.go([done] + k.m_vecs, nc.vector.tensor_tensor, k.mod[l][:, 2 * s:2 * s + 2, :],
                   bank.ap[:, 0:4].rearrange("p (j n) -> p j n", j=2), bias, ALU.add)
        k.banks.give(bank, [t])
        if s == MOD_SLABS - 1:
            for i, (m, add) in enumerate(((1, 1.0), (2, 0.0), (4, 1.0), (5, 0.0))):
                for j in range(2):
                    k.m_gain = k.v.go([t], nc.vector.scalar_tensor_tensor, k.gains[l][i][:, :, j],
                                      k.mod[l][:, m * DC:(m + 1) * DC, j], add, k.vec("norm_g", (4 * l + i) * DC, DC),
                                      ALU.add, ALU.mult)
        self.at += 1

    def steps(self, n, row_buffers):
        k, nc = self.k, self.k.nc
        pending = None
        for _ in range(n):
            w, _, ready, slots = k.w.take("mod")
            bank = k.banks.take()
            k.pe.wait(ready + k.m_cond + bank.free)
            for kk in range(DC):
                last = nc.tensor.matmul(bank.ap[0:2, 0:SLAB_F], k.cond[:, kk, :], w[:, kk, :],
                                        start=kk == 0, stop=kk == DC - 1)
            done = k.pe.mark(last)
            for slot in slots:
                slot.free = [done]
            if pending:
                self.columns(*pending)
            yield
            row = row_buffers.take()
            copied = k.v.go([done] + row.free, nc.vector.tensor_copy, row.ap[0:2, :], bank.ap[0:2, 0:SLAB_F])
            k.banks.give(bank, [copied])
            pending = (row, copied)
        self.columns(*pending)


def adaln(k, l, which, x, x_ready, before, hi, lo, sides, rstd, temps):
    nc = k.nc
    spans = [LAT, CTXS][0:sides]
    root = inverse_rms(k, x_ready, [x[:, c, :] for c in range(DC)], spans, temps, rstd, before, D)
    gain, shift = k.gains[l][2 * which], 3 * DC * which
    marks, work = [], {}

    def normed(c):
        t = temps.take()
        work[c] = [t, []]
        for j, (a, b) in enumerate(spans):
            n = k.v.go(root + t.free + [k.m_gain], nc.vector.scalar_tensor_tensor, t.ap[:, a:b], x[:, c, a:b],
                       gain[:, c, j:j + 1], rstd[:, a:b], ALU.mult, ALU.mult)
            work[c][1] += [n, k.a.go([n] + before, nc.scalar.activation, hi[:, c, a:b], t.ap[:, a:b], ACT.Identity,
                                     bias=k.mod[l][:, shift + c, j:j + 1])]

    def rest(c):
        t, done = work.pop(c)
        for j, (a, b) in enumerate(spans):
            m_lo = k.v.go(done + before, nc.vector.scalar_tensor_tensor, lo[:, c, a:b], t.ap[:, a:b],
                          k.mod[l][:, shift + c, j:j + 1], hi[:, c, a:b].bitcast(F32), ALU.add, ALU.subtract)
        t.free = done + [m_lo]
        marks.append(t.free)

    ahead(DC, normed, rest)
    return marks


def add_normed(k, l, which, x, y, y_ready, before, sides, rstd, temps):
    nc = k.nc
    spans = [LAT, CTXS][0:sides]
    root = inverse_rms(k, y_ready, [y[:, c, :] for c in range(DC)], spans, temps, rstd, before, D)
    gain = k.gains[l][2 * which + 1]
    marks, work = [], {}
    end = spans[-1][1]

    def normed(c):
        for j, (a, b) in enumerate(spans):
            work[c] = k.v.go(root + y_ready[c], nc.vector.scalar_tensor_tensor, y[:, c, a:b], y[:, c, a:b],
                             gain[:, c, j:j + 1], rstd[:, a:b], ALU.mult, ALU.mult)

    def added(c):
        stream, op = (k.g, nc.gpsimd.tensor_tensor) if c % 2 else (k.v, nc.vector.tensor_tensor)
        marks.append([stream.go([work.pop(c)], op, x[:, c, 0:end], x[:, c, 0:end], y[:, c, 0:end], ALU.add)])

    ahead(DC, normed, added)
    return marks


def fourier_matrices(k, l):
    tag, start = f"b{l}_", now(k)
    m = Core()
    m.dl = place(k, tag + "dftl", AT_WORK + 42, [2, ST, S])
    m.dc = place(k, tag + "dftc", AT_WORK + 58, [2, CT, CTX])
    m.d64 = place(k, tag + "dft64", AT_WORK + 62, [2, P])
    m.m_64 = k.rows.start(start, m.d64[:], k.ins["c_dft64"])
    m.m_dl = k.rows.start(start, m.dl[:], k.ins["c_dftl"])
    m.m_dc = k.rows.start(start, m.dc[:], k.ins["c_dftc"])
    return m


def fourier(k, l, h, h_ready, y, start, sides, mats):
    nc = k.nc
    tag = f"b{l}_"
    u = place(k, tag + "u", AT_WORK + 24, [2, T2])
    half = place(k, tag + "half", AT_WORK + 30, [ST + CT, 2, 2, P])
    dl, dc, dft64, m_dl, m_dc, m_64 = mats.dl, mats.dc, mats.d64, mats.m_dl, mats.m_dc, mats.m_64
    spans = [LAT, CTXS][0:sides]
    ready = []

    def keep(chunk, banks, done):
        ready[:] = ready[-2:] + [copy_out(k, [done] + start, u[:, chunk, a:b], src) for src, a, b in banks]
        return ready[-len(banks):]

    yield from project(k, "ft", 1, h[:, 0], h[:, 1], h_ready, spans, keep)
    ready = [k.a.now(), k.v.now()]
    tiles = ST + CT if sides == 2 else ST
    for i in range(tiles):
        bank = k.banks.take()
        k.pe.wait(ready + [m_64] + bank.free)
        for c in range(2):
            last = nc.tensor.matmul(bank.ap[:, 256 * c:256 * c + 256], u[:, c, i * P:(i + 1) * P],
                                    dft64[:].rearrange("p s f -> p (s f)"), start=True, stop=True)
        mark = copy_out(k, [k.pe.mark(last)] + start, half[:, i].rearrange("p c s f -> p (c s f)"), bank.ap[:, :])
        k.banks.give(bank, [mark])
    ready = [k.a.now(), k.v.now()]
    for c in range(2):
        for (a, b), mat, m_mat, i0, n in ((LAT, dl, m_dl, 0, ST), (CTXS, dc, m_dc, ST, CT))[0:sides]:
            bank = k.banks.take()
            k.pe.wait(ready + [m_mat] + bank.free)
            for i in range(n):
                for s in range(2):
                    last = nc.tensor.matmul(bank.ap[:, 0:b - a], half[:, i0 + i, c, s, :], mat[:, s, i, :],
                                            start=i + s == 0, stop=i == n - 1 and s == 1)
            mark = copy_out(k, [k.pe.mark(last)] + start, y[:, 6 + c, a:b], bank.ap[:, 0:b - a])
            k.banks.give(bank, [mark])
        yield


def diff_attention(k, l, h, h_ready, y, sides):
    nc = k.nc
    tag = f"b{l}_"
    start = now(k)
    at = AT_WORK + 39
    dq, dk = place(k, tag + "dq", at, [2, T2]), place(k, tag + "dk", at + 6, [2, T2])
    dv = place(k, tag + "dv", at + 12, [ST + CT, 256])
    cos, sin = place(k, tag + "cos", at + 18, [S]), place(k, tag + "sin", at + 20, [S])
    probs = Ring([place(k, f"{tag}p{i}", AT_WORK + 6 * i, [2, T2]) for i in range(2)])
    turned = Ring([place(k, f"{tag}pt{i}", at + 22 + 3 * i, [ST + CT, P]) for i in range(2)])
    temps = Ring([place(k, f"{tag}dt{i}", at + 28 + 3 * i, [T2]) for i in range(2)])
    stats = Ring([place(k, f"{tag}ds{i}", at + 34 + 0.5 * i, [16]) for i in range(4)])
    for r in (probs, turned, temps, stats):
        for slot in r.slots:
            slot.free = start
    rot = place(k, tag + "rot", at + 36, [P])
    m_cos, m_sin = k.rows.start(start, cos[:], k.ins["c_cos"]), k.rows.start(start, sin[:], k.ins["c_sin"])
    m_rot = k.rows.start(start, rot[:], k.ins["c_rot"])
    scale = 32 ** -0.5

    def keep(dst, spans):
        def evacuate(chunk, banks, done):
            marks = [copy_out(k, [done] + start, dst[:, chunk, a:b], src) for src, a, b in banks]
            bank = k.banks.take()
            k.pe.wait(marks[0:1] + [m_rot] + bank.free)
            done = k.pe.mark(nc.tensor.matmul(bank.ap[:, :], rot[:], dst[:, chunk, 0:S], start=True, stop=True))
            t = temps.take()
            m1 = k.v.go([done, m_sin] + t.free, nc.vector.tensor_tensor, t.ap[:, 0:S], bank.ap[:, :], sin[:], ALU.mult)
            k.banks.give(bank, [m1])
            m2 = k.g.go([done, m_cos], nc.gpsimd.tensor_tensor, dst[:, chunk, 0:S], dst[:, chunk, 0:S], cos[:], ALU.mult)
            t.free = [k.v.go([m1, m2], nc.vector.tensor_tensor, dst[:, chunk, 0:S], dst[:, chunk, 0:S], t.ap[:, 0:S],
                             ALU.add)]
            return marks
        return evacuate

    both = [LAT, CTXS]
    for _ in project(k, "dq", 1, h[:, 0], h[:, 1], h_ready, both[0:sides], keep(dq, both[0:sides])):
        pass
    for _ in project(k, "dk", 1, h[:, 0], h[:, 1], h_ready, both, keep(dk, both)):
        pass

    def keep_v(i, src, done):
        return [copy_out(k, [done] + start, dv[:, i, :], src)]

    for _ in project_tokens(k, "dv", h[:, 0], h[:, 1], h_ready, [slice(i * P, (i + 1) * P) for i in range(ST + CT)],
                            keep_v):
        pass
    ready = [k.a.now(), k.v.now()]
    units = [(c, i, par, mp) for c in range(2) for i in range(ST + CT if sides == 2 else ST) for par in range(2)
             for mp in range(2)]
    state, held = {}, {}

    def key_span(i):
        return both if i < ST else both[1:]

    def scores(u):
        c, i, par, mp = u
        if mp == 0:
            state[c, i, par] = (probs.take(), stats.take())
        p, st = state[c, i, par]
        at = 64 * par + 32 * mp
        banks = []
        for j, (a, b) in enumerate(key_span(i)):
            bank = k.banks.take()
            k.pe.wait(ready + bank.free)
            done = k.pe.mark(nc.tensor.matmul(bank.ap[:, 0:b - a], dq[at:at + 32, c, i * P:(i + 1) * P],
                                              dk[at:at + 32, c, a:b], start=True, stop=True, tile_position=(at, 0)))
            t = k.v.go([done] + st.free, nc.vector.tensor_reduce, st.ap[:, 2 * mp + j:2 * mp + j + 1],
                       bank.ap[:, 0:b - a], AX.X, ALU.max)
            banks.append(bank)
        if len(banks) == 2:
            t = k.v.go([t], nc.vector.tensor_reduce, st.ap[:, 12 + mp:13 + mp], st.ap[:, 2 * mp:2 * mp + 2], AX.X, ALU.max)
            top = 12 + mp
        else:
            top = 2 * mp
        t = k.v.go([t], nc.vector.tensor_scalar, st.ap[:, 4 + mp:5 + mp], st.ap[:, top:top + 1], -scale, None, ALU.mult)
        state[u] = (banks, t)

    def soft(u):
        c, i, par, mp = u
        banks, t = state.pop(u)
        p, st = state[c, i, par]
        spans = key_span(i)
        for j, (a, b) in enumerate(spans):
            e = k.a.go([t] + p.free, nc.scalar.activation, p.ap[:, mp, a:b], banks[j].ap[:, 0:b - a], ACT.Exp,
                       bias=st.ap[:, 4 + mp:5 + mp], scale=scale, accum_out=st.ap[:, 6 + 2 * mp + j:7 + 2 * mp + j])
            k.banks.give(banks[j], [e])
        if mp == 0:
            return
        if len(spans) == 2:
            t = k.v.go([e], nc.vector.tensor_tensor, st.ap[:, 10:12], st.ap[:, 6:10:2], st.ap[:, 7:11:2], ALU.add)
        else:
            t = k.v.go([e], nc.vector.tensor_copy, st.ap[:, 10:12], st.ap[:, 6:10:2])
        t = k.v.go([t], nc.vector.reciprocal, st.ap[:, 12:14], st.ap[:, 10:12])
        t = k.v.go([t] + k.m_lam, nc.vector.tensor_tensor, st.ap[:, 14:15], st.ap[:, 13:14], k.neg_lam[:, l:l + 1], ALU.mult)
        a, b = spans[0][0], spans[-1][1]
        t = k.v.go([t], nc.vector.tensor_scalar, p.ap[:, 0, a:b], p.ap[:, 0, a:b], st.ap[:, 12:13], None, ALU.mult)
        t = k.v.go([t], nc.vector.scalar_tensor_tensor, p.ap[:, 0, a:b], p.ap[:, 1, a:b], st.ap[:, 14:15],
                   p.ap[:, 0, a:b], ALU.mult, ALU.add)
        st.free = [t]
        state[c, i, par] = (p, t)

    def turn(u):
        c, i, par, mp = u
        if mp == 0:
            return
        p, t = state[c, i, par]
        pt = turned.take()
        marks = []
        for group in (range(0, 3), range(3, 6)) if i < ST else (range(4, 6),):
            bank = k.banks.take()
            k.pe.wait([t] + bank.free)
            for n, b in enumerate(group):
                last = nc.tensor.transpose(bank.ap[:, n * P:(n + 1) * P], p.ap[:, 0, b * P:(b + 1) * P], k.ident[:])
            done = k.pe.mark(last)
            marks.append(copy_out(k, [done] + pt.free, pt.ap[:, group[0]:group[-1] + 1, :].rearrange("p b q -> p (b q)"),
                                  bank.ap[:, 0:len(group) * P]))
            k.banks.give(bank, marks[-1:])
        p.free = [done]
        state[c, i, par] = (pt, marks)

    def values(u):
        c, i, par, mp = u
        if mp == 0:
            return
        pt, marks = state.pop((c, i, par))
        side = 0 if i < ST else 1
        if (c, side) not in held:
            held[c, side] = k.banks.take()
        bank = held[c, side]
        k.pe.wait(marks + ready + bank.free)
        tiles = list(range(0 if side == 0 else ST, ST + CT))
        q0 = (i - ST * side) * P
        for b in tiles:
            last = nc.tensor.matmul(bank.ap[64 * par:64 * par + 64, q0:q0 + P], dv[:, b, (2 * c + par) * 64:(2 * c + par + 1) * 64],
                                    pt.ap[:, b, :], start=b == tiles[0], stop=b == tiles[-1])
        done = k.pe.mark(last)
        pt.free = [done]
        if par == 1 and i in (ST - 1, ST + CT - 1):
            a, b = both[side]
            m1 = copy_out(k, [done], y[:, 4 + c, a:b], bank.ap[:, 0:b - a])
            k.banks.give(bank, [m1])
            rstd = temps.take()
            root = inverse_rms(k, [[m1]], [y[:, 4 + c, :]], [(a, b)], without(temps, rstd), rstd.ap, rstd.free, 64,
                               ones=k.pair)
            rstd.free = [k.v.go(root + k.m_lam, nc.vector.scalar_tensor_tensor, y[:, 4 + c, a:b], y[:, 4 + c, a:b],
                                k.sub[:, l:l + 1], rstd.ap[:, a:b], ALU.mult, ALU.mult)]

    return pipeline(units, [scores, soft, lambda u: None, turn, values])


class Recurrent:

    def __init__(self, k, l, h, h_ready, y, sides):
        self.k, self.l, self.h, self.h_ready, self.y, self.sides = k, l, h, h_ready, y, sides
        self.heads, self.units, self.work = {}, {}, {}
        self.tiles = ST + CT if sides == 2 else ST
        self.bank_tiles = [(0, ST), (ST, ST + CT)][0:sides]
        names = "fbqvg"
        self.sets = [{n: place(k, f"b{l}_r{s}_{n}", AT_WORK + 24 + 15 * s + 3 * i, [T2])
                      for i, n in enumerate(names)} for s in range(2)]
        self.free = [{n: now(k) for n in names} for s in range(2)]

    def project(self, hc):
        k, l, nc = self.k, self.l, self.k.nc
        m = self.heads[hc] = Core()
        buffers, free = self.sets[hc % 2], self.free[hc % 2]
        m.ready = {n: [] for n in buffers}
        spans = [LAT, CTXS]

        def sigmoid(dst, banks, done, before):
            for src, a, b in banks:
                t = k.a.go([done] + before, nc.scalar.activation, dst[:, a:b], src, ACT.Exp, scale=-1.0)
            all_ = dst[:, 0:banks[-1][2]]
            one = k.v.go([t], nc.vector.tensor_scalar, all_, all_, 1e38, 1.0, ALU.min, ALU.add)
            ln = k.a.go([one], nc.scalar.activation, all_, all_, ACT.Ln)
            return t, k.a.go([ln], nc.scalar.activation, all_, all_, ACT.Exp, scale=-1.0)

        def keep_silu(name):
            def evacuate(chunk, banks, done):
                dst = buffers[name]
                _, t = sigmoid(dst, banks, done, free.pop(name))
                for src, a, b in banks:
                    m.ready[name].append(k.v.go([t], nc.vector.tensor_tensor, dst[:, a:b], dst[:, a:b], src, ALU.mult))
                return m.ready[name]
            return evacuate

        def keep_gate(name):
            d = "fb".index(name)

            def evacuate(chunk, banks, done):
                dst = buffers[name]
                read, t = sigmoid(dst, banks, done, free.pop(name))
                m.ready[name] = [k.v.go([t] + k.m_lb, nc.vector.tensor_scalar, dst[:], dst[:],
                                        k.lb1[:, l, d, hc:hc + 1], k.lb[:, l, d, hc:hc + 1], ALU.mult, ALU.add)]
                return [read]
            return evacuate

        def keep_v(i, src, done):
            if i == 0:
                m.v_free = free.pop("v")
            m.ready["v"].append(copy_out(k, [done] + m.v_free, buffers["v"][:, i * P:(i + 1) * P], src))
            return m.ready["v"][-1:]

        def feature_major(name, sp, evacuate):
            return project(k, name, 1, self.h[:, 0], self.h[:, 1], self.h_ready, sp, evacuate)

        yield from feature_major("f", spans, keep_gate("f"))
        yield from feature_major("b", spans, keep_gate("b"))
        yield from feature_major("q", spans[0:self.sides], keep_silu("q"))
        yield from project_tokens(k, "v", self.h[:, 0], self.h[:, 1], self.h_ready,
                                  [slice(i * P, (i + 1) * P) for i in range(ST + CT)], keep_v)
        yield from feature_major("g", spans[0:self.sides], keep_silu("g"))

    def set_up(self):
        k, l, nc, at = self.k, self.l, self.k.nc, AT_WORK + 54
        start = now(k)
        self.gla = nc.alloc_sbuf_tensor_at(f"b{l}_gla", [P, 2, LEVELS + 1, P], U8, offset=ARENA + (at + 21) * 1024)
        wide = place(k, f"b{l}_gla_wide", AT_WORK + 39, [2, LEVELS + 1, P])
        self.wide, self.wide_loaded = wide, k.rows.start(start, wide[:], k.ins["c_gla"])
        buffers = [Slot(place(k, f"b{l}_u{i}", at + 3 * i, [T2])) for i in range(7)]
        for slot in buffers:
            slot.free = start
        self.keys, self.scores = Ring([]), Ring([])
        self.keys.slots, self.scores.slots = buffers[0:2], buffers[2:4]
        self.ex = Shared([])
        self.ex.idle = buffers[4:7]
        self.decays_free = start

    def convert_masks(self):
        self.m_gla = self.k.v.go([self.wide_loaded] + self.start, self.k.nc.vector.tensor_copy, self.gla[:],
                                 self.wide[:])

    def begin(self, hc, d):
        k, nc = self.k, self.k.nc
        u = self.units[hc, d] = Core()
        head, name = self.heads[hc], "fb"[d]
        f = self.sets[hc % 2][name][:]
        ready = head.ready[name]
        u.keys, u.scores = self.keys.take(), self.scores.take()
        u.m_k = k.g.go(ready + u.keys.free, nc.gpsimd.tensor_scalar, u.keys.ap[:], f, -1.0, 1.0, ALU.mult, ALU.add)
        u.m_scores = k.g.go(u.scores.free, nc.gpsimd.memset, u.scores.ap[:, 0:self.tiles * P], 0.0)
        t = k.v.go(ready + [u.m_k], nc.vector.tensor_scalar, f, f, 2.0 ** -64, None, ALU.max)
        yield
        t = k.a.go([t], nc.scalar.activation, f, f, ACT.Ln)
        if d == 0:
            u.m_b = k.v.go([t] + k.m_resets, nc.vector.tensor_tensor_scan, f, k.resets[:, 0:T2], f, 0.0,
                           ALU.mult, ALU.add)
        else:
            u.m_b = k.v.go([t] + k.m_resets, nc.vector.tensor_tensor_scan, f[:, ::-1], k.resets[:, T2:0:-1],
                           f[:, ::-1], 0.0, ALU.mult, ALU.add)
        yield

    def decays(self, item):
        (hc, d), lv = item
        k, nc, u, bc = self.k, self.k.nc, self.units[hc, d], self.sets[hc % 2]["fb"[d]]
        if lv == LEVELS:
            return
        T, n = self.tiles * P, 1 << lv
        x = self.ex.take()
        bp = bc[:, 0:T].rearrange("p (n s m) -> p n s m", s=2, m=n)
        xp = x.ap[:, 0:T].rearrange("p (n s m) -> p n s m", s=2, m=n)
        key, query = (0, 1) if d == 0 else (1, 0)
        edge = bp[:, :, 0, n - 1:n] if d == 0 else bp[:, :, 1, 0:1]
        edge = edge.broadcast_to([P, T // (2 * n), n])
        a1 = k.g.go([u.m_b] + x.free, nc.gpsimd.tensor_tensor, xp[:, :, key, :], edge, bp[:, :, key, :], ALU.subtract)
        a2 = k.v.go([u.m_b] + x.free, nc.vector.tensor_tensor, xp[:, :, query, :], bp[:, :, query, :], edge,
                    ALU.subtract)
        e = k.a.go([a1, a2], nc.scalar.activation, x.ap[:, 0:T], x.ap[:, 0:T], ACT.Exp)
        self.work[item] = (x, xp, key, query, n, e)

    def pairs(self, item):
        (hc, d), lv = item
        k, nc, u, q_ready = self.k, self.k.nc, self.units[hc, d], self.heads[hc].ready["q"]
        q, kk, T = self.sets[hc % 2]["q"][:], u.keys.ap, self.tiles * P
        if lv < LEVELS:
            x, xp, key, query, n, e = self.work[item]
            parts = lambda ap: ap[:, 0:T].rearrange("p (n s m) -> p n s m", s=2, m=n)
            e1 = k.g.go([e, u.m_k], nc.gpsimd.tensor_tensor, xp[:, :, key, :], xp[:, :, key, :],
                        parts(kk)[:, :, key, :], ALU.mult)
            e2 = k.v.go([e] + q_ready, nc.vector.tensor_tensor, xp[:, :, query, :], xp[:, :, query, :],
                        parts(q)[:, :, query, :], ALU.mult)
            keys, queries, e = x.ap, x.ap, [e1, e2]
        else:
            keys, queries, e = kk, q, [u.m_k] + q_ready
        banks = []
        for i0, i1 in self.bank_tiles:
            bank = k.banks.take()
            k.pe.wait(e + bank.free)
            for i in range(i0, i1):
                last = nc.tensor.matmul(bank.ap[:, (i - i0) * P:(i - i0 + 1) * P], keys[:, i * P:(i + 1) * P],
                                        queries[:, i * P:(i + 1) * P], start=True, stop=True)
            banks.append((bank, i0, i1, k.pe.mark(last)))
        if lv < LEVELS:
            self.ex.give(x, [banks[-1][3]])
        self.work[item] = banks

    def masked(self, item):
        (hc, d), lv = item
        k, nc, u = self.k, self.k.nc, self.units[hc, d]
        for bank, i0, i1, done in self.work.pop(item):
            n = i1 - i0
            mask = self.gla[:, d, lv, :].unsqueeze(1).broadcast_to([P, n, P])
            u.m_scores = k.v.go([done, self.m_gla, u.m_scores], nc.vector.copy_predicated,
                                u.scores.ap[:, i0 * P:i1 * P].rearrange("p (n t) -> p n t", n=n), mask,
                                bank.ap[:, 0:n * P].rearrange("p (n t) -> p n t", n=n))
            k.banks.give(bank, [u.m_scores])

    def end(self, hc, d):
        k, l, nc, y, ex, dec = self.k, self.l, self.k.nc, self.y, self.ex, self.k.decays
        u, head, buffers, free = self.units.pop((hc, d)), self.heads[hc], self.sets[hc % 2], self.free[hc % 2]
        q, v, bc, kk, sc = buffers["q"], buffers["v"], buffers["fb"[d]], u.keys.ap, u.scores.ap
        T = self.tiles * P
        last_of = bc[:, P - 1::P] if d == 0 else bc[:, 0::P]
        m_dec = k.a.go([u.m_b] + self.decays_free, nc.scalar.activation, dec[:], last_of, ACT.Exp)
        kd = ex.take()
        m_gap = k.g.go([u.m_b] + kd.free, nc.gpsimd.tensor_tensor, kd.ap[:].rearrange("p (n t) -> p n t", t=P),
                       last_of.unsqueeze(2).broadcast_to([P, ST + CT, P]), bc[:].rearrange("p (n t) -> p n t", t=P),
                       ALU.subtract)
        yield
        t = k.a.go([m_gap], nc.scalar.activation, kd.ap[:], kd.ap[:], ACT.Exp)
        m_kd = k.v.go([t, u.m_k], nc.vector.tensor_tensor, kd.ap[:], kd.ap[:], kk[:], ALU.mult)
        t = k.a.go([m_gap, m_dec, u.m_scores], nc.scalar.activation, bc[:, 0:T], bc[:, 0:T], ACT.Exp)
        m_qd = k.v.go([t], nc.vector.tensor_tensor, bc[:, 0:T], bc[:, 0:T], q[:, 0:T], ALU.mult)
        yield
        order = [4, 5, 0, 1, 2, 3] if d == 0 else [5, 4, 3, 2, 1, 0]
        kdt = kk[:].rearrange("p (n k) -> p n k", n=ST + CT)
        m_t = []
        for group in (range(0, 3), range(3, 6)):
            bank = k.banks.take()
            k.pe.wait([m_kd] + bank.free)
            for n, i in enumerate(group):
                last = nc.tensor.transpose(bank.ap[:, n * P:(n + 1) * P], kd.ap[:, i * P:(i + 1) * P], k.ident[:])
            done = k.pe.mark(last)
            m_t.append(copy_out(k, [done, m_kd, u.m_scores], kdt[:, group[0]:group[-1] + 1, :].rearrange("p n k -> p (n k)"),
                                bank.ap[:, 0:3 * P]))
            k.banks.give(bank, m_t[-1:])
        ex.give(kd, [done, m_kd])
        yield
        sums = [k.banks.take(), k.banks.take()]
        for bank in sums:
            k.pe.wait(bank.free)
        k.pe.wait(m_t + head.ready["v"])
        for n, i in enumerate(order[:-1]):
            last = nc.tensor.matmul(sums[n // 4].ap[:, (n % 4) * P:(n % 4 + 1) * P], kdt[:, i, :],
                                    v[:, i * P:(i + 1) * P], start=True, stop=True)
        done = k.pe.mark(last)
        u.keys.free = [done]
        yield
        st = ex.take()
        states = st.ap[:].rearrange("p (n v) -> p n v", v=P)
        for n, i in enumerate(order[:-1]):
            part = sums[n // 4].ap[:, (n % 4) * P:(n % 4 + 1) * P]
            if n == 0:
                m_st = k.v.go([done] + st.free, nc.vector.tensor_copy, states[:, 1, :], part)
            else:
                m_st = k.v.go([m_st, m_dec], nc.vector.scalar_tensor_tensor, states[:, n + 1, :], states[:, n, :],
                              dec[:, i:i + 1], part, ALU.mult, ALU.add)
        for bank in sums:
            k.banks.give(bank, [m_st])
        self.decays_free = [m_st]
        yield
        for i0, i1 in self.bank_tiles:
            bank = k.banks.take()
            k.pe.wait([m_st, m_qd, u.m_scores] + bank.free)
            for i in range(i0, i1):
                out = bank.ap[:, (i - i0) * P:(i - i0 + 1) * P]
                n = order.index(i)
                if n:
                    nc.tensor.matmul(out, states[:, n, :], bc[:, i * P:(i + 1) * P], start=True, stop=False)
                last = nc.tensor.matmul(out, v[:, i * P:(i + 1) * P], sc[:, i * P:(i + 1) * P],
                                        start=n == 0, stop=True)
            done = k.pe.mark(last)
            a, b = i0 * P, i1 * P
            if d == 0:
                head.m_o = k.v.go([done] + self.start, nc.vector.tensor_copy, y[:, hc, a:b], bank.ap[:, 0:b - a])
            else:
                head.m_o = k.v.go([done, head.m_o], nc.vector.tensor_tensor, y[:, hc, a:b], y[:, hc, a:b],
                                  bank.ap[:, 0:b - a], ALU.add)
            k.banks.give(bank, [head.m_o])
        ex.give(st, [done])
        u.scores.free = [done]
        free["fb"[d]] = [done, m_qd]
        yield
        if d == 0:
            return
        free["q"] = free["v"] = [done, m_qd]
        rstd = ex.take()
        one = Ring([])
        one.slots = [rstd]
        root = inverse_rms(k, [[head.m_o]], [y[:, hc, :]], [LAT, CTXS][0:self.sides], one, rstd.ap, rstd.free, P)
        yield
        t = k.v.go(root, nc.vector.scalar_tensor_tensor, y[:, hc, 0:T], y[:, hc, 0:T], k.vec("onorm", l),
                   rstd.ap[:, 0:T], ALU.mult, ALU.mult)
        t = k.v.go([t] + head.ready["g"], nc.vector.tensor_tensor, y[:, hc, 0:T], y[:, hc, 0:T],
                   buffers["g"][:, 0:T], ALU.mult)
        ex.give(rstd, [t])
        free["g"] = [t]
        yield

    def run(self, beside):
        self.start = now(self.k)
        self.set_up()
        for _ in self.begin(0, 0):
            pass
        self.convert_masks()
        self.free[1] = {n: self.start + [self.m_gla] for n in self.free[1]}
        units = [(hc, d) for hc in range(HGH) for d in range(2)]
        per_unit, stages = LEVELS + 1, [self.decays, self.pairs, self.masked]

        def between(n):
            if n:
                yield from self.end(*units[n - 1])
            if n + 1 < len(units):
                yield from self.begin(*units[n + 1])

        def filler_of(hc):
            yield from beside[hc]
            if hc + 1 < HGH:
                yield from self.project(hc + 1)

        others, filler, owed = iter(()), None, 0.0
        for step, _ in enumerate(pipeline([(u, lv) for u in units for lv in range(per_unit)], stages)):
            n, lv = divmod(step, per_unit)
            if lv == 0 and n % 2 == 0 and n < len(units):
                filler, owed = filler_of(n // 2), 0.0
            if lv == len(stages) - 1 and n < len(units):
                others = between(n)
            for _ in range(2):
                next(others, None)
            if n % 2 or lv >= (0 if self.sides == 2 else 3):
                owed += 1.15
                while owed >= 1:
                    owed -= 1
                    next(filler, None)
            if lv == per_unit - 1:
                for _ in others:
                    pass
                if n % 2:
                    for _ in filler:
                        pass
        for _ in self.end(*units[-1]):
            pass


def second_layer(k, l, x, x_ready, before):
    nc = k.nc
    tag = f"b{l}_"
    sides = 2 if l < DEPTH - 1 else 1
    start = now(k)
    h = place(k, tag + "h", AT_H, [2, DC, T2], F32R)
    y = place(k, tag + "y", AT_WORK, [DC, T2])
    rstd = place(k, tag + "rstd", AT_WORK + 74, [T2])
    norm_buffers = [place(k, f"{tag}n{i}", AT_WORK + 24 + 3 * i, [T2]) for i in range(3)]

    mats = fourier_matrices(k, l)
    h_ready = adaln(k, l, 0, x, x_ready, before + [k.v.now()], h[:, 0], h[:, 1], 2, rstd, fresh(norm_buffers, start))
    start = now(k)
    for _ in fourier(k, l, h, h_ready, y, start, sides, mats):
        pass
    rec = Recurrent(k, l, h, h_ready, y, sides)
    attention = diff_attention(k, l, h, h_ready, y, sides)
    for _ in weave(attention, rec.project(0), 14 / (48 if sides == 2 else 32)):
        pass
    beside = [iter(()) for _ in range(HGH)]
    if l + 1 < DEPTH:
        before = now(k)
        n = MOD_SLABS // (2 * (HGH - 1))
        early, late = [fresh([memory[:, i * SLAB_F:(i + 1) * SLAB_F] for i in range(2)], before)
                       for memory in (y[:, HGH - 1], rec.sets[HGH % 2]["f"])]
        for hc in range(HGH):
            beside[hc] = k.modulation.steps(n, early) if hc < HGH - 1 else k.modulation.steps(MOD_SLABS // 2, late)
    rec.run(beside)
    mixed = now(k)
    ys = place(k, tag + "ys", AT_H, [2, DC, T2], F32R)
    end = T2 if sides == 2 else S
    ys_ready = [split_into(k, mixed, ys[:, 0, c, 0:end], ys[:, 1, c, 0:end], y[:, c, 0:end]) for c in range(DC)]
    spans = [LAT, CTXS][0:sides]
    out = place(k, tag + "out", AT_WORK + 33, [DC, T2])
    out_ready = [None] * DC

    def keep(chunk, banks, done):
        out_ready[chunk] = [copy_out(k, [done] + mixed, out[:, chunk, a:b], src) for src, a, b in banks]
        return out_ready[chunk]

    for _ in project(k, "w_out", 4, ys[:, 0], ys[:, 1], ys_ready, spans, keep):
        pass
    temps = fresh(norm_buffers, mixed)
    x_ready = add_normed(k, l, 0, x, out, out_ready, mixed, sides, rstd, temps)

    h_ready = adaln(k, l, 1, x, x_ready, [k.pe.now(), k.v.now()], h[:, 0], h[:, 1], sides, rstd, temps)
    hidden = place(k, tag + "hidden", AT_WORK + 33, [2, 6, T2], F32R)
    acts_ring = temps
    acts, hidden_ready, hidden_free = {}, [None] * 6, now(k)

    def ff_g(chunk, banks, done):
        t = acts_ring.take()
        freed = []
        for src, a, b in banks:
            m = k.a.go([done] + t.free, nc.scalar.activation, t.ap[:, a:b], src, ACT.Sigmoid)
            freed.append(k.v.go([m], nc.vector.tensor_tensor, t.ap[:, a:b], t.ap[:, a:b], src, ALU.mult))
        acts[chunk] = (t, freed)
        return freed

    def ff_u(c0):
        def evacuate(chunk, banks, done):
            t, ms = acts.pop(chunk)
            for src, a, b in banks:
                last = k.v.go([done] + ms, nc.vector.tensor_tensor, t.ap[:, a:b], t.ap[:, a:b], src, ALU.mult)
            end = banks[-1][2]
            t.free = split_into(k, [last] + hidden_free, hidden[:, 0, chunk - c0, 0:end], hidden[:, 1, chunk - c0, 0:end],
                                t.ap[:, 0:end])
            hidden_ready[chunk - c0] = t.free
            return [last]
        return evacuate

    def down(first):
        def evacuate(chunk, banks, done):
            if first:
                y_ready[chunk] = [copy_out(k, [done] + hidden_free, y[:, chunk, a:b], src) for src, a, b in banks]
            else:
                y_ready[chunk] = [k.v.go([done] + y_ready[chunk], nc.vector.tensor_tensor, y[:, chunk, a:b],
                                         y[:, chunk, a:b], src, ALU.add) for src, a, b in banks]
            return y_ready[chunk]
        return evacuate

    y_ready = [None] * DC
    for c0, n in FF_PARTS2:
        for c in range(0, n, 2):
            for _ in project(k, "ff_g", 1, h[:, 0], h[:, 1], h_ready, spans, ff_g, c0 + c):
                pass
            for _ in project(k, "ff_u", 1, h[:, 0], h[:, 1], h_ready, spans, ff_u(c0), c0 + c):
                pass
        before = now(k)
        for _ in project(k, "ff_out", 4, hidden[:, 0], hidden[:, 1], hidden_ready, spans, down(c0 == 0)):
            pass
        hidden_free = [k.pe.now()]
    x_ready = add_normed(k, l, 1, x, y, y_ready, before, sides, rstd, temps)
    return x_ready, before


def program(nc, ins, out, order=None):
    k = set_up(nc, ins)
    x = place(k, "x", AT_X, [DC, T2])
    rows = place(k, "x_rows", AT_WORK + 16, [ST, D])
    rows_ctx = place(k, "ctx_rows", AT_WORK + 32, [CT, D])
    loaded = load_rows(k, ins["x"][0], ST, rows, [])
    load_constants(k)
    stage = place(k, "vector_rows", AT_WORK, [4 * P])
    load_vectors(k, stage)
    k.w = Weights(k, first_slabs(ins) + modulation_slabs(ins) + second_slabs(ins), order)
    k.w.prefetch()
    x1 = x[:, :, 0:S]
    x_ready = transpose_in(k, loaded, ST, x1, rows)
    before = now(k)
    for l in range(DEPTH):
        x_ready, before = first_layer(k, l, x1, x[:, :, S:T2], x_ready, before)
    rstd = place(k, "f_rstd", AT_WORK + 74, [S])
    temps = fresh([place(k, f"f_t{i}", AT_WORK + 64 + 2 * i, [S]) for i in range(3)], before)
    loaded = load_rows(k, ins["ctx_2"][0], CT, rows_ctx, now(k))
    x_ready = norm_plain(k, x1, x_ready, before, lambda c: k.vec("norm_f", c), None, None, SPAN1, rstd, temps, out=x1)
    ctx_ready = transpose_in(k, loaded, CT, x[:, :, S:T2], rows_ctx)
    x_ready = [a + b for a, b in zip(x_ready, ctx_ready)]
    for l in range(DEPTH):
        x_ready, before = second_layer(k, l, x, x_ready, before)
    transpose_out(k, x, x_ready, out[0])
    return k.w.used


INPUTS = ("x", "norm1", "w_in", "b_gate", "w_br", "w_o", "norm2", "w_up", "conv_w", "conv_b", "w_down", "norm_f",
          "c_2", "ctx_2", "c_ctx_2", "w_mod_2", "b_mod_2", "norm_g_2", "w_in_2", "w_out_2", "hg_lb_logits_2",
          "hg_onorm_2", "da_lambda_2", "da_subln_2", "w_ffn_in_2", "w_ffn_out_2")


def kernel(**inputs):
    import concourse.bacc as bacc
    from concourse.bass_utils import run_bass_kernel_spmd

    arrays = {name: np.ascontiguousarray(inputs[name]) for name in INPUTS}
    arrays.update(constants())
    order = None
    for _ in range(2):
        nc = bacc.Bacc("TRN2", target_bir_lowering=False, num_devices=1)
        ins = {name: nc.dram_tensor(name, a.shape, mybir.dt.from_np(a.dtype), kind="ExternalInput").ap()
               for name, a in arrays.items()}
        out = nc.dram_tensor("y_out", (1, S, D), F32, kind="ExternalOutput").ap()
        order = program(nc, ins, out, order)
    return run_bass_kernel_spmd(nc, [arrays], core_ids=[0]).results[0]["y_out"]
```
